# Optimizing a Trainium2 kernel written in Bass

```python
import math
import jax, jax.numpy as jnp
from jax import lax
import numpy as np

D_MODEL = 1024
BATCH = 1
SEQ = 512
DEPTH = 1

CHUNK = 64
EPS = 1e-6

MLA_HEADS = 8
MLA_Q_RANK = 384
MLA_KV_RANK = 256
MLA_NOPE = 64
MLA_ROPE = 32
MLA_V = 64
MLA_QK = MLA_NOPE + MLA_ROPE
ROPE_THETA = 10000.0
Q_BLOCK = 128

RWKV_HEADS = 8
RWKV_HEAD = 64
RWKV_DIM = RWKV_HEADS * RWKV_HEAD
W_LORA = 64
A_LORA = 64
G_LORA = 128
LN_X_EPS = 64e-5

MIX_WIDTH = MLA_HEADS * MLA_V + RWKV_DIM
MLA_COLS = MLA_Q_RANK + MLA_KV_RANK + MLA_ROPE
RWKV_COLS = 3 * RWKV_DIM + W_LORA + A_LORA + G_LORA
IN_COLS = MLA_COLS + RWKV_COLS
MLA_SPLITS = (MLA_Q_RANK, MLA_Q_RANK + MLA_KV_RANK)
RWKV_SPLITS = (RWKV_DIM, 2 * RWKV_DIM, 3 * RWKV_DIM, 3 * RWKV_DIM + W_LORA, 3 * RWKV_DIM + W_LORA + A_LORA)

PEER_HEADS = 8
N_KEYS = 128
N_EXPERTS = N_KEYS * N_KEYS
PEER_DQ = 256
PEER_DHALF = PEER_DQ // 2
PEER_TOPK = 16
TOK_BLOCK = 128


def rms_norm(x, g, eps=EPS):
    xf = x.astype(jnp.float32)
    y = xf * lax.rsqrt(jnp.mean(xf * xf, axis=-1, keepdims=True) + eps)
    return (y * g.astype(jnp.float32)).astype(x.dtype)

def apply_rope(t, positions):
    half = MLA_ROPE // 2
    inv = ROPE_THETA ** (-jnp.arange(half, dtype=jnp.float32) / half)
    ang = positions.astype(jnp.float32)[..., None] * inv
    cos = jnp.cos(ang)[:, :, None, :]
    sin = jnp.sin(ang)[:, :, None, :]
    tf = t.astype(jnp.float32)
    t1, t2 = tf[..., :half], tf[..., half:]
    out = jnp.concatenate([t1 * cos - t2 * sin, t1 * sin + t2 * cos], axis=-1)
    return out.astype(t.dtype)

def mla_group(p_mla, positions, g_cq, g_ckv, w_uq, w_uk, w_uv, g_qnorm, g_knorm, g_attn_out):
    B, S, _ = p_mla.shape
    c_q, c_kv, k_rope = jnp.split(p_mla, MLA_SPLITS, axis=-1)
    q = (rms_norm(c_q, g_cq) @ w_uq).reshape(B, S, MLA_HEADS, MLA_QK)
    c_kv = rms_norm(c_kv, g_ckv)
    k_nope = (c_kv @ w_uk).reshape(B, S, MLA_HEADS, MLA_NOPE)
    v = (c_kv @ w_uv).reshape(B, S, MLA_HEADS, MLA_V)
    k = jnp.concatenate([k_nope, jnp.broadcast_to(k_rope[:, :, None, :], (B, S, MLA_HEADS, MLA_ROPE))], axis=-1)
    q = rms_norm(q, g_qnorm)
    k = rms_norm(k, g_knorm)
    q = jnp.concatenate([q[..., :MLA_NOPE], apply_rope(q[..., MLA_NOPE:], positions)], axis=-1)
    k = jnp.concatenate([k[..., :MLA_NOPE], apply_rope(k[..., MLA_NOPE:], positions)], axis=-1)
    scale = MLA_QK ** -0.5
    n_blk = S // Q_BLOCK
    q_blocks = q.reshape(B, n_blk, Q_BLOCK, MLA_HEADS, MLA_QK).transpose(1, 0, 2, 3, 4)
    key_chunk = jnp.arange(S) // CHUNK

    def attend(args):
        qb, bi = args
        q_chunk = (bi * Q_BLOCK + jnp.arange(Q_BLOCK)) // CHUNK
        s = jnp.einsum('bqhd,bkhd->bhqk', qb, k).astype(jnp.float32) * scale
        mask = key_chunk[None, :] <= q_chunk[:, None]
        s = jnp.where(mask[None, None], s, -jnp.inf)
        pr = jax.nn.softmax(s, axis=-1).astype(v.dtype)
        return jnp.einsum('bhqk,bkhd->bqhd', pr, v)

    o = lax.map(attend, (q_blocks, jnp.arange(n_blk)))
    o = o.transpose(1, 0, 2, 3, 4).reshape(B, S, MLA_HEADS, MLA_V)
    o = rms_norm(o, g_attn_out.reshape(MLA_HEADS, MLA_V))
    return o.reshape(B, S, MLA_HEADS * MLA_V)

def rwkv7_step(state, inp):
    r_t, w_t, k_t, v_t, kk_t, a_t = inp
    sk = jnp.einsum('bhij,bhj->bhi', state, kk_t)
    state = (state * w_t[:, :, None, :]
             - sk[..., None] * (kk_t * a_t)[:, :, None, :]
             + v_t[..., None] * k_t[:, :, None, :])
    y = jnp.einsum('bhij,bhj->bhi', state, r_t)
    return state, y

def rwkv7_group(p_rwkv, rwkv_mu, w0, w2, a0, a2, g2, k_k, k_a, r_k, ln_x_w, ln_x_b):
    B, S, _ = p_rwkv.shape
    prev = jnp.pad(p_rwkv, ((0, 0), (1, 0), (0, 0)))[:, :S]
    p = p_rwkv + (prev - p_rwkv) * rwkv_mu
    r, k, v, wl, al, gl = jnp.split(p, RWKV_SPLITS, axis=-1)
    w = -jax.nn.softplus(-(w0 + jnp.tanh(wl) @ w2)) - 0.5
    decay = jnp.exp(-jnp.exp(w.astype(jnp.float32)))
    a = jax.nn.sigmoid(a0 + al @ a2)
    g = jax.nn.sigmoid(gl) @ g2
    heads = lambda t: t.astype(jnp.float32).reshape(B, S, RWKV_HEADS, RWKV_HEAD)
    kk = heads(k * k_k)
    kk = kk / jnp.maximum(jnp.sqrt(jnp.sum(kk * kk, axis=-1, keepdims=True)), 1e-12)
    k = k * (1.0 + (a - 1.0) * k_a)
    r_h, k_h, v_h, a_h, w_h = heads(r), heads(k), heads(v), heads(a), heads(decay)
    xs = tuple(jnp.moveaxis(t, 1, 0) for t in (r_h, w_h, k_h, v_h, kk, a_h))
    state0 = jnp.zeros((B, RWKV_HEADS, RWKV_HEAD, RWKV_HEAD), jnp.float32)
    _, y = lax.scan(rwkv7_step, state0, xs)
    y = jnp.moveaxis(y, 0, 1)
    mu = jnp.mean(y, axis=-1, keepdims=True)
    var = jnp.mean(jnp.square(y - mu), axis=-1, keepdims=True)
    y = ((y - mu) * lax.rsqrt(var + LN_X_EPS) * ln_x_w.astype(jnp.float32).reshape(RWKV_HEADS, RWKV_HEAD)
         + ln_x_b.astype(jnp.float32).reshape(RWKV_HEADS, RWKV_HEAD))
    bonus = jnp.sum(r_h * k_h * r_k.astype(jnp.float32), axis=-1, keepdims=True) * v_h
    y = (y + bonus).reshape(B, S, RWKV_DIM).astype(p_rwkv.dtype)
    return y * g

def peer_ffn(h, w_pq, sub_keys, expert_u, expert_v):
    B, S, D = h.shape
    hb_all = h.reshape(B * S // TOK_BLOCK, TOK_BLOCK, D)

    def block(hb):
        q = (hb @ w_pq).reshape(TOK_BLOCK, PEER_HEADS, 2, PEER_DHALF)
        s = jnp.einsum('thpd,hpnd->thpn', q, sub_keys).astype(jnp.float32)
        s1, i1 = lax.top_k(s[:, :, 0], PEER_TOPK)
        s2, i2 = lax.top_k(s[:, :, 1], PEER_TOPK)
        cand_s = (s1[..., :, None] + s2[..., None, :]).reshape(TOK_BLOCK, PEER_HEADS, PEER_TOPK * PEER_TOPK)
        cand_i = (i1[..., :, None] * N_KEYS + i2[..., None, :]).reshape(TOK_BLOCK, PEER_HEADS, PEER_TOPK * PEER_TOPK)
        top_s, pos = lax.top_k(cand_s, PEER_TOPK)
        idx = jnp.take_along_axis(cand_i, pos, axis=-1)
        gate = jax.nn.softmax(top_s, axis=-1).astype(hb.dtype)
        u = expert_u[idx]
        act = jax.nn.gelu(jnp.einsum('thkd,td->thk', u, hb), approximate=False)
        vv = expert_v[idx]
        return jnp.einsum('thk,thkd->td', gate * act, vv)

    out = lax.map(block, hb_all)
    return out.reshape(B, S, D)

def first_inputs(seed: int = 0) -> dict:
    key = jax.random.key(seed)
    ks = iter(jax.random.split(key, 40))
    f32 = jnp.float32
    nrm = lambda shape, scale: jax.random.normal(next(ks), shape, f32) * scale
    gain = lambda shape: 1.0 + 0.02 * jax.random.normal(next(ks), shape, f32)
    L = DEPTH
    x = jax.random.normal(next(ks), (BATCH, SEQ, D_MODEL), f32)
    offset = jax.random.randint(next(ks), (BATCH, 1), 0, 64, dtype=jnp.int32) * CHUNK
    positions = offset + jnp.arange(SEQ, dtype=jnp.int32)[None, :]
    return {
        'x': x,
        'positions': positions,
        'g_mix': gain((L, D_MODEL)),
        'w_in': nrm((L, D_MODEL, IN_COLS), D_MODEL ** -0.5),
        'rwkv_mu': jax.random.uniform(next(ks), (L, RWKV_COLS), f32),
        'g_cq': gain((L, MLA_Q_RANK)),
        'g_ckv': gain((L, MLA_KV_RANK)),
        'w_uq': nrm((L, MLA_Q_RANK, MLA_HEADS * MLA_QK), MLA_Q_RANK ** -0.5),
        'w_uk': nrm((L, MLA_KV_RANK, MLA_HEADS * MLA_NOPE), MLA_KV_RANK ** -0.5),
        'w_uv': nrm((L, MLA_KV_RANK, MLA_HEADS * MLA_V), MLA_KV_RANK ** -0.5),
        'g_qnorm': gain((L, MLA_QK)),
        'g_knorm': gain((L, MLA_QK)),
        'g_attn_out': gain((L, MLA_HEADS * MLA_V)),
        'w0': -6.0 + 5.0 * jax.random.uniform(next(ks), (L, RWKV_DIM), f32),
        'w2': nrm((L, W_LORA, RWKV_DIM), 0.1),
        'a0': nrm((L, RWKV_DIM), 0.1),
        'a2': nrm((L, A_LORA, RWKV_DIM), 0.1),
        'g2': nrm((L, G_LORA, RWKV_DIM), G_LORA ** -0.5),
        'k_k': 0.85 + nrm((L, RWKV_DIM), 0.05),
        'k_a': 1.0 + nrm((L, RWKV_DIM), 0.05),
        'r_k': nrm((L, RWKV_HEADS, RWKV_HEAD), 0.1),
        'ln_x_w': gain((L, RWKV_DIM)),
        'ln_x_b': nrm((L, RWKV_DIM), 0.02),
        'w_o': nrm((L, MIX_WIDTH, D_MODEL), MIX_WIDTH ** -0.5),
        'g_ffn': gain((L, D_MODEL)),
        'w_pq': nrm((L, D_MODEL, PEER_HEADS * PEER_DQ), D_MODEL ** -0.5),
        'sub_keys': nrm((L, PEER_HEADS, 2, N_KEYS, PEER_DHALF), PEER_DHALF ** -0.5),
        'expert_u': nrm((L, N_EXPERTS, D_MODEL), D_MODEL ** -0.5),
        'expert_v': nrm((L, N_EXPERTS, D_MODEL), PEER_HEADS ** -0.5),
    }

def first_block(x, positions, g_mix, w_in, rwkv_mu, g_cq, g_ckv, w_uq, w_uk, w_uv, g_qnorm, g_knorm,
              g_attn_out, w0, w2, a0, a2, g2, k_k, k_a, r_k, ln_x_w, ln_x_b, w_o, g_ffn, w_pq,
              sub_keys, expert_u, expert_v):
    for l in range(DEPTH):
        h = rms_norm(x, g_mix[l])
        p = h @ w_in[l]
        y_a = mla_group(p[..., :MLA_COLS], positions, g_cq[l], g_ckv[l], w_uq[l], w_uk[l], w_uv[l],
                        g_qnorm[l], g_knorm[l], g_attn_out[l])
        y_b = rwkv7_group(p[..., MLA_COLS:], rwkv_mu[l], w0[l], w2[l], a0[l], a2[l], g2[l], k_k[l], k_a[l],
                          r_k[l], ln_x_w[l], ln_x_b[l])
        x = x + jnp.concatenate([y_a, y_b], axis=-1) @ w_o[l]
        x = x + peer_ffn(rms_norm(x, g_ffn[l]), w_pq[l], sub_keys[l], expert_u[l], expert_v[l])
    return x


CONV_CH = D_MODEL // 2
CONV_K = 31
CONV_GROUPS = 8
POOL_CH = D_MODEL // 2
POOL_WINDOWS = (2, 4, 8, 16)
N_POOL_GROUPS = len(POOL_WINDOWS)
POOL_GROUP_CH = POOL_CH // N_POOL_GROUPS
POOL_GROUP_OUT = D_MODEL // N_POOL_GROUPS
N_BRANCH = 2
COL_A_VAL = CONV_CH
COL_A_GATE = 2 * CONV_CH
COL_POOL = 2 * CONV_CH + POOL_CH
COL_GATE_A = COL_POOL + D_MODEL
IN_COLS_2 = COL_POOL + N_BRANCH * D_MODEL
D_FF = ((8 * D_MODEL // 3 + 127) // 128) * 128
FFN_K = 3
ALPHA = (2.0 * DEPTH) ** 0.25
BETA = (8.0 * DEPTH) ** -0.25
LN_EPS = 1e-5
N_MOD = 6


def layer_norm(x, g=None, b=None):
    xf = x.astype(jnp.float32)
    mu = jnp.mean(xf, axis=-1, keepdims=True)
    var = jnp.mean(jnp.square(xf - mu), axis=-1, keepdims=True)
    y = (xf - mu) * lax.rsqrt(var + LN_EPS)
    if g is not None:
        y = y * g.astype(jnp.float32) + b.astype(jnp.float32)
    return y.astype(x.dtype)

def causal_dwconv(x, w, b):
    k, ch = w.shape
    y = lax.conv_general_dilated(
        x, w[:, None, :].astype(x.dtype), window_strides=(1,),
        padding=[(k - 1, 0)], dimension_numbers=("NWC", "WIO", "NWC"),
        feature_group_count=ch)
    return y + b.astype(x.dtype)

def causal_multiscale_pool(u):
    bsz, s, _ = u.shape
    ug = u.reshape(bsz, s, N_POOL_GROUPS, POOL_GROUP_CH).astype(jnp.float32)
    cs = jnp.cumsum(ug, axis=1)
    pos = jnp.arange(s)
    outs = []
    for gi, w in enumerate(POOL_WINDOWS):
        c_g = cs[:, :, gi]
        lag = jnp.pad(c_g, ((0, 0), (w, 0), (0, 0)))[:, :s]
        cnt = jnp.minimum(pos + 1, w).astype(jnp.float32)[None, :, None]
        outs.append((c_g - lag) / cnt)
    pooled = jnp.stack(outs, axis=2)
    return (pooled - ug).astype(u.dtype)

def second_inputs(seed: int = 0) -> dict:
    key = jax.random.key(seed)
    ks = jax.random.split(key, 24)
    f32 = jnp.float32
    L = DEPTH

    def nrm(k, shape, scale):
        return jax.random.normal(k, shape, f32) * scale

    def gain(k, shape):
        return 1.0 + 0.05 * jax.random.normal(k, shape, f32)

    return {
        "x": jax.random.normal(ks[0], (BATCH, SEQ, D_MODEL), f32),
        "c": jax.random.normal(ks[1], (BATCH, D_MODEL), f32),
        "w_ada": nrm(ks[2], (L, D_MODEL, N_MOD * D_MODEL), 0.5 * D_MODEL ** -0.5),
        "b_ada": nrm(ks[3], (L, N_MOD * D_MODEL), 0.02),
        "w_in": nrm(ks[4], (L, D_MODEL, IN_COLS_2), D_MODEL ** -0.5),
        "w_dw_a": nrm(ks[5], (L, CONV_K, CONV_CH), CONV_K ** -0.5),
        "b_dw_a": nrm(ks[6], (L, CONV_CH), 0.02),
        "ln_a_g": gain(ks[7], (L, CONV_CH)),
        "ln_a_b": nrm(ks[8], (L, CONV_CH), 0.02),
        "w_pw_a": nrm(ks[9], (L, CONV_CH, D_MODEL), BETA * CONV_CH ** -0.5),
        "w_pool": nrm(ks[10], (L, N_POOL_GROUPS, POOL_GROUP_CH, POOL_GROUP_OUT), BETA * POOL_GROUP_CH ** -0.5),
        "pool_scale": gain(ks[11], (L, D_MODEL)),
        "w_out": nrm(ks[12], (L, D_MODEL, D_MODEL), BETA * D_MODEL ** -0.5),
        "ln1_g": gain(ks[13], (L, D_MODEL)),
        "ln1_b": nrm(ks[14], (L, D_MODEL), 0.02),
        "w_up": nrm(ks[15], (L, D_MODEL, 2 * D_FF), BETA * D_MODEL ** -0.5),
        "w_dw_f": nrm(ks[16], (L, FFN_K, 2 * D_FF), FFN_K ** -0.5),
        "b_dw_f": nrm(ks[17], (L, 2 * D_FF), 0.02),
        "w_down": nrm(ks[18], (L, D_FF, D_MODEL), BETA * D_FF ** -0.5),
        "ln2_g": gain(ks[19], (L, D_MODEL)),
        "ln2_b": nrm(ks[20], (L, D_MODEL), 0.02),
    }

def second_block(x, c, w_ada, b_ada, w_in, w_dw_a, b_dw_a, ln_a_g, ln_a_b, w_pw_a,
              w_pool, pool_scale, w_out, ln1_g, ln1_b, w_up, w_dw_f, b_dw_f,
              w_down, ln2_g, ln2_b):
    bsz, s, _ = x.shape
    for l in range(DEPTH):
        mod = jax.nn.silu(c) @ w_ada[l] + b_ada[l]
        sh1, sc1, g1, sh2, sc2, g2 = jnp.split(mod, N_MOD, axis=-1)

        h = layer_norm(x) * (1.0 + sc1[:, None]) + sh1[:, None]
        proj = h @ w_in[l]
        a_val, a_gate, u_pool, gate_a, gate_b = jnp.split(
            proj, [COL_A_VAL, COL_A_GATE, COL_POOL, COL_GATE_A], axis=-1)

        ya = a_val * jax.nn.sigmoid(a_gate)
        ya = causal_dwconv(ya, w_dw_a[l], b_dw_a[l])
        ya = jax.nn.silu(layer_norm(ya, ln_a_g[l], ln_a_b[l]))
        ya = ya @ w_pw_a[l]

        pooled = causal_multiscale_pool(u_pool)
        yb = jnp.einsum("bsgc,gcd->bsgd", pooled, w_pool[l]).reshape(bsz, s, D_MODEL)
        yb = yb * pool_scale[l]

        merged = jax.nn.sigmoid(gate_a) * ya + jax.nn.sigmoid(gate_b) * yb
        mix = merged @ w_out[l]
        x = layer_norm(ALPHA * x + g1[:, None] * mix, ln1_g[l], ln1_b[l])

        h = layer_norm(x) * (1.0 + sc2[:, None]) + sh2[:, None]
        up = causal_dwconv(h @ w_up[l], w_dw_f[l], b_dw_f[l])
        v, gt = jnp.split(up, 2, axis=-1)
        f = (jax.nn.gelu(gt) * v) @ w_down[l]
        x = layer_norm(ALPHA * x + g2[:, None] * f, ln2_g[l], ln2_b[l])
    return x


def setup_inputs(seed=0):
    out = dict(first_inputs(seed))
    for name, value in second_inputs(seed + 1).items():
        if name != "x":
            out[name + "_2"] = value
    return out


def reference(
    x, positions, g_mix, w_in, rwkv_mu, g_cq, g_ckv, w_uq, w_uk, w_uv, g_qnorm, g_knorm,
    g_attn_out, w0, w2, a0, a2, g2, k_k, k_a, r_k, ln_x_w, ln_x_b, w_o, g_ffn, w_pq, sub_keys,
    expert_u, expert_v, c_2, w_ada_2, b_ada_2, w_in_2, w_dw_a_2, b_dw_a_2, ln_a_g_2, ln_a_b_2,
    w_pw_a_2, w_pool_2, pool_scale_2, w_out_2, ln1_g_2, ln1_b_2, w_up_2, w_dw_f_2, b_dw_f_2,
    w_down_2, ln2_g_2, ln2_b_2,
):
    x = first_block(
        x, positions, g_mix, w_in, rwkv_mu, g_cq, g_ckv, w_uq, w_uk, w_uv, g_qnorm, g_knorm,
        g_attn_out, w0, w2, a0, a2, g2, k_k, k_a, r_k, ln_x_w, ln_x_b, w_o, g_ffn, w_pq,
        sub_keys, expert_u, expert_v,
    )
    return second_block(
        x, c_2, w_ada_2, b_ada_2, w_in_2, w_dw_a_2, b_dw_a_2, ln_a_g_2, ln_a_b_2, w_pw_a_2,
        w_pool_2, pool_scale_2, w_out_2, ln1_g_2, ln1_b_2, w_up_2, w_dw_f_2, b_dw_f_2, w_down_2,
        ln2_g_2, ln2_b_2,
    )


_drawn_inputs = setup_inputs


def setup_inputs(seed=0):
    import zlib

    import numpy as np

    out = dict(_drawn_inputs(seed))
    spreads = {}
    factors = {'g_cq': 2.83,
     'g_qnorm': 2.874,
     'g_knorm': 3.053,
     'g_attn_out': 9.706,
     'w2': 2.963,
     'a0': 2.846,
     'ln_x_w': 14.013,
     'ln_x_b': 13.756,
     'g_ffn': 8.037,
     'b_ada_2': 8.0,
     'b_dw_a_2': 8.0,
     'ln_a_g_2': 200.0,
     'ln_a_b_2': 200.0,
     'pool_scale_2': 164.107,
     'ln1_b_2': 2.854,
     'b_dw_f_2': 27.502,
     'ln2_b_2': 2.831}
    for name, (base, spread) in spreads.items():
        noise = np.random.default_rng([zlib.crc32(name.encode()), seed]).standard_normal(out[name].shape)
        drawn = base * np.exp(spread * noise) if base else spread * noise
        out[name] = __import__('jax').numpy.asarray(drawn.astype(out[name].dtype))
    for name, factor in factors.items():
        out[name] = (out[name] * factor).astype(out[name].dtype)
    return out
```

```python
from contextlib import ExitStack

import numpy as np

import concourse.bass as bass
from concourse import mybir

ALU = mybir.AluOpType
ACT = mybir.ActivationFunctionType
F32 = mybir.dt.float32
I32 = mybir.dt.int32
U32 = mybir.dt.uint32
AX = mybir.AxisListType.X

P = 128
S = 512
NT = S // P
D = 1024
KD = D // P
EPS = 1e-6
LN_EPS = 1e-5

H = 8
DQK = 96
DN = 64
DR = 32
HALF = DR // 2
QR = 384
KVR = 256
MLA_COLS = QR + KVR + DR
RD = 512
RM = RD // P
LN_X_EPS = 64e-5
KAPPA = float(np.exp(-0.5))
LEVELS = 7
NK = 128
TOPK = 16
NSEL = H * TOPK
RING = 8
GRP = 2
CONV_K = 31
POOL = (2, 4, 8, 16)
D_FF = 2816
NF = D_FF // P
ALPHA = 2.0 ** 0.25

CH = 4096
NWR = 3

JOBS = [
    ("hT", 4, 4), ("pm", 4, 4), ("cT", 3, 2), ("q", 4, 4), ("kv", 4, 4), ("qkT", 8, 8),
    ("att", 32, 64), ("pr", 14, 0), ("lora", 12, 0), ("kn", 0, 4), ("bonus", 0, 1),
    ("tok", 4, 8),
    ("pair0", 26, 34), ("pair1", 26, 34), ("pair2", 26, 34), ("pair3", 26, 34),
    ("yT", 4, 4), ("wo", 0, 8), ("hT2", 4, 4), ("pq", 8, 8), ("s", 16, 0), ("ada", 12, 0),
    ("modc", 0, 1), ("acc", 0, 8), ("hT3", 4, 4), ("in2", 24, 4), ("ln", 0, 2), ("pw", 0, 8),
    ("yb", 0, 8), ("wout", 0, 8), ("hT4", 4, 4), ("up", 44, 0), ("down", 4, 4), ("end", 0, 0),
]
FIRST_A, FIRST_D = {}, {}
_a = _d = 0
for _name, _na, _nd in JOBS:
    FIRST_A[_name], FIRST_D[_name] = _a, _d
    _a, _d = _a + _na, _d + _nd


def _cols(items):
    at, n = {}, 0
    for name, w in items:
        at[name] = (n, n + w)
        n += w
    return at, n


CONST, NCONST = _cols([("ident", P), ("ones", P), ("zero", P), ("lowrow", P), ("negrow", P),
                       ("level", LEVELS * P), ("strict", P), ("incl", P), ("heads", P), ("head2", 2),
                       ("invfreq", HALF), ("iota", TOPK), ("cnt", 4 * 16), ("mhalf", 1)])
VECS = [("g_mix", 8), ("mu", 14), ("g_cq", 3), ("g_ckv", 2), ("w0", 4), ("a0", 4), ("k_k", 4), ("k_a", 4),
        ("r_k", 4), ("c", 8), ("b_mod", 32), ("w_conv", 4 * CONV_K), ("b_conv", 4), ("ln_a_g", 4),
        ("ln_a_b", 4), ("pool_scale", 8), ("w_ff", 44 * 3), ("b_ff", 44)]
VEC, NVEC = _cols(VECS)
ROW1, NROW1 = _cols([("g_q", DQK), ("g_k", DQK), ("g_attn", RD), ("ln_x_w", RD), ("ln_x_b", RD)])
ROW2, NROW2 = _cols([("b_g1", D), ("b_g2", D), ("ln1_g", D), ("ln1_b", D), ("ln2_g", D), ("ln2_b", D)])


def constants():
    c = np.zeros((P, NCONST), np.float32)

    def put(name, v):
        a, b = CONST[name]
        c[:, a:b] = v

    i, j = np.arange(P)[:, None], np.arange(P)[None, :]
    put("ident", i == j)
    put("ones", 1.0)
    lev = [((j & (1 << l)) > 0) & ((i & (1 << l)) == 0) & ((i >> (l + 1)) == (j >> (l + 1)))
           for l in range(LEVELS)]
    put("level", np.concatenate(lev, 1))
    put("strict", i < j)
    put("incl", i <= j)
    put("heads", (i // 64) == (j // 64))
    put("head2", (i // 64) == np.arange(2)[None, :])
    put("lowrow", (j < 64) & (i == 0))
    put("negrow", np.where((j >= 64) & (i == 0), np.float32(-1e30), np.float32(0)))
    put("invfreq", (np.float32(10000.0) ** (-np.arange(HALF, dtype=np.float32) / np.float32(HALF)))[None, :])
    put("iota", np.arange(TOPK)[None, :])
    put("mhalf", -0.5)
    cnt = [1.0 / np.minimum(np.arange(16) + 1, w) for w in POOL]
    put("cnt", np.concatenate(cnt)[None, :])
    return c


def build(nc, x, pos, cst, vec, row1, gffn, row2, w_in, w_uq, w_uk, w_uv, lora, w_o, w_pq, keys, uv,
          w_ada, w_in2, w_pw, w_pool, w_out, w_up, w_down, out, dbg=None, upto="end", dumps=()):
    with ExitStack() as ctx:
        def sb(name, shape, dt=F32):
            return ctx.enter_context(nc.sbuf_tensor(name, shape, dt))

        X = sb("X", [P, NT, D])
        HN = sb("HN", [P, NT, D])
        HT = sb("HT", [P, KD, S])
        WR = sb("WR", [P, NWR, CH])
        AR = sb("AR", [P, 22784])
        C = sb("C", [P, NCONST])
        V = sb("V", [P, NVEC])
        RW = sb("RW", [P, 2048])
        SC = sb("SC", [P, 1240])
        PA = ctx.enter_context(nc.psum_tensor("PA", [P, 4, 512], F32))
        PD = ctx.enter_context(nc.psum_tensor("PD", [P, 4, 512], F32))

        def cc(name):
            return C[:, CONST[name][0]:CONST[name][1]]

        def vv(name, m=None):
            a, b = VEC[name]
            return V[:, a:b] if m is None else V[:, a + m:a + m + 1]

        def r1(name):
            return RW[:, ROW1[name][0]:ROW1[name][1]]

        def ar(a, n, *dims):
            v = AR[:, a:a + n]
            if len(dims) == 1:
                return v.rearrange("p (a b) -> p a b", a=dims[0])
            if len(dims) == 2:
                return v.rearrange("p (a b c) -> p a b c", a=dims[0], b=dims[1])
            return v

        ident = cc("ident")
        LV = cc("level").rearrange("p (l n) -> p l n", l=LEVELS)

        names = ["a_full", "a_free", "d_full", "d_free", "dve", "act", "pool",
                 "in_x", "in_const", "in_gffn", "in_row2", "out_done",
                 "xn", "xn2", "xn3", "xn4",
                 "cn", "qk_normed", "kr", "smax", "probs", "o_normed", "raw_used", "lora_in", "prt",
                 "kx_sq", "rkk", "rexp", "rexp_used", "rhat", "vcopy",
                 "mt", "ct", "x1t", "tmid", "ycomb",
                 "topk", "idx", "dots", "geluv", "diag", "uv_used", "accs", "csil",
                 "bufs", "sg", "conv", "convsq", "rstd_a", "silu_in", "silu", "pooled", "merged",
                 "lnx", "upraw_used", "gelu_in", "gelu", "ff", "ffadd", "fin", "row2free",
                 "peer_clear", "sscan", "Lm", "ffgelu", "var", "rstd"]
        s = {}
        for nm in names:
            s[nm] = ctx.enter_context(nc.semaphore(nm))
        w_sem = [ctx.enter_context(nc.semaphore(f"w_slot{i}")) for i in range(NWR)]
        uv_full = [ctx.enter_context(nc.semaphore(f"uv_full{i}")) for i in range(RING)]
        n = {nm: 0 for nm in names}

        def tell(ins, name):
            n[name] += 1
            ins.then_inc(s[name], 1)

        ORDER = [j[0] for j in JOBS]

        def upon(phase):
            return ORDER.index(phase) <= ORDER.index(upto)

        QK = ar(0, 6144).rearrange("p (t g d) -> p t g d", t=NT, g=2 * H)
        QKT = ar(6144, 8192, 2 * H)
        VA = ar(14336, 2048, NT)
        CT = ar(16384, 2560, 5)
        PM = ar(18944, 2688, NT)
        PB = ar(18944, 1024, 2)
        PT = ar(19968, 1024, 2)
        RT, KT, VT, LT = (ar(2048 * i, 2048, 4) for i in range(4))
        SG, CS, AT, KK, GT, E1, E2 = (ar(2048 * i, 2048, 4) for i in range(4, 11))
        RAW = ar(18432, 4 * 513, 4)
        VTOK = HT[:, 0:4, :]
        KTOK, BTOK = SG, CS
        PAIR1 = ar(4096, 4096, 4, 2)
        PAIR2 = ar(18432, 4096, 4, 2)
        UV = AR[:, 0:RING * 2048].rearrange("p (r n) -> p r n", r=RING)
        QPT = ar(0, 8192, 16)
        SS = [HT[:, 0:4, :].rearrange("p a b -> p (a b)"), HT[:, 4:8, :].rearrange("p a b -> p (a b)"),
              ar(16384, 2048), ar(18432, 2048)]
        CAND = ar(20480, 2048)
        GF = ar(20480, 1024)
        SGA = ar(0, 2048, 4)
        PO = ar(0, 2048, 4)
        YAP = ar(2048, 4 * 542, 4)
        UP = ar(4216, 4 * 528, 4)
        CV = ar(6328, 2048, 4)
        GA = ar(8376, 4096, 8)
        GB = ar(12472, 4096, 8)
        R2 = ar(16600, NROW2)
        MG = HT
        EQ = VT
        SILU = ar(0, 1024, 8)
        MODROW = ar(1024, 4096)
        FT = ar(0, NF * S, NF)
        UR = ar(11264, 4 * 514, 4)
        UC = ar(13320, 4 * 512, 4)

        sc_at = [0]

        def small(w, dt=F32):
            a = sc_at[0]
            sc_at[0] += w
            assert sc_at[0] <= 1240, sc_at[0]
            v = SC[:, a:a + w]
            return v if dt is F32 else v.bitcast(dt)

        st_a = small(64)
        rsum = small(32)
        nmax = small(32)
        cosb = small(64)
        sinb = small(64)
        bon = small(32)
        fdec = small(16)
        modc = small(32)
        t_end = sc_at[0]
        posf = small(4)
        posi = small(4, I32)
        ang = small(64)
        kint = small(64)
        tmid = small(512)
        csil = small(8)
        sc_at[0] = t_end
        s1v = small(256)
        i1u = small(256, U32)
        tpv = small(128)
        tpu = small(128, U32)
        gmx = small(24)
        scr_free = sc_at[0]
        lvl = C[:, CONST["level"][0]:CONST["level"][0] + 1280]
        DG = lvl[:, 0:1024].rearrange("p (r n) -> p r n", r=RING)
        GATE = lvl[:, 1024:1280].rearrange("p (r n) -> p r n", r=2)
        IDX = C[:, CONST["lowrow"][0]:CONST["negrow"][1]].rearrange("p (r n) -> p r n", r=2).bitcast(U32)
        DOT = small(8).rearrange("p (r n) -> p r n", r=4)
        GEL = small(8).rearrange("p (r n) -> p r n", r=4)
        csil2 = small(8)
        ffst = lvl[:, 0:96]

        chunks = []

        def col_chunk(w, c0, w_cols, chan, job, k=KD):
            chunks.append((k * w_cols, w[:, c0:c0 + w_cols].rearrange("(k p) n -> p k n", p=P), k, chan, job))

        col_chunk(w_in, 0, 512, "a", FIRST_A["pm"] + 3)
        col_chunk(w_in, 512, 160, "d", FIRST_D["pm"] + 3)
        col_chunk(w_uq, 0, 768, "d", FIRST_D["q"] + 3, 3)
        chunks.append((1024, w_uk.rearrange("(k p) n -> p k n", p=P), 2, "d", FIRST_D["kv"] + 3))
        chunks.append((1024, w_uv.rearrange("(k p) n -> p k n", p=P), 2, "d", FIRST_D["kv"] + 3))
        for i, w in enumerate((512, 512, 512, 256)):
            col_chunk(w_in, MLA_COLS + 512 * i, w, "a", FIRST_A["pr"] + min(4 * i + 3, 13))
        chunks.append((1024, lora, 1, "a", FIRST_A["lora"] + 11))
        for i in range(2):
            col_chunk(w_o, 512 * i, 512, "d", FIRST_D["wo"] + 4 * i + 3)
        for i in range(4):
            col_chunk(w_pq, 512 * i, 512, "d", FIRST_D["pq"] + 2 * i + 1)
        chunks.append((2048, keys, 1, "a", FIRST_A["s"] + 15))
        for i in range(12):
            col_chunk(w_ada, 512 * i, 512, "a", FIRST_A["ada"] + i)
        in2_order = [1, 0, 2, 3, 4, 5, 6]
        in2_last = [("a", 3), ("d", 3), ("a", 7), ("a", 11), ("a", 15), ("a", 19), ("a", 23)]
        for i, (ch, j) in zip(in2_order, in2_last):
            col_chunk(w_in2, 512 * i, 512, ch, (FIRST_A if ch == "a" else FIRST_D)["in2"] + j)
        chunks.append((4096, w_pw.rearrange("(k p) n -> p k n", p=P), 4, "d", FIRST_D["pw"] + 7))
        chunks.append((1024, w_pool.rearrange("g p n -> p g n"), 4, "d", FIRST_D["yb"] + 7))
        for i in range(2):
            col_chunk(w_out, 512 * i, 512, "d", FIRST_D["wout"] + 4 * i + 3)
        for i in range(11):
            col_chunk(w_up, 512 * i, 512, "a", FIRST_A["up"] + 4 * i + 3)
        for i in range(6):
            k = min(4, NF - 4 * i)
            chunks.append((k * D, w_down[512 * i:512 * i + k * P, :].rearrange("(k p) n -> p k n", p=P), k, "down", i))
        s_down = ctx.enter_context(nc.semaphore("down_chunk"))
        CNUM = {}
        at = 0
        for nm, cnt in (("pm", 2), ("uq", 1), ("uk", 1), ("uv", 1), ("pr", 4), ("lora", 1), ("wo", 2), ("pq", 4),
                        ("keys", 1), ("ada", 12), ("in2", 7), ("pw", 1), ("pool", 1), ("wout", 2), ("up", 11),
                        ("down", 6)):
            CNUM[nm] = at
            at += cnt
        assert at == len(chunks)
        last_chunk = {"hT": 2, "pm": 2, "cT": 2, "q": 3, "kv": 5, "qkT": 5, "att": 5, "pr": 9}

        def chunk(pe, number, k=None):
            cols, _, kk, _, _ = chunks[number]
            pe.wait_ge(w_sem[number % NWR], 16 * (number // NWR + 1))
            return WR[:, number % NWR, 0:cols].rearrange("p (k n) -> p k n", k=k or kk)

        block = ctx.enter_context(nc.Block())

        @block.sync
        def _(sp):
            for t in range(NT):
                sp.dma_start(X[:, t, :], x[P * t:P * t + P, :]).then_inc(s["in_x"], 16)
            sp.dma_start(C[:, :], cst).then_inc(s["in_const"], 16)
            sp.dma_start(V[:, :], vec).then_inc(s["in_const"], 16)
            sp.dma_start(RW[:, 0:NROW1], row1).then_inc(s["in_const"], 16)
            sp.dma_start(posi[:, :], pos).then_inc(s["in_const"], 16)

            def load(i):
                cols, src, k, _, _ = chunks[i]
                if i >= NWR:
                    _, _, _, chan, job = chunks[i - NWR]
                    if chan == "down":
                        sp.wait_ge(s_down, job + 1)
                    else:
                        sp.wait_ge(s[chan + "_full"], job + 1)
                dst = WR[:, i % NWR, 0:cols]
                if len(src.shape) == 3:
                    dst = dst.rearrange("p (k n) -> p k n", k=k)
                sp.dma_start(dst, src).then_inc(w_sem[i % NWR], 16)

            stop = last_chunk.get(upto, len(chunks))
            if upto.startswith("pair") or upto in ("lora", "kn", "bonus", "tok"):
                stop = 10
            if upto in ("yT", "wo"):
                stop = 12
            if upto in ("hT2", "pq", "s"):
                stop = 17
            if upto in ("ada", "modc", "acc"):
                stop = 29
            if upto in ("hT3", "in2", "ln"):
                stop = 36
            for i in range(stop):
                load(i)
                if i == CNUM["pq"]:
                    sp.wait_ge(s["d_free"], FIRST_D["wo"])
                    sp.dma_start(GF, gffn).then_inc(s["in_gffn"], 16)
                if i == CNUM["wout"]:
                    sp.wait_ge(s["row2free"], 1)
                    sp.dma_start(R2, row2).then_inc(s["in_row2"], 16)
            if dbg is None:
                for t in range(NT):
                    sp.wait_ge(s["fin"], t + 1)
                    sp.dma_start(out[P * t:P * t + P, :], X[:, t, :]).then_inc(s["out_done"], 16)
                sp.wait_ge(s["out_done"], 16 * NT)
            else:
                sp.wait_ge(s["fin"], 3)
                n_out = 0
                flat = {"X": X, "HN": HN, "HT": HT}
                for nm, a_, b_ in dumps:
                    z = flat[nm][:, :, :].rearrange("p a b -> p (a b)") if nm in flat else {"AR": AR, "SC": SC, "C": C, "RW": RW}[nm]
                    sp.dma_start(dbg[:, n_out:n_out + b_ - a_], z[:, a_:b_]).then_inc(s["out_done"], 16)
                    n_out += b_ - a_
                sp.wait_ge(s["out_done"], 16 * len(dumps))

        @block.tensor
        def _(pe):
            cnt = {"a": 0, "d": 0}

            def bank(chan):
                j = cnt[chan]
                cnt[chan] += 1
                if j >= 4:
                    pe.wait_ge(s[chan + "_free"], j - 3)
                return (PA if chan == "a" else PD)[:, j % 4, :]

            def full(chan, ins):
                ins.then_inc(s[chan + "_full"], 1)

            def transposes(chan, srcs, rows=P, cols=P):
                b = bank(chan)
                for i, src in enumerate(srcs):
                    ins = nc.tensor.transpose(b[0:cols, rows * i:rows * i + rows], src, ident[0:rows, 0:rows])
                full(chan, ins)

            def product(chan, pairs, w=512, rows=P):
                b = bank(chan)[0:rows, 0:w]
                for i, (lhsT, rhs) in enumerate(pairs):
                    ins = nc.tensor.matmul(b, lhsT, rhs, start=(i == 0), stop=(i == len(pairs) - 1))
                full(chan, ins)

            def turn(ready, count=1):
                for k in range(KD):
                    if k == 0:
                        pe.wait_ge(s[ready], NT * count)
                    transposes("ad"[k % 2], [HN[:, t, P * k:P * k + P] for t in range(NT)])

            pe.wait_ge(s["in_const"], 64)
            turn("xn")

            pe.wait_ge(s["a_free"], FIRST_A["pm"])
            pe.wait_ge(s["d_free"], FIRST_D["pm"])
            if upon("pm"):
                w0_, w1_ = chunk(pe, 0), chunk(pe, 1)
                for t in range(NT):
                    product("a", [(HT[:, k, P * t:P * t + P], w0_[:, k, :]) for k in range(KD)])
                for t in range(NT):
                    product("d", [(HT[:, k, P * t:P * t + P], w1_[:, k, :]) for k in range(KD)], 160)
            if upon("cT"):
                pe.wait_ge(s["cn"], NT)
                for g in range(5):
                    transposes("ad"[g % 2], [PM[:, t, P * g:P * g + P] for t in range(NT)])
                pe.wait_ge(s["a_free"], FIRST_A["q"])
                pe.wait_ge(s["d_free"], FIRST_D["q"])
            if upon("q"):
                uq = chunk(pe, CNUM["uq"])
                for t in range(NT):
                    for half in range(2):
                        product("ad"[half], [(CT[:, k, P * t:P * t + P], uq[:, k, 384 * half:384 * half + 384])
                                             for k in range(3)], 384)
            if upon("kv"):
                uk, uvw = chunk(pe, CNUM["uk"]), chunk(pe, CNUM["uv"])
                for t in range(NT):
                    product("a", [(CT[:, 3 + k, P * t:P * t + P], uk[:, k, :]) for k in range(2)])
                    product("d", [(CT[:, 3 + k, P * t:P * t + P], uvw[:, k, :]) for k in range(2)])
            if upon("qkT"):
                pe.wait_ge(s["qk_normed"], NT)
                for g in range(2 * H):
                    transposes("ad"[g % 2], [QK[:, t, g, :] for t in range(NT)], P, DQK)
                pe.wait_ge(s["a_free"], FIRST_A["att"])
                pe.wait_ge(s["d_free"], FIRST_D["att"])
            if upon("att"):
                units = [(t, h) for t in range(NT) for h in range(H)]
                for u in range(len(units) + 2):
                    if u < len(units):
                        t, h = units[u]
                        nk = P * (t + 1)
                        b = bank("a")
                        nc.tensor.matmul(b[:, 0:nk], QKT[0:DQK, h, P * t:P * t + P], QKT[0:DQK, H + h, 0:nk],
                                         start=True, stop=False)
                        full("a", nc.tensor.matmul(b[:, nk - P:nk], cc("lowrow")[0:1, :], cc("negrow")[0:1, :],
                                                   start=False, stop=True))
                    if 1 <= u <= len(units):
                        t, h = units[u - 1]
                        pe.wait_ge(s["probs"], u)
                        transposes("d", [PB[:, (u - 1) % 2, P * j:P * j + P] for j in range(t + 1)])
                    if u >= 2:
                        t, h = units[u - 2]
                        pe.wait_ge(s["d_free"], FIRST_D["att"] + (1 if u == 2 else 2 * (u - 2)))
                        product("d", [(PT[:, (u - 2) % 2, P * j:P * j + P], VA[:, j, 64 * h:64 * h + 64])
                                      for j in range(t + 1)], 64)
            if upon("pr"):
                for m in range(14):
                    w = chunk(pe, CNUM["pr"] + m // 4)
                    product("a", [(w[:, k, P * (m % 4):P * (m % 4) + P], HT[:, k, :]) for k in range(KD)])
            if upon("lora"):
                lw = chunk(pe, CNUM["lora"], 1)[:, 0, :]
                pe.wait_ge(s["lora_in"], 2)
                pe.wait_ge(s["prt"], 14)
                for m in range(4):
                    product("a", [(lw[0:64, P * m:P * m + P], LT[0:64, 2, :])])
                for m in range(4):
                    product("a", [(lw[64:128, P * m:P * m + P], LT[64:128, 0, :])])
                for t in range(NT):
                    product("a", [(LT[:, 3, P * t:P * t + P], lw[:, 512:1024])])
            if upon("kn"):
                for m in range(4):
                    pe.wait_ge(s["kx_sq"], m + 1)
                    product("d", [(cc("heads"), E1[:, m, :])])
            if upon("bonus"):
                pe.wait_ge(s["rkk"], 1)
                b = bank("d")
                for t in range(NT):
                    for m in range(4):
                        o = 8 * t + 2 * m
                        ins = nc.tensor.matmul(b[:, o:o + 2], E1[:, m, P * t:P * t + P], cc("head2"),
                                               start=True, stop=True)
                full("d", ins)
            if upon("tok"):
                for t in range(NT):
                    transposes("d", [VT[:, m, P * t:P * t + P] for m in range(4)])
                pe.wait_ge(s["rhat"], 4)
                for t in range(NT):
                    transposes("a", [KT[:, m, P * t:P * t + P] for m in range(4)])
                    transposes("d", [AT[:, m, P * t:P * t + P] for m in range(4)])
            for pr in range(4):
                if not upon(f"pair{pr}"):
                    break
                fa, fd = FIRST_A[f"pair{pr}"], FIRST_D[f"pair{pr}"]
                if pr == 0:
                    pe.wait_ge(s["a_free"], fa)
                    pe.wait_ge(s["d_free"], fd)
                for hh in range(2):
                    o = 64 * hh
                    kt, bt, qt, rt = (Z[o:o + 64, pr, :] for Z in (KT, AT, KK, RT))
                    for left, right in ((bt, qt), (bt, rt), (kt, qt), (kt, rt)):
                        b = bank("d")
                        for c in range(NT):
                            sl = slice(P * c, P * c + P)
                            ins = nc.tensor.matmul(b[:, sl], left[:, sl], right[:, sl], start=True, stop=True)
                        full("d", ins)
                for hh in range(2):
                    pe.wait_ge(s["x1t"], 2 * pr + hh + 1)
                    transposes("a", [PAIR1[:, 3, hh, P * c:P * c + P] for c in range(NT)])
                dn = fd + 8
                an = fa + 2
                for lev in range(1, LEVELS):
                    last = lev == LEVELS - 1
                    for hh in range(2):
                        if lev == 1:
                            pe.wait_ge(s["a_free"], fa + hh + 1)
                        else:
                            pe.wait_ge(s["d_free"], dn - (2 if hh == 0 else 0))
                        pe.wait_ge(s["ct"], 12 * pr + 2 * (lev - 1) + hh + 1)
                        b = bank("a")
                        for c in range(NT):
                            sl = slice(P * c, P * c + P)
                            ins = nc.tensor.matmul(b[:, sl], PAIR2[:, 1, hh, sl], PAIR2[:, 2, hh, sl],
                                                   start=True, stop=True)
                        full("a", ins)
                    for hh in range(2):
                        an += 1
                        pe.wait_ge(s["a_free"], an)
                        b = bank("d")
                        for c in range(NT):
                            sl = slice(P * c, P * c + P)
                            ins = nc.tensor.matmul(b[:, sl], PAIR2[:, 3, hh, sl], PAIR1[:, 3, hh, sl],
                                                   start=True, stop=True)
                        full("d", ins)
                        dn += 1
                        if not last:
                            b = bank("d")
                            for c in range(NT):
                                sl = slice(P * c, P * c + P)
                                ins = nc.tensor.matmul(b[:, sl], PAIR1[:, 3, hh, sl], PAIR2[:, 3, hh, sl],
                                                       start=True, stop=True)
                            full("d", ins)
                            dn += 1
                pe.wait_ge(s["d_free"], dn)
                f2 = slice(P * pr, P * pr + P)
                for c in range(NT):
                    sl = slice(P * c, P * c + P)
                    pe.wait_ge(s["tmid"], pr + 1)
                    if c:
                        pe.wait_ge(s["d_free"], dn + c)
                    b = bank("a")
                    for hh in range(2):
                        o, hv = b[:, 64 * hh:64 * hh + 64], slice(P * pr + 64 * hh, P * pr + 64 * hh + 64)
                        nc.tensor.matmul(o, KK[:, pr, sl], tmid[:, hv], start=True, stop=False)
                        ins = nc.tensor.matmul(o, PAIR1[:, 0, hh, sl], VTOK[:, c, hv], start=False, stop=True)
                    full("a", ins)
                    an += 1
                    pe.wait_ge(s["a_free"], an)
                    b = bank("a")
                    for hh in range(2):
                        ins = nc.tensor.matmul(b[:, 64 * hh:64 * hh + 64], PAIR1[:, 3, hh, sl],
                                               PAIR2[:, 3, 0, 64 * hh:64 * hh + 64], start=True, stop=True)
                    full("a", ins)
                    an += 1
                    pe.wait_ge(s["a_free"], an)
                    b = bank("a")
                    for hh in range(2):
                        o, hv = b[:, 64 * hh:64 * hh + 64], slice(P * pr + 64 * hh, P * pr + 64 * hh + 64)
                        nc.tensor.matmul(o, RT[:, pr, sl], tmid[:, hv], start=True, stop=False)
                        nc.tensor.matmul(o, PAIR1[:, 1, hh, sl], VTOK[:, c, hv], start=False, stop=False)
                        ins = nc.tensor.matmul(o, PAIR1[:, 2, hh, sl], PAIR2[:, 3, 1, 64 * hh:64 * hh + 64],
                                               start=False, stop=True)
                    full("a", ins)
                    an += 1
                    product("d", [(ident, tmid[:, P * pr:P * pr + P]), (KTOK[:, c, f2], VTOK[:, c, f2]),
                                  (BTOK[:, c, f2], PAIR2[:, 3, 1, 0:P])], P)
            if upon("yT"):
                turn("ycomb")
            if upon("wo"):
                pe.wait_ge(s["a_free"], FIRST_A["wo"])
                pe.wait_ge(s["d_free"], FIRST_D["wo"])
                for half in range(2):
                    w = chunk(pe, CNUM["wo"] + half)
                    for t in range(NT):
                        product("d", [(HT[:, k, P * t:P * t + P], w[:, k, :]) for k in range(KD)])
            if upon("hT2"):
                turn("xn2")
            if upon("pq"):
                pe.wait_ge(s["a_free"], FIRST_A["pq"])
                pe.wait_ge(s["d_free"], FIRST_D["pq"])
                for m in range(16):
                    w = chunk(pe, CNUM["pq"] + m // 4)
                    product("ad"[m % 2], [(w[:, k, P * (m % 4):P * (m % 4) + P], HT[:, k, :]) for k in range(KD)])
            if upon("s"):
                pe.wait_ge(s["a_free"], FIRST_A["s"])
                pe.wait_ge(s["d_free"], FIRST_D["ada"])
                kw = chunk(pe, CNUM["keys"], 16)
                for t in range(NT):
                    for g4 in range(4):
                        b = bank("a")
                        for i in range(4):
                            g = 4 * g4 + i
                            ins = nc.tensor.matmul(b[:, P * i:P * i + P], QPT[:, g, P * t:P * t + P], kw[:, g, :],
                                                   start=True, stop=True)
                        full("a", ins)
            if upon("ada"):
                pe.wait_ge(s["csil"], 8)
                for i in range(12):
                    w = chunk(pe, CNUM["ada"] + i)
                    b = bank("a")
                    for k in range(KD):
                        ins = nc.tensor.matmul(b, SILU[:, k, :], w[:, k, :], start=(k == 0), stop=(k == KD - 1))
                    full("a", ins)
            if upon("modc"):
                pe.wait_ge(s["a_free"], FIRST_A["hT3"])
                b = bank("d")
                for i in range(32):
                    ins = nc.tensor.matmul(b[:, i:i + 1], MODROW[0:1, P * i:P * i + P], cc("ones")[0:1, 0:1],
                                           start=True, stop=True)
                full("d", ins)
            if upon("acc"):
                fours = cc("ones")[0:1, :].unsqueeze(1).broadcast_to([1, 4, P])
                for t in range(NT):
                    acc = [bank("d"), bank("d")]
                    for half in range(2):
                        nc.tensor.matmul(acc[half], cc("zero")[0:1, :], fours, start=True, stop=False)
                    with pe.Fori(0, NSEL // RING) as it:
                        for j in range(RING):
                            pe.wait_ge(s["diag"], it * RING + (NSEL * t + j + 1))
                            for half in range(2):
                                ins = nc.tensor.matmul(acc[half], DG[:, j, :],
                                                       UV[:, j, D + 512 * half:D + 512 * half + 512],
                                                       start=False, stop=False)
                            ins.then_inc(s["uv_used"], 1)
                    for half in range(2):
                        full("d", nc.tensor.matmul(acc[half], cc("zero")[0:1, :], fours, start=False,
                                                   stop=True))
            if upon("hT3"):
                turn("xn3")
            if upon("in2"):
                pe.wait_ge(s["a_free"], FIRST_A["in2"])
                pe.wait_ge(s["d_free"], FIRST_D["in2"])
                for i in range(7):
                    w = chunk(pe, CNUM["in2"] + i)
                    for m in range(4):
                        product("d" if i == 1 else "a",
                                [(w[:, k, P * m:P * m + P], HT[:, k, :]) for k in range(KD)])
            if upon("ln"):
                pe.wait_ge(s["conv"], 4)
                product("d", [(cc("ones"), CV[:, m, :]) for m in range(4)])
                pe.wait_ge(s["convsq"], 4)
                product("d", [(cc("ones"), HN[:, m, 0:512]) for m in range(4)])
            if upon("pw"):
                pe.wait_ge(s["silu"], 4)
                w = chunk(pe, CNUM["pw"])
                for m in range(8):
                    product("d", [(w[:, k, P * m:P * m + P], CV[:, k, :]) for k in range(4)])
            if upon("yb"):
                w = chunk(pe, CNUM["pool"])
                pe.wait_ge(s["pooled"], 4)
                for m in range(8):
                    product("d", [(w[:, m // 2, P * (m % 2):P * (m % 2) + P], PO[:, m // 2, :])])
            if upon("wout"):
                pe.wait_ge(s["merged"], 8)
                for half in range(2):
                    w = chunk(pe, CNUM["wout"] + half)
                    for t in range(NT):
                        product("d", [(MG[:, k, P * t:P * t + P], w[:, k, :]) for k in range(KD)])
            if upon("hT4"):
                turn("xn4")
            if upon("up"):
                pe.wait_ge(s["a_free"], FIRST_A["up"])
                pe.wait_ge(s["d_free"], FIRST_D["up"])
                for i in range(11):
                    w = chunk(pe, CNUM["up"] + i)
                    for m in range(4):
                        product("a", [(w[:, k, P * m:P * m + P], HT[:, k, :]) for k in range(KD)])
            if upon("down"):
                banks = [[bank("a") for _ in range(NT)], [bank("d") for _ in range(NT)]]
                for i in range(6):
                    w = chunk(pe, CNUM["down"] + i)
                    nk = w.shape[1]
                    for kk in range(nk):
                        k = 4 * i + kk
                        pe.wait_ge(s["ff"], k + 1)
                        for half in range(2):
                            for t in range(NT):
                                ins = nc.tensor.matmul(banks[half][t], FT[:, k, P * t:P * t + P],
                                                       w[:, kk, 512 * half:512 * half + 512],
                                                       start=(k == 0), stop=(k == NF - 1))
                                if k == NF - 1:
                                    full("ad"[half], ins)
                    if i < 3:
                        pe.drain().then_inc(s_down, 1)
            if dbg is not None:
                tell(pe.drain(), "fin")

        @block.scalar
        def _(act):
            A = nc.scalar.activation

            def take():
                j = n["a_free"]
                act.wait_ge(s["a_full"], j + 1)
                return PA[:, j % 4, :]

            def link():
                act.wait_ge(s["act"], n["act"])

            def turned(dst, scale=None, bias=None):
                for k in range(0, KD, 2):
                    tell(A(dst[:, k, :], take(), ACT.Identity, scale=scale(k) if scale else 1.0,
                           bias=bias(k) if bias else 0.0), "a_free")

            def roots(*tiles):
                for v in tiles:
                    act.wait_ge(s["var"], n["rstd"] + 1)
                    tell(A(v, v, ACT.Sqrt), "rstd")

            def ffv(t):
                return ffst[:, 24 * t + 13:24 * t + 14]

            roots(st_a[:, 0:4])
            act.wait_ge(s["in_const"], 64)
            turned(HT, lambda k: vv("g_mix", k))
            if upon("pm"):
                for t in range(NT):
                    tell(nc.scalar.copy(PM[:, t, 0:512], take()), "a_free")
                act.wait_ge(s["sscan"], 1)
                tell(A(sinb[:, :], ang[:, :], ACT.Sin), "act")
                act.wait_ge(s["sscan"], 2)
                tell(A(cosb[:, :], kint[:, :], ACT.Sin), "act")
            if upon("cT"):
                roots(st_a[:, 8:16])
                for g in (0, 2, 4):
                    sc_ = vv("g_cq", g) if g < 3 else vv("g_ckv", g - 3)
                    tell(A(CT[:, g, :], take(), ACT.Copy, scale=sc_), "a_free")
            if upon("q"):
                for t in range(NT):
                    tell(nc.scalar.copy(QK[:, t, 0:4, :].rearrange("p g d -> p (g d)"), take()[:, 0:384]), "a_free")
            if upon("kv"):
                for t in range(NT):
                    tell(nc.scalar.copy(QK[:, t, H:2 * H, 0:DN], take().rearrange("p (h d) -> p h d", h=H)), "a_free")
            if upon("qkT"):
                roots(*[st_a[:, 16:32]] * NT)
                for g in range(0, 2 * H, 2):
                    tell(nc.scalar.copy(QKT[0:DQK, g, :], take()[0:DQK, :]), "a_free")
            if upon("att"):
                u = 0
                for t in range(NT):
                    for h in range(H):
                        b = take()
                        nk = P * (t + 1)
                        act.wait_ge(s["smax"], u + 1)
                        if u >= 2:
                            act.wait_ge(s["d_full"], FIRST_D["att"] + (1 if u == 2 else 2 * u - 4))
                        tell(A(PB[:, u % 2, 0:nk], b[:, 0:nk], ACT.Exp, bias=nmax[:, u:u + 1], scale=DQK ** -0.5,
                               accum_out=rsum[:, u:u + 1]), "probs")
                        act.wait_ge(s["probs"], u + 1)
                        tell(nc.scalar.copy(st_a[:, 63:64], rsum[:, u:u + 1]), "a_free")
                        u += 1
                roots(*[st_a[:, 16:24]] * NT)
            if upon("pr"):
                for m in range(14):
                    b = take()
                    if m == 0:
                        act.wait_ge(s["raw_used"], 1)
                    if m >= 4:
                        act.wait_ge(s["raw_used"], m - 2)
                    tell(nc.scalar.copy(RAW[:, m % 4, 1:513], b), "a_free")
            if upon("lora"):
                act.wait_ge(s["prt"], 14)
                tell(A(LT[0:64, 2, :], LT[0:64, 0, :], ACT.Tanh), "lora_in")
                tell(A(LT[:, 3, :], LT[:, 1, :], ACT.Sigmoid), "lora_in")
                for m in range(4):
                    tell(A(SG[:, m, :], take(), ACT.Sigmoid, bias=vv("w0", m)), "a_free")
                for m in range(4):
                    tell(A(AT[:, m, :], take(), ACT.Sigmoid, bias=vv("a0", m)), "a_free")
                for t in range(NT):
                    tell(nc.scalar.copy(GT[:, t, :], take()), "a_free")
            if upon("kn"):
                roots(*[E2[:, m, :] for m in range(4)])
            if upon("tok"):
                act.wait_ge(s["Lm"], 1)
                tell(A(fdec[:, :], fdec[:, :], ACT.Exp, scale=-KAPPA), "rexp")
                act.wait_ge(s["Lm"], 2)
                act.wait_ge(s["d_full"], FIRST_D["tok"])
                tell(A(E1[:, :, :], CS[:, :, :], ACT.Exp, scale=-KAPPA), "rexp")
                tell(A(E2[:, :, :], CS[:, :, :], ACT.Exp, scale=KAPPA), "rexp")
                act.wait_ge(s["Lm"], 3)
                act.wait_ge(s["d_full"], FIRST_D["tok"] + 4)
                tell(A(EQ[:, :, :], SG[:, :, :], ACT.Exp, scale=-KAPPA), "rexp")
                act.wait_ge(s["rexp"], n["rexp"])
                for t in range(NT):
                    tell(nc.scalar.copy(KTOK[:, t, :], take()), "a_free")
            for pr in range(4):
                if not upon(f"pair{pr}"):
                    break
                for hh in range(2):
                    tell(nc.scalar.copy(PAIR2[:, 2, hh, :], take()), "a_free")
                for lev in range(1, LEVELS):
                    for hh in range(2):
                        b = take()
                        if lev > 1:
                            base = FIRST_D[f"pair{pr}"] + 8 + 4 * (lev - 2)
                            act.wait_ge(s["d_full"], base + 2 * hh + 2)
                        tell(nc.scalar.copy(PAIR2[:, 3, hh, :], b), "a_free")
                dn = FIRST_D[f"pair{pr}"] + 30
                for c in range(NT):
                    b = take()
                    act.wait_ge(s["d_full"], dn + c)
                    tell(nc.scalar.copy(PAIR2[:, 3, 0, 0:P], b[:, 0:P]), "a_free")
                    tell(nc.scalar.copy(PAIR2[:, 3, 1, 0:P], take()[:, 0:P]), "a_free")
                    tell(nc.scalar.copy(HN[:, c, 512 + P * pr:512 + P * pr + P], take()[:, 0:P]), "a_free")
            if upon("yT"):
                roots(*[st_a[:, 16:24]] * NT)
                turned(HT)
            if upon("hT2"):
                roots(st_a[:, 0:4])
                turned(HT)
            if upon("pq"):
                for m in range(0, 16, 2):
                    tell(nc.scalar.copy(QPT[:, m, :], take()), "a_free")
            if upon("s"):
                for t in range(NT):
                    for g4 in range(4):
                        tell(nc.scalar.copy(SS[t][:, 512 * g4:512 * g4 + 512], take()), "a_free")
            if upon("ada"):
                tell(A(csil2, vv("c"), ACT.Silu), "act")
                link()
                act.wait_ge(s["a_full"], FIRST_A["ada"])
                for k in range(KD):
                    tell(A(SILU[:, k, :], cc("ones"), ACT.Copy, scale=csil2[:, k:k + 1]), "csil")
                for i in range(12):
                    b = take()
                    if i // 2 in (2, 5):
                        g = (0 if i < 6 else 1024) + 512 * (i % 2)
                        tell(nc.scalar.copy(RW[:, g:g + 512], b), "a_free")
                    else:
                        r = i if i < 4 else i - 2
                        tell(nc.scalar.copy(MODROW[0:1, 512 * r:512 * r + 512], b[0:1, :]), "a_free")
            if upon("acc"):
                def gate_exp(t):
                    act.wait_ge(s["topk"], t + 1)
                    tell(A(GATE[:, t % 2, :], GATE[:, t % 2, :], ACT.Exp), "geluv")

                gate_exp(0)
                for t in range(NT):
                    if t + 1 < NT:
                        gate_exp(t + 1)
                    with act.Fori(0, NSEL // RING) as it:
                        for g in range(RING // GRP):
                            act.wait_ge(s["dots"], it * RING + (NSEL * t + GRP * (g + 1)))
                            A(GEL[:, g, :], DOT[:, g, :], ACT.Gelu).then_inc(s["gelu"], 1)
            if upon("hT3"):
                roots(*[ffv(t) for t in range(NT)])
                turned(HT, lambda k: modc[:, 8 + k:9 + k], lambda k: modc[:, k:k + 1])
            if upon("in2"):
                for m in range(4):
                    tell(A(SGA[:, m, :], take(), ACT.Sigmoid), "a_free")
                for m in range(4):
                    tell(nc.scalar.copy(UP[:, m, 16:528], take()), "a_free")
                for m in range(8):
                    tell(A(GA[:, m, :], take(), ACT.Sigmoid), "a_free")
                for m in range(8):
                    tell(A(GB[:, m, :], take(), ACT.Sigmoid), "a_free")
            if upon("ln"):
                roots(HN[:, 0, 512:1024])
                for m in range(4):
                    act.wait_ge(s["silu_in"], m + 1)
                    tell(A(CV[:, m, :], CV[:, m, :], ACT.Silu, scale=vv("ln_a_g", m), bias=vv("ln_a_b", m)), "silu")
            if upon("hT4"):
                roots(*[ffv(t) for t in list(range(NT)) * 2])
                turned(HT, lambda k: modc[:, 24 + k:25 + k], lambda k: modc[:, 16 + k:17 + k])
            if upon("up"):
                for j in range(NF):
                    for i in range(2):
                        b = take()
                        q = 2 * (j % 2) + i
                        act.wait_ge(s["upraw_used"], max(1, 2 * (j - 2) + i + 2))
                        tell(nc.scalar.copy(UR[:, q, 2:514], b), "a_free")
                    if j >= 1:
                        act.wait_ge(s["gelu_in"], j)
                        tell(A(UC[:, 2 * ((j - 1) % 2) + 1, :], UC[:, 2 * ((j - 1) % 2) + 1, :],
                               ACT.Gelu_apprx_tanh), "ffgelu")
                act.wait_ge(s["gelu_in"], NF)
                tell(A(UC[:, 2 * ((NF - 1) % 2) + 1, :], UC[:, 2 * ((NF - 1) % 2) + 1, :],
                       ACT.Gelu_apprx_tanh), "ffgelu")
            if upon("down"):
                for t in range(NT):
                    tell(nc.scalar.copy(HN[:, t, 0:512], take()), "a_free")
                roots(*[ffv(t) for t in range(NT)])
            if dbg is not None:
                act.wait_ge(s["a_free"], n["a_free"])
                tell(act.drain(), "fin")

        @block.vector
        def _(dve):
            tt, ts, stt = nc.vector.tensor_tensor, nc.vector.tensor_scalar, nc.vector.scalar_tensor_tensor
            ttr = nc.vector.tensor_tensor_reduce

            def take():
                j = n["d_free"]
                dve.wait_ge(s["d_full"], j + 1)
                return PD[:, j % 4, :]

            def link(ins=None, name="dve"):
                if ins is not None:
                    tell(ins, name)
                dve.wait_ge(s[name], n[name])

            def rstd(dst, scale, eps):
                tell(ts(dst, dst, scale, eps, ALU.mult, ALU.add), "var")
                dve.wait_ge(s["rstd"], n["var"])
                link(nc.vector.reciprocal(dst, dst))

            def turned(dst, scale=None, bias=None):
                for k in range(1, KD, 2):
                    b = take()
                    if bias:
                        tell(ts(dst[:, k, :], b, scale(k), bias(k), ALU.mult, ALU.add), "d_free")
                    elif scale:
                        tell(ts(dst[:, k, :], b, scale(k), None, ALU.mult), "d_free")
                    else:
                        tell(nc.vector.tensor_copy(dst[:, k, :], b), "d_free")

            def rms_rows(ready, gain=None):
                for t in range(NT):
                    link(ttr(HN[:, t, :], X[:, t, :], X[:, t, :], 1.0, 0.0, ALU.mult, ALU.add, st_a[:, t:t + 1]))
                rstd(st_a[:, 0:NT], 1.0 / D, EPS)
                for t in range(NT):
                    if gain is None:
                        tell(ts(HN[:, t, :], X[:, t, :], st_a[:, t:t + 1], None, ALU.mult), ready)
                    else:
                        tell(stt(HN[:, t, :], X[:, t, :], st_a[:, t:t + 1], gain, ALU.mult, ALU.mult), ready)

            dve.wait_ge(s["in_x"], 64)
            rms_rows("xn")
            dve.wait_ge(s["in_const"], 64)
            if upon("pm"):
                TWO_PI = [6.28125, 0.0019350051879882812, 3.0199159819567e-07]
                MAGIC = 12582912.0
                link(nc.vector.tensor_copy(posf[:, :], posi[:, :]))
                a3 = ang.rearrange("p (t i) -> p t i", t=NT)
                k3 = kint.rearrange("p (t i) -> p t i", t=NT)
                link(tt(a3, posf.unsqueeze(2).broadcast_to([P, NT, HALF]),
                        cc("invfreq").unsqueeze(1).broadcast_to([P, NT, HALF]), ALU.mult))
                link(ts(kint[:, :], ang[:, :], 1.0 / (2 * np.pi), 0.25, ALU.mult, ALU.add))
                link(ts(kint[:, :], kint[:, :], MAGIC, -MAGIC, ALU.add, ALU.add))
                link(stt(cosb[:, :], kint[:, :], -TWO_PI[0], ang[:, :], ALU.mult, ALU.add))
                link(stt(cosb[:, :], kint[:, :], -TWO_PI[1], cosb[:, :], ALU.mult, ALU.add))
                link(stt(cosb[:, :], kint[:, :], -TWO_PI[2], cosb[:, :], ALU.mult, ALU.add))
                link(ts(cosb[:, :], cosb[:, :], np.pi / 2, 3.1415925, ALU.add, ALU.min))
                link(ts(cosb[:, :], cosb[:, :], -3.1415925, None, ALU.max))
                link(ts(sinb[:, :], ang[:, :], 1.0 / (2 * np.pi), None, ALU.mult))
                link(ts(sinb[:, :], sinb[:, :], MAGIC, -MAGIC, ALU.add, ALU.add))
                for c_ in TWO_PI:
                    link(stt(ang[:, :], sinb[:, :], -c_, ang[:, :], ALU.mult, ALU.add))
                link(ts(ang[:, :], ang[:, :], 3.1415925, -3.1415925, ALU.min, ALU.max), "sscan")
                link(nc.vector.tensor_copy(kint[:, :], cosb[:, :]), "sscan")
            turned(HT, lambda k: vv("g_mix", k))
            if upon("pm"):
                for t in range(NT):
                    tell(nc.vector.tensor_copy(PM[:, t, 512:672], take()[:, 0:160]), "d_free")
                dve.wait_ge(s["a_free"], FIRST_A["cT"])
                dve.wait_ge(s["d_free"], n["d_free"])
            TMP = HN[:, 0:2, :].rearrange("p a b -> p (a b)")
            if upon("cT"):
                dve.wait_ge(s["a_full"], FIRST_A["pm"])
                dve.wait_ge(s["d_full"], FIRST_D["pm"])
                st = st_a[:, 8:16]
                for t in range(NT):
                    link(ttr(TMP[:, 0:QR], PM[:, t, 0:QR], PM[:, t, 0:QR], 1.0 / QR, 0.0, ALU.mult, ALU.add,
                             st[:, 2 * t:2 * t + 1]))
                    link(ttr(TMP[:, QR:QR + KVR], PM[:, t, QR:QR + KVR], PM[:, t, QR:QR + KVR], 1.0 / KVR, 0.0,
                             ALU.mult, ALU.add, st[:, 2 * t + 1:2 * t + 2]))
                rstd(st, 1.0, EPS)
                for t in range(NT):
                    link(ts(PM[:, t, 0:QR], PM[:, t, 0:QR], st[:, 2 * t:2 * t + 1], None, ALU.mult))
                    tell(ts(PM[:, t, QR:QR + KVR], PM[:, t, QR:QR + KVR], st[:, 2 * t + 1:2 * t + 2], None,
                            ALU.mult), "cn")
                for t in range(NT):
                    link(nc.vector.tensor_copy(QK[:, t, H:2 * H, DN:DQK],
                                               PM[:, t, QR + KVR:MLA_COLS].unsqueeze(1).broadcast_to([P, H, DR])))
                for g in (1, 3):
                    sc_ = vv("g_cq", g) if g < 3 else vv("g_ckv", g - 3)
                    tell(ts(CT[:, g, :], take(), sc_, None, ALU.mult), "d_free")
            if upon("q"):
                for t in range(NT):
                    tell(nc.vector.tensor_copy(QK[:, t, 4:8, :].rearrange("p g d -> p (g d)"), take()[:, 0:384]),
                         "d_free")
            if upon("kv"):
                for t in range(NT):
                    tell(nc.vector.tensor_copy(VA[:, t, :], take()), "d_free")
                dve.wait_ge(s["d_free"], n["d_free"])
            if upon("qkT"):
                dve.wait_ge(s["a_free"], FIRST_A["qkT"])
                dve.wait_ge(s["act"], 2)
                tmp3 = TMP[:, 0:1536].rearrange("p (g d) -> p g d", g=2 * H)
                ro = [TMP[:, 256 * i:256 * i + 256].rearrange("p (g i) -> p g i", g=2 * H) for i in range(4)]
                for t in range(NT):
                    st = st_a[:, 16:32]
                    q3 = QK[:, t, :, :]
                    link(tt(tmp3, q3, q3, ALU.mult))
                    link(nc.vector.tensor_reduce(st, tmp3, AX, ALU.add))
                    rstd(st, 1.0 / DQK, EPS)
                    link(tt(q3, q3, st.unsqueeze(2).broadcast_to([P, 2 * H, DQK]), ALU.mult))
                    link(tt(q3[:, 0:H, :], q3[:, 0:H, :], r1("g_q").unsqueeze(1).broadcast_to([P, H, DQK]), ALU.mult))
                    link(tt(q3[:, H:2 * H, :], q3[:, H:2 * H, :], r1("g_k").unsqueeze(1).broadcast_to([P, H, DQK]),
                            ALU.mult))
                    co = cosb[:, HALF * t:HALF * t + HALF].unsqueeze(1).broadcast_to([P, 2 * H, HALF])
                    si = sinb[:, HALF * t:HALF * t + HALF].unsqueeze(1).broadcast_to([P, 2 * H, HALF])
                    t1, t2 = q3[:, :, DN:DN + HALF], q3[:, :, DN + HALF:DQK]
                    tell(tt(ro[0], t1, co, ALU.mult), "dve")
                    tell(tt(ro[1], t2, si, ALU.mult), "dve")
                    tell(tt(ro[2], t1, si, ALU.mult), "dve")
                    link(tt(ro[3], t2, co, ALU.mult))
                    tell(tt(t1, ro[0], ro[1], ALU.subtract), "dve")
                    link(tt(t2, ro[2], ro[3], ALU.add), "qk_normed")
                    link()
                for g in range(1, 2 * H, 2):
                    tell(nc.vector.tensor_copy(QKT[0:DQK, g, :], take()[0:DQK, :]), "d_free")
            if upon("att"):
                units = [(t, h) for t in range(NT) for h in range(H)]
                for u in range(len(units) + 2):
                    if u < len(units):
                        t, h = units[u]
                        nk = P * (t + 1)
                        dve.wait_ge(s["a_full"], FIRST_A["att"] + u + 1)
                        b = PA[:, (FIRST_A["att"] + u) % 4, 0:nk]
                        link(nc.vector.tensor_reduce(nmax[:, u:u + 1], b, AX, ALU.max))
                        tell(ts(nmax[:, u:u + 1], nmax[:, u:u + 1], -DQK ** -0.5, None, ALU.mult), "smax")
                    if 1 <= u <= len(units):
                        t, h = units[u - 1]
                        b = take()
                        if u >= 3:
                            dve.wait_ge(s["d_full"], FIRST_D["att"] + 2 * (u - 3) + 3)
                        tell(nc.vector.tensor_copy(PT[:, (u - 1) % 2, 0:P * (t + 1)], b[:, 0:P * (t + 1)]), "d_free")
                    if u >= 2:
                        t, h = units[u - 2]
                        b = take()
                        dve.wait_ge(s["a_free"], FIRST_A["att"] + u - 1)
                        link(nc.vector.reciprocal(st_a[:, 32:33], rsum[:, u - 2:u - 1]))
                        link(ts(HN[:, t, 64 * h:64 * h + 64], b[:, 0:64], st_a[:, 32:33], None, ALU.mult), "d_free")
                dve.wait_ge(s["d_free"], n["d_free"])
                tmp8 = TMP[:, 1536:2048].rearrange("p (h d) -> p h d", h=H)
                for t in range(NT):
                    o3 = HN[:, t, 0:512].rearrange("p (h d) -> p h d", h=H)
                    t3 = AR[:, 0:512].rearrange("p (h d) -> p h d", h=H)
                    st = st_a[:, 16:24]
                    link(tt(t3, o3, o3, ALU.mult))
                    link(nc.vector.tensor_reduce(st, t3, AX, ALU.add))
                    rstd(st, 1.0 / 64, EPS)
                    link(tt(o3, o3, st.unsqueeze(2).broadcast_to([P, H, 64]), ALU.mult))
                    link(tt(HN[:, t, 0:512], HN[:, t, 0:512], r1("g_attn"), ALU.mult), "o_normed")
            if upon("pr"):
                dve.wait_ge(s["dve"], n["dve"])
                tell(nc.vector.memset(RAW[:, :, 0:1], 0.0), "raw_used")
                for m in range(14):
                    dst = (RT, KT, VT, LT)[m // 4][:, m % 4, :]
                    dve.wait_ge(s["a_free"], FIRST_A["pr"] + m + 1)
                    raw = RAW[:, m % 4, :]
                    link(tt(dst, raw[:, 0:512], raw[:, 1:513], ALU.subtract))
                    link(stt(dst, dst, vv("mu", m), raw[:, 1:513], ALU.mult, ALU.add), "raw_used")
                    tell(dve.nop(), "prt")
            if upon("kn"):
                for m in range(4):
                    link(ts(KK[:, m, :], KT[:, m, :], vv("k_k", m), None, ALU.mult))
                    tell(tt(E1[:, m, :], KK[:, m, :], KK[:, m, :], ALU.mult), "kx_sq")
                for m in range(4):
                    b = take()
                    link(ts(E2[:, m, :], b, 1e-24, None, ALU.max), "d_free")
                    tell(dve.nop(), "var")
                for m in range(4):
                    dve.wait_ge(s["rstd"], n["var"] - 3 + m)
                    link(nc.vector.reciprocal(E2[:, m, :], E2[:, m, :]))
                    link(tt(KK[:, m, :], KK[:, m, :], E2[:, m, :], ALU.mult))
            if upon("bonus"):
                dve.wait_ge(s["a_free"], FIRST_A["lora"] + 8)
                omk = st_a[:, 40:44]
                link(ts(omk, vv("k_a"), -1.0, 1.0, ALU.mult, ALU.add))
                for m in range(4):
                    link(ts(E2[:, m, :], AT[:, m, :], vv("k_a", m), omk[:, m:m + 1], ALU.mult, ALU.add))
                    link(tt(KT[:, m, :], KT[:, m, :], E2[:, m, :], ALU.mult))
                    link(stt(E1[:, m, :], RT[:, m, :], vv("r_k", m), KT[:, m, :], ALU.mult, ALU.mult))
                tell(dve.nop(), "rkk")
                b = take()
                tell(nc.vector.tensor_copy(bon[:, :], b[:, 0:32]), "d_free")
            if upon("tok"):
                for m in range(4):
                    for c in range(NT):
                        sl = slice(P * c, P * c + P)
                        tell(nc.vector.tensor_tensor_scan(CS[:, m, sl], cc("ones"), SG[:, m, sl], 0.0,
                                                          ALU.mult, ALU.add), "dve")
                link()
                cs4 = CS.rearrange("p m (c n) -> p m c n", c=NT)
                f4 = fdec.rearrange("p (m c) -> p m c", m=4)
                mid, end = cs4[:, :, :, 63:64].squeeze(3), cs4[:, :, :, 127:128].squeeze(3)
                md = st_a[:, 44:60].rearrange("p (m c) -> p m c", m=4)
                link(nc.vector.tensor_copy(md, mid))
                link(tt(f4, end, md, ALU.subtract))
                link(tt(f4[:, :, 0:3], f4[:, :, 0:3], md[:, :, 1:4], ALU.add), "Lm")
                link()
                for m in range(4):
                    tell(tt(cs4[:, m, :, :], cs4[:, m, :, :], md[:, m, :].unsqueeze(2).broadcast_to([P, NT, P]),
                            ALU.subtract), "dve")
                link()
                tell(dve.nop(), "Lm")
                link(tt(SG[:, :, :], CS[:, :, :], SG[:, :, :], ALU.subtract), "Lm")
                for t in range(NT):
                    tell(nc.vector.tensor_copy(VTOK[:, t, :], take()), "d_free")
                dve.wait_ge(s["rexp"], 2)
                link(tt(RT[:, :, :], RT[:, :, :], E1[:, :, :], ALU.mult), "rhat")
                dve.wait_ge(s["rexp"], 3)
                link(tt(KT[:, :, :], KT[:, :, :], E2[:, :, :], ALU.mult), "rhat")
                link(stt(AT[:, :, :], AT[:, :, :], -1.0, KK[:, :, :], ALU.mult, ALU.mult))
                link(tt(AT[:, :, :], AT[:, :, :], E2[:, :, :], ALU.mult), "rhat")
                dve.wait_ge(s["rexp"], 4)
                link(tt(KK[:, :, :], KK[:, :, :], EQ[:, :, :], ALU.mult), "rhat")
                for t in range(NT):
                    tell(nc.vector.tensor_copy(BTOK[:, t, :], take()), "d_free")
            for pr in range(4):
                if not upon(f"pair{pr}"):
                    break
                if pr == 0:
                    dve.wait_ge(s["a_free"], FIRST_A["pair0"])
                    dve.wait_ge(s["d_free"], n["d_free"])
                    dve.wait_ge(s["rhat"], 4)
                else:
                    dve.wait_ge(s["d_full"], FIRST_D[f"pair{pr}"])
                    dve.wait_ge(s["a_free"], FIRST_A[f"pair{pr}"])
                tell(nc.vector.memset(tmid[:, P * pr:P * pr + P], 0.0), "tmid")

                def mask(m_):
                    return m_.unsqueeze(1).broadcast_to([P, NT, P])

                def v4(z):
                    return z.rearrange("p (c n) -> p c n", c=NT)
                for hh in range(2):
                    for dst, mk in ((PAIR2[:, 0, hh, :], "strict"), (PAIR1[:, 2, hh, :], "incl"),
                                    (PAIR1[:, 0, hh, :], "strict"), (PAIR1[:, 1, hh, :], "incl")):
                        b = take()
                        tell(tt(v4(dst), v4(b), mask(cc(mk)), ALU.mult), "d_free")
                dve.wait_ge(s["d_free"], n["d_free"])
                for hh in range(2):
                    xt = PAIR1[:, 3, hh, :]
                    link(tt(v4(xt), v4(PAIR2[:, 0, hh, :]), mask(LV[:, 0, :]), ALU.mult))
                    link(tt(v4(xt), v4(xt), mask(ident), ALU.add), "x1t")
                for hh in range(2):
                    tell(tt(v4(PAIR2[:, 1, hh, :]), v4(PAIR2[:, 0, hh, :]), mask(LV[:, 1, :]), ALU.mult), "ct")
                fa = FIRST_A[f"pair{pr}"]
                for lev in range(1, LEVELS):
                    for hh in range(2):
                        b = take()
                        if lev < LEVELS - 1:
                            dve.wait_ge(s["d_full"], n["d_free"] + 2)
                        tell(tt(PAIR1[:, 3, hh, :], PAIR1[:, 3, hh, :], b, ALU.add), "d_free")
                        if lev < LEVELS - 1:
                            b = take()
                            tell(tt(PAIR2[:, 2, hh, :], PAIR2[:, 2, hh, :], b, ALU.add), "d_free")
                            dve.wait_ge(s["a_full"], fa + 2 + 2 * (lev - 1) + hh + 1)
                            tell(tt(v4(PAIR2[:, 1, hh, :]), v4(PAIR2[:, 0, hh, :]), mask(LV[:, lev + 1, :]),
                                    ALU.mult), "ct")
                for c in range(NT):
                    b = take()
                    dve.wait_ge(s["a_full"], fa + 14 + 3 * c + 3)
                    fd_ = fdec[:, 4 * pr + c:4 * pr + c + 1]
                    tell(stt(tmid[:, P * pr:P * pr + P], b[:, 0:P], fd_, cc("heads"), ALU.mult, ALU.mult), "d_free")
            if upon("yT"):
                dve.wait_ge(s["a_free"], FIRST_A["yT"])
                dve.wait_ge(s["d_full"], FIRST_D["yT"])
                dve.wait_ge(s["d_free"], n["d_free"])
                g1_, g2_ = AR[:, 18432:18944], AR[:, 18944:19456]
                h3 = lambda z: z.rearrange("p (h d) -> p h d", h=H)
                for t in range(NT):
                    y = HN[:, t, 512:1024]
                    st = st_a[:, 16:24]
                    bc = lambda z: z.unsqueeze(2).broadcast_to([P, H, 64])
                    link(nc.vector.tensor_reduce(st, h3(y), AX, ALU.add))
                    link(ts(st, st, 1.0 / 64, None, ALU.mult))
                    link(tt(h3(y), h3(y), bc(st), ALU.subtract))
                    link(tt(g1_, y, y, ALU.mult))
                    link(nc.vector.tensor_reduce(st, h3(g1_), AX, ALU.add))
                    rstd(st, 1.0 / 64, LN_X_EPS)
                    link(tt(h3(y), h3(y), bc(st), ALU.mult))
                    link(tt(y, y, r1("ln_x_w"), ALU.mult))
                    link(tt(y, y, r1("ln_x_b"), ALU.add))
                    link(tt(h3(g2_), h3(VTOK[:, t, :]), bc(bon[:, 8 * t:8 * t + 8]), ALU.mult))
                    link(tt(y, y, g2_, ALU.add))
                    link(tt(y, y, GT[:, t, :], ALU.mult), "ycomb")
                turned(HT)
            if upon("wo"):
                for half in range(2):
                    for t in range(NT):
                        b = take()
                        xs = X[:, t, 512 * half:512 * half + 512]
                        link(tt(xs, xs, b, ALU.add), "d_free")
            if upon("hT2"):
                dve.wait_ge(s["in_gffn"], 16)
                rms_rows("xn2", GF)
                turned(HT)
            if upon("pq"):
                for m in range(1, 16, 2):
                    tell(nc.vector.tensor_copy(QPT[:, m, :], take()), "d_free")

            def top_sixteen(vals, idx, src, width, groups):
                for g in range(groups):
                    tell(nc.vector.max(vals[:, 16 * g:16 * g + 8], src[:, width * g:width * g + width]), "dve")
                link()
                for g in range(groups):
                    tell(nc.vector.max_index(idx[:, 16 * g:16 * g + 8], vals[:, 16 * g:16 * g + 8],
                                             src[:, width * g:width * g + width]), "dve")
                link()
                for g in range(groups):
                    sg_ = src[:, width * g:width * g + width]
                    tell(nc.vector.match_replace(sg_, vals[:, 16 * g:16 * g + 8], sg_, -3e38), "dve")
                link()
                for g in range(groups):
                    tell(nc.vector.max(vals[:, 16 * g + 8:16 * g + 16], src[:, width * g:width * g + width]), "dve")
                link()
                for g in range(groups):
                    tell(nc.vector.max_index(idx[:, 16 * g + 8:16 * g + 16], vals[:, 16 * g + 8:16 * g + 16],
                                             src[:, width * g:width * g + width]), "dve")
                link()

            def select(t):
                dve.wait_ge(s["a_free"], FIRST_A["s"] + 4 * t + 4)
                top_sixteen(s1v, i1u, SS[t], NK, 16)
                sv = s1v.rearrange("p (h q k) -> p h q k", h=H, q=2)
                c4 = CAND.rearrange("p (h a b) -> p h a b", h=H, a=TOPK)
                for h in range(H):
                    link(tt(c4[:, h, :, :], sv[:, h, 0, :].unsqueeze(2).broadcast_to([P, TOPK, TOPK]),
                            sv[:, h, 1, :].unsqueeze(1).broadcast_to([P, TOPK, TOPK]), ALU.add))
                top_sixteen(tpv, tpu, CAND, TOPK * TOPK, H)
                g3 = GATE[:, t % 2, :].rearrange("p (h k) -> p h k", h=H)
                p3 = tpv.rearrange("p (h k) -> p h k", h=H)
                if t >= 2:
                    dve.wait_ge(s["uv_used"], NSEL * (t - 1))
                link(tt(g3, p3, p3[:, :, 0:1].broadcast_to([P, H, TOPK]), ALU.subtract), "topk")
                f_i = s1v.rearrange("p (h q k) -> p h q k", h=H, q=2)
                link(nc.vector.tensor_copy(s1v[:, :], i1u[:, :]))
                pa_, pb_ = i1u[:, 0:128], i1u[:, 128:256]
                link(ts(pa_, tpu[:, :], 4, None, ALU.logical_shift_right))
                link(ts(pb_, tpu[:, :], 15, None, ALU.bitwise_and))
                fa_ = tpv
                acc_ = [SS[t][:, 0:NSEL], SS[t][:, NSEL:2 * NSEL]]
                for q, pp in ((0, pa_), (1, pb_)):
                    link(nc.vector.tensor_copy(fa_[:, :], pp))
                    eq = CAND.rearrange("p (k a) -> p k a", k=NSEL)
                    link(tt(eq, fa_.unsqueeze(2).broadcast_to([P, NSEL, TOPK]),
                            cc("iota").unsqueeze(1).broadcast_to([P, NSEL, TOPK]), ALU.is_equal))
                    for h in range(H):
                        e3 = c4[:, h, :, :]
                        link(tt(e3, e3, f_i[:, h, q, :].unsqueeze(1).broadcast_to([P, TOPK, TOPK]), ALU.mult))
                    link(nc.vector.tensor_reduce(acc_[q], eq, AX, ALU.add))
                link(stt(acc_[0], acc_[0], float(NK), acc_[1], ALU.mult, ALU.add))
                link(nc.vector.tensor_copy(IDX[:, t % 2, :], acc_[0]), "idx")

            def gates(t):
                dve.wait_ge(s["geluv"], t + 1)
                g3 = GATE[:, t % 2, :].rearrange("p (h k) -> p h k", h=H)
                link(nc.vector.tensor_reduce(gmx[:, 0:8], g3, AX, ALU.add))
                link(nc.vector.reciprocal(gmx[:, 8:16], gmx[:, 0:8]))
                link(tt(g3, g3, gmx[:, 8:16].unsqueeze(2).broadcast_to([P, H, TOPK]), ALU.mult))

            if upon("modc"):
                if upon("acc"):
                    select(0)
                b = take()
                link(tt(modc[:, :], b[:, 0:32], vv("b_mod"), ALU.add), "d_free")
                for o in (8, 24):
                    link(ts(modc[:, o:o + 8], modc[:, o:o + 8], 1.0, None, ALU.add))
                tell(dve.nop(), "peer_clear")
            if upon("acc"):
                for t in range(NT):
                    if t + 1 < NT:
                        select(t + 1)
                    gates(t)
                    with dve.Fori(0, NSEL // RING) as it:
                        for g in range(RING // GRP + 1):
                            if g < RING // GRP:
                                for j in range(GRP * g, GRP * g + GRP):
                                    dve.wait_ge(uv_full[j], it * 16 + 16 * (NSEL // RING * t + 1))
                                    ttr(UV[:, j, 0:D], UV[:, j, 0:D], HN[:, t, :], 1.0, 0.0, ALU.mult, ALU.add,
                                        DOT[:, g, j % GRP:j % GRP + 1]).then_inc(s["dots"], 1)
                            if g >= 1:
                                dve.wait_ge(s["gelu"], it * (RING // GRP) + (NSEL // GRP * t + g))
                                for j in range(GRP * (g - 1), GRP * g):
                                    sel_ = GATE[:, t % 2, bass.ds(it * RING + j, 1)]
                                    ts(DG[:, j, :], ident, GEL[:, g - 1, j % GRP:j % GRP + 1], sel_,
                                       ALU.mult, ALU.mult).then_inc(s["diag"], 1)
                    for half in range(2):
                        b = take()
                        xs = X[:, t, 512 * half:512 * half + 512]
                        link(tt(xs, xs, b, ALU.add), "d_free")

            def layer_rows(ready, t, src, dst, gain=None, shift=None):
                st = ffst[:, 24 * t:24 * t + 24]
                for i in range(2):
                    tell(nc.vector.bn_stats(st[:, 6 * i:6 * i + 6], src[:, 512 * i:512 * i + 512]), "dve")
                link()
                link(nc.vector.bn_aggr(st[:, 12:14], st[:, 0:12]))
                rstd(st[:, 13:14], 1.0, LN_EPS)
                if gain is None:
                    tell(ts(dst, src, st[:, 12:13], st[:, 13:14], ALU.subtract, ALU.mult), ready)
                else:
                    link(ts(dst, src, st[:, 12:13], st[:, 13:14], ALU.subtract, ALU.mult))
                    link(tt(dst, dst, gain, ALU.mult))
                    link(tt(dst, dst, shift, ALU.add), ready)

            if upon("hT3"):
                tell(dve.nop(), "row2free")
                for t in range(NT):
                    layer_rows("xn3", t, X[:, t, :], HN[:, t, :])
                turned(HT, lambda k: modc[:, 8 + k:9 + k], lambda k: modc[:, k:k + 1])
            if upon("in2"):
                tell(nc.vector.memset(YAP[:, :, 0:30], 0.0), "bufs")
                link(nc.vector.memset(UP[:, :, 0:16], 0.0), "bufs")
                dve.wait_ge(s["a_free"], FIRST_A["in2"] + 4)
                for m in range(4):
                    b = take()
                    link(tt(YAP[:, m, 30:542], b, SGA[:, m, :], ALU.mult), "d_free")
            if upon("ln"):
                for m in range(4):
                    w = vv("w_conv")[:, CONV_K * m:CONV_K * m + CONV_K]
                    link(ts(CV[:, m, :], YAP[:, m, 0:512], w[:, 0:1], vv("b_conv", m), ALU.mult, ALU.add))
                    for j in range(1, CONV_K):
                        link(stt(CV[:, m, :], YAP[:, m, j:j + 512], w[:, j:j + 1], CV[:, m, :], ALU.mult, ALU.add))
                    tell(dve.nop(), "conv")
                b = take()
                for m in range(4):
                    ins = stt(CV[:, m, :], b, -1.0 / RD, CV[:, m, :], ALU.mult, ALU.add)
                    if m < 3:
                        tell(ins, "dve")
                    else:
                        tell(ins, "d_free")
                dve.wait_ge(s["d_free"], n["d_free"])
                link()
                dve.wait_ge(s["a_full"], FIRST_A["in2"])
                for m in range(4):
                    tell(tt(HN[:, m, 0:512], CV[:, m, :], CV[:, m, :], ALU.mult), "convsq")
                b = take()
                link(ts(HN[:, 0, 512:1024], b, 1.0 / RD, LN_EPS, ALU.mult, ALU.add), "d_free")
                tell(dve.nop(), "var")
                dve.wait_ge(s["rstd"], n["var"])
                link(nc.vector.reciprocal(HN[:, 0, 512:1024], HN[:, 0, 512:1024]))
                for m in range(4):
                    tell(tt(CV[:, m, :], CV[:, m, :], HN[:, 0, 512:1024], ALU.mult), "silu_in")
            if upon("yb"):
                for m, w in enumerate(POOL):
                    if m == 0:
                        dve.wait_ge(s["a_free"], FIRST_A["in2"] + 8)
                    u = UP[:, m, :]
                    src = u
                    step = 1
                    bufs_ = [HN[:, 1, 0:528], HN[:, 2, 0:528]]
                    i = 0
                    while step < w:
                        dst = bufs_[i % 2]
                        if 2 * step == w:
                            link(tt(dst[:, 16:528], src[:, 16:528], src[:, 16 - step:528 - step], ALU.add))
                        else:
                            link(nc.vector.memset(dst[:, 0:16], 0.0))
                            link(tt(dst[:, 16:528], src[:, 16:528], src[:, 16 - step:528 - step], ALU.add))
                        src = dst
                        step *= 2
                        i += 1
                    cn_ = cc("cnt")[:, 16 * m:16 * m + 16]
                    link(tt(src[:, 16:32], src[:, 16:32], cn_, ALU.mult))
                    link(ts(src[:, 32:528], src[:, 32:528], 1.0 / w, None, ALU.mult))
                    link(tt(PO[:, m, :], src[:, 16:528], u[:, 16:528], ALU.subtract), "pooled")
            if upon("pw"):
                dve.wait_ge(s["a_free"], FIRST_A["in2"] + 24)
                for m in range(8):
                    b = take()
                    link(tt(MG[:, m, :], b, GA[:, m, :], ALU.mult), "d_free")
            if upon("yb"):
                dve.wait_ge(s["a_free"], FIRST_A["in2"] + 24)
                for m in range(8):
                    b = take()
                    q = HN[:, 3, 512 * (m % 2):512 * (m % 2) + 512]
                    link(stt(q, b, vv("pool_scale", m), GB[:, m, :], ALU.mult, ALU.mult), "d_free")
                    link(tt(MG[:, m, :], MG[:, m, :], q, ALU.add), "merged")
            if upon("wout"):
                dve.wait_ge(s["in_row2"], 16)

                def r2(name):
                    return R2[:, ROW2[name][0]:ROW2[name][1]]
                link(tt(RW[:, 0:2048], RW[:, 0:2048], R2[:, 0:2048], ALU.add))
                for half in range(2):
                    sl = slice(512 * half, 512 * half + 512)
                    for t in range(NT):
                        b = take()
                        q = HN[:, t, sl]
                        link(tt(q, b, RW[:, sl], ALU.mult), "d_free")
                        link(stt(X[:, t, sl], X[:, t, sl], ALPHA, q, ALU.mult, ALU.add))
                for t in range(NT):
                    layer_rows("lnx", t, X[:, t, :], X[:, t, :], r2("ln1_g"), r2("ln1_b"))
            if upon("hT4"):
                for t in range(NT):
                    layer_rows("xn4", t, X[:, t, :], HN[:, t, :])
                turned(HT, lambda k: modc[:, 24 + k:25 + k], lambda k: modc[:, 16 + k:17 + k])
            if upon("up"):
                link(nc.vector.memset(UR[:, :, 0:2], 0.0), "upraw_used")

                def gated(j):
                    dve.wait_ge(s["ffgelu"], j + 1)
                    v_ = UC[:, 2 * (j % 2), :]
                    link(tt(FT[:, j, :], v_, UC[:, 2 * (j % 2) + 1, :], ALU.mult), "ff")
                for j in range(NF):
                    for i in range(2):
                        f = j + NF * i
                        q = 2 * (j % 2) + i
                        w = vv("w_ff")[:, 3 * f:3 * f + 3]
                        dve.wait_ge(s["a_free"], FIRST_A["up"] + 2 * j + i + 1)
                        u, o = UR[:, q, :], UC[:, q, :]
                        link(ts(o, u[:, 0:512], w[:, 0:1], vv("b_ff", f), ALU.mult, ALU.add))
                        link(stt(o, u[:, 1:513], w[:, 1:2], o, ALU.mult, ALU.add))
                        link(stt(o, u[:, 2:514], w[:, 2:3], o, ALU.mult, ALU.add), "upraw_used")
                        if i == 1:
                            tell(dve.nop(), "gelu_in")
                    if j >= 1:
                        gated(j - 1)
                gated(NF - 1)
            if upon("down"):
                for t in range(NT):
                    b = take()
                    link(tt(HN[:, t, 512:1024], b, RW[:, 1536:2048], ALU.mult), "d_free")
                dve.wait_ge(s["a_free"], FIRST_A["end"])
                for t in range(NT):
                    link(tt(HN[:, t, 0:512], HN[:, t, 0:512], RW[:, 1024:1536], ALU.mult))
                    link(stt(X[:, t, :], X[:, t, :], ALPHA, HN[:, t, :], ALU.mult, ALU.add))
                    layer_rows("fin", t, X[:, t, :], X[:, t, :], r2("ln2_g"), r2("ln2_b"))
            if dbg is not None:
                tell(dve.drain(), "fin")

        @block.gpsimd
        def _(pool):
            if upon("acc"):
                pool.wait_ge(s["a_full"], FIRST_A["ada"])
                pool.wait_ge(s["peer_clear"], 1)

                for t in range(NT):
                    pool.wait_ge(s["idx"], t + 1)
                    for i in range(NSEL):
                        turn = NSEL * t + i
                        if turn >= RING:
                            pool.wait_ge(s["uv_used"], turn - RING + 1)
                        nc.gpsimd.indirect_dma_start(
                            UV[:, turn % RING, :], None, uv,
                            bass.IndirectOffsetOnAxis(ap=IDX[:, t % 2, i:i + 1], axis=0),
                        ).then_inc(uv_full[turn % RING], 16)


def kernel(**inputs):
    import numpy as _np
    import concourse.bacc as _bacc
    from concourse import mybir as _mybir
    from concourse.bass_utils import run_bass_kernel_spmd as _run

    def f(name):
        return _np.asarray(inputs[name])

    def cols(v):
        return _np.ascontiguousarray(_np.asarray(v).reshape(-1, P).T)

    def rows(*vs):
        return _np.ascontiguousarray(_np.broadcast_to(_np.concatenate([_np.asarray(v).reshape(-1) for v in vs])[None], (P, sum(_np.asarray(v).size for v in vs))))

    b_ada = f("b_ada_2")[0].reshape(6, D)
    w_conv = f("w_dw_a_2")[0].reshape(CONV_K, 4, P).transpose(2, 1, 0).reshape(P, 4 * CONV_K)
    w_ff = f("w_dw_f_2")[0].reshape(3, 44, P).transpose(2, 1, 0).reshape(P, 44 * 3)
    vec = _np.concatenate([
        cols(f("g_mix")[0]), cols(f("rwkv_mu")[0]), cols(f("g_cq")[0]), cols(f("g_ckv")[0]), cols(f("w0")[0]),
        cols(f("a0")[0]), cols(f("k_k")[0]), cols(f("k_a")[0]), cols(f("r_k")[0]), cols(f("c_2")[0]),
        cols(b_ada[0]), cols(b_ada[1]), cols(b_ada[3]), cols(b_ada[4]), w_conv, cols(f("b_dw_a_2")[0]),
        cols(f("ln_a_g_2")[0]), cols(f("ln_a_b_2")[0]), cols(f("pool_scale_2")[0]), w_ff,
        cols(f("b_dw_f_2")[0])], 1)
    lora = _np.concatenate([_np.concatenate([f("w2")[0], f("a2")[0]], 0), f("g2")[0]], 1)
    keys = f("sub_keys")[0].transpose(3, 0, 1, 2).reshape(P, 16 * NK)
    uv = _np.concatenate([f("expert_u")[0], f("expert_v")[0]], 1)
    w_up = f("w_up_2")[0].reshape(D, 2, NF, P).transpose(0, 2, 1, 3).reshape(D, 2 * D_FF)
    arrays = {
        "x": f("x")[0], "pos": _np.ascontiguousarray(f("positions")[0].reshape(NT, P).T), "cst": constants(),
        "vec": vec, "row1": rows(f("g_qnorm"), f("g_knorm"), f("g_attn_out"), f("ln_x_w"), f("ln_x_b")),
        "gffn": rows(f("g_ffn")),
        "row2": rows(b_ada[2], b_ada[5], f("ln1_g_2"), f("ln1_b_2"), f("ln2_g_2"), f("ln2_b_2")),
        "w_in": f("w_in")[0], "w_uq": f("w_uq")[0], "w_uk": f("w_uk")[0], "w_uv": f("w_uv")[0], "lora": lora,
        "w_o": f("w_o")[0], "w_pq": f("w_pq")[0], "keys": keys, "uv": uv, "w_ada": f("w_ada_2")[0],
        "w_in2": f("w_in_2")[0], "w_pw": f("w_pw_a_2")[0], "w_pool": f("w_pool_2")[0], "w_out": f("w_out_2")[0],
        "w_up": w_up, "w_down": f("w_down_2")[0],
    }
    nc = _bacc.Bacc("TRN2", target_bir_lowering=False, num_devices=1)
    arrays = {f"in_{k}": _np.ascontiguousarray(v) for k, v in arrays.items()}
    args = [nc.dram_tensor(k, v.shape, _mybir.dt.from_np(v.dtype), kind="ExternalInput").ap()
            for k, v in arrays.items()]
    out = nc.dram_tensor("out_0", (S, D), F32, kind="ExternalOutput").ap()
    build(nc, *args, out)
    r = _run(nc, [arrays], core_ids=[0])
    return r.results[0]["out_0"].reshape(1, S, D)
```

```python
from contextlib import ExitStack

import numpy as np

import concourse.bass as bass
from concourse import mybir

ALU = mybir.AluOpType
ACT = mybir.ActivationFunctionType
F32 = mybir.dt.float32
I32 = mybir.dt.int32
U32 = mybir.dt.uint32
AX = mybir.AxisListType.X

P = 128
S = 512
NT = S // P
D = 1024
KD = D // P
EPS = 1e-6
LN_EPS = 1e-5

H = 8
DQK = 96
DN = 64
DR = 32
HALF = DR // 2
QR = 384
KVR = 256
MLA_COLS = QR + KVR + DR
RD = 512
RM = RD // P
LN_X_EPS = 64e-5
KAPPA = float(np.exp(-0.5))
LEVELS = 7
NK = 128
TOPK = 16
NSEL = H * TOPK
RING = 8
GRP = 2
CONV_K = 31
POOL = (2, 4, 8, 16)
D_FF = 2816
NF = D_FF // P
ALPHA = 2.0 ** 0.25

CH = 4096
NWR = 3

JOBS = [
    ("hT", 4, 4), ("pm", 4, 4), ("cT", 3, 2), ("q", 4, 4), ("kv", 4, 4), ("qkT", 8, 8),
    ("att", 32, 64), ("pr", 14, 0), ("lora", 12, 0), ("kn", 0, 4), ("bonus", 0, 1),
    ("tok", 4, 8),
    ("inv0", 28, 48), ("inv1", 28, 48), ("chain", 12, 28),
    ("yT", 4, 4), ("wo", 0, 8), ("hT2", 4, 4), ("pq", 8, 8), ("s", 16, 0), ("ada", 12, 0),
    ("modc", 0, 1), ("acc", 0, 8), ("hT3", 4, 4), ("in2", 24, 4), ("ln", 0, 2), ("pw", 0, 8),
    ("yb", 0, 8), ("wout", 0, 8), ("hT4", 4, 4), ("up", 44, 0), ("down", 4, 4), ("end", 0, 0),
]
FIRST_A, FIRST_D = {}, {}
_a = _d = 0
for _name, _na, _nd in JOBS:
    FIRST_A[_name], FIRST_D[_name] = _a, _d
    _a, _d = _a + _na, _d + _nd


def _cols(items):
    at, n = {}, 0
    for name, w in items:
        at[name] = (n, n + w)
        n += w
    return at, n


CONST, NCONST = _cols([("ident", P), ("ones", P), ("zero", P), ("lowrow", P), ("negrow", P),
                       ("level", LEVELS * P), ("strict", P), ("incl", P), ("heads", P), ("head2", 2),
                       ("invfreq", HALF), ("iota", TOPK), ("cnt", 4 * 16), ("mhalf", 1)])
VECS = [("g_mix", 8), ("mu", 14), ("g_cq", 3), ("g_ckv", 2), ("w0", 4), ("a0", 4), ("k_k", 4), ("k_a", 4),
        ("r_k", 4), ("c", 8), ("b_mod", 32), ("w_conv", 4 * CONV_K), ("b_conv", 4), ("ln_a_g", 4),
        ("ln_a_b", 4), ("pool_scale", 8), ("w_ff", 44 * 3), ("b_ff", 44)]
VEC, NVEC = _cols(VECS)
ROW1, NROW1 = _cols([("g_q", DQK), ("g_k", DQK), ("g_attn", RD), ("ln_x_w", RD), ("ln_x_b", RD)])
ROW2, NROW2 = _cols([("b_g1", D), ("b_g2", D), ("ln1_g", D), ("ln1_b", D), ("ln2_g", D), ("ln2_b", D)])


def constants():
    c = np.zeros((P, NCONST), np.float32)

    def put(name, v):
        a, b = CONST[name]
        c[:, a:b] = v

    i, j = np.arange(P)[:, None], np.arange(P)[None, :]
    put("ident", i == j)
    put("ones", 1.0)
    lev = [((j & (1 << l)) > 0) & ((i & (1 << l)) == 0) & ((i >> (l + 1)) == (j >> (l + 1)))
           for l in range(LEVELS)]
    put("level", np.concatenate(lev, 1))
    put("strict", i < j)
    put("incl", i <= j)
    put("heads", (i // 64) == (j // 64))
    put("head2", (i // 64) == np.arange(2)[None, :])
    put("lowrow", (j < 64) & (i == 0))
    put("negrow", np.where((j >= 64) & (i == 0), np.float32(-1e30), np.float32(0)))
    put("invfreq", (np.float32(10000.0) ** (-np.arange(HALF, dtype=np.float32) / np.float32(HALF)))[None, :])
    put("iota", np.arange(TOPK)[None, :])
    put("mhalf", -0.5)
    cnt = [1.0 / np.minimum(np.arange(16) + 1, w) for w in POOL]
    put("cnt", np.concatenate(cnt)[None, :])
    return c


def build(nc, x, pos, cst, vec, row1, gffn, row2, w_in, w_uq, w_uk, w_uv, lora, w_o, w_pq, keys, uv,
          w_ada, w_in2, w_pw, w_pool, w_out, w_up, w_down, out, dbg=None, upto="end", dumps=()):
    with ExitStack() as ctx:
        def sb(name, shape, dt=F32):
            return ctx.enter_context(nc.sbuf_tensor(name, shape, dt))

        X = sb("X", [P, NT, D])
        HN = sb("HN", [P, NT, D])
        HT = sb("HT", [P, KD, S])
        WR = sb("WR", [P, NWR, CH])
        AR = sb("AR", [P, 22784])
        C = sb("C", [P, NCONST])
        V = sb("V", [P, NVEC])
        RW = sb("RW", [P, 2048])
        SC = sb("SC", [P, 1240])
        PA = ctx.enter_context(nc.psum_tensor("PA", [P, 4, 512], F32))
        PD = ctx.enter_context(nc.psum_tensor("PD", [P, 4, 512], F32))

        def cc(name):
            return C[:, CONST[name][0]:CONST[name][1]]

        def vv(name, m=None):
            a, b = VEC[name]
            return V[:, a:b] if m is None else V[:, a + m:a + m + 1]

        def r1(name):
            return RW[:, ROW1[name][0]:ROW1[name][1]]

        def ar(a, n, *dims):
            v = AR[:, a:a + n]
            if len(dims) == 1:
                return v.rearrange("p (a b) -> p a b", a=dims[0])
            if len(dims) == 2:
                return v.rearrange("p (a b c) -> p a b c", a=dims[0], b=dims[1])
            return v

        ident = cc("ident")
        LV = cc("level").rearrange("p (l n) -> p l n", l=LEVELS)

        names = ["a_full", "a_free", "d_full", "d_free", "dve", "act", "pool",
                 "in_x", "in_const", "in_gffn", "in_row2", "out_done",
                 "xn", "xn2", "xn3", "xn4",
                 "cn", "qk_normed", "kr", "smax", "probs", "o_normed", "raw_used", "lora_in", "prt",
                 "kx_sq", "rkk", "rexp", "rexp_used", "rhat", "vcopy",
                 "mt", "ct", "x1t", "tmid", "ycomb",
                 "topk", "idx", "dots", "geluv", "diag", "uv_used", "accs", "csil",
                 "bufs", "sg", "conv", "convsq", "rstd_a", "silu_in", "silu", "pooled", "merged",
                 "lnx", "upraw_used", "gelu_in", "gelu", "ff", "ffadd", "fin", "row2free",
                 "peer_clear", "sscan", "Lm", "ffgelu", "var", "rstd"]
        s = {}
        for nm in names:
            s[nm] = ctx.enter_context(nc.semaphore(nm))
        w_sem = [ctx.enter_context(nc.semaphore(f"w_slot{i}")) for i in range(NWR)]
        uv_full = [ctx.enter_context(nc.semaphore(f"uv_full{i}")) for i in range(RING)]
        n = {nm: 0 for nm in names}

        def tell(ins, name):
            n[name] += 1
            ins.then_inc(s[name], 1)

        ORDER = [j[0] for j in JOBS]

        def upon(phase):
            return ORDER.index(phase) <= ORDER.index(upto)

        QK = ar(0, 6144).rearrange("p (t g d) -> p t g d", t=NT, g=2 * H)
        QKT = ar(6144, 8192, 2 * H)
        VA = ar(14336, 2048, NT)
        CT = ar(16384, 2560, 5)
        PM = ar(18944, 2688, NT)
        PB = ar(18944, 1024, 2)
        PT = ar(19968, 1024, 2)
        RT, KT, VT, LT = (ar(2048 * i, 2048, 4) for i in range(4))
        SG, CS, AT, KK, GT, E1, E2 = (ar(2048 * i, 2048, 4) for i in range(4, 11))
        RAW = ar(18432, 4 * 513, 4)
        VTOK = HT[:, 0:4, :]
        KTOK, BTOK = SG, CS
        MT, CTL, XI, ZI = VT, LT, E1, E2

        def XT(h):
            return HT[:, 4 + h, :] if h < 4 else WR[:, 0, 512 * (h - 4):512 * (h - 4) + 512]

        MATS = [ar(4096, 3072).rearrange("p (m h n) -> p m h n", m=3, h=H),
                ar(18432, 3072).rearrange("p (m h n) -> p m h n", m=3, h=H)]
        FS = [ar(4096 + 3072, 1024, 2), ar(18432 + 3072, 1024, 2)]
        UV = AR[:, 0:RING * 2048].rearrange("p (r n) -> p r n", r=RING)
        QPT = ar(0, 8192, 16)
        SS = [HT[:, 0:4, :].rearrange("p a b -> p (a b)"), HT[:, 4:8, :].rearrange("p a b -> p (a b)"),
              ar(16384, 2048), ar(18432, 2048)]
        CAND = ar(20480, 2048)
        GF = ar(20480, 1024)
        SGA = ar(0, 2048, 4)
        PO = ar(0, 2048, 4)
        YAP = ar(2048, 4 * 542, 4)
        UP = ar(4216, 4 * 528, 4)
        CV = ar(6328, 2048, 4)
        GA = ar(8376, 4096, 8)
        GB = ar(12472, 4096, 8)
        R2 = ar(16600, NROW2)
        MG = HT
        EQ = VT
        SILU = ar(8192, 1024, 8)
        MODROW = ar(9216, 4096)
        FT = ar(0, NF * S, NF)
        UR = ar(11264, 4 * 514, 4)
        UC = ar(13320, 4 * 512, 4)

        sc_at = [0]

        def small(w, dt=F32):
            a = sc_at[0]
            sc_at[0] += w
            assert sc_at[0] <= 1240, sc_at[0]
            v = SC[:, a:a + w]
            return v if dt is F32 else v.bitcast(dt)

        st_a = small(64)
        rsum = small(32)
        nmax = small(32)
        cosb = small(64)
        sinb = small(64)
        bon = small(32)
        fdec = small(16)
        modc = small(32)
        root = small(32)
        t_end = sc_at[0]
        posf = small(4)
        posi = small(4, I32)
        ang = small(64)
        kint = small(64)
        tmid = small(512)
        csil = small(8)
        sc_at[0] = t_end
        s1v = small(256)
        i1u = small(256, U32)
        tpv = small(128)
        tpu = small(128, U32)
        gmx = small(24)
        scr_free = sc_at[0]
        lvl = C[:, CONST["level"][0]:CONST["level"][0] + 1280]
        DG = lvl[:, 0:1024].rearrange("p (r n) -> p r n", r=RING)
        GATE = lvl[:, 1024:1280].rearrange("p (r n) -> p r n", r=2)
        IDX = C[:, CONST["lowrow"][0]:CONST["negrow"][1]].rearrange("p (r n) -> p r n", r=2).bitcast(U32)
        DOT = small(8).rearrange("p (r n) -> p r n", r=4)
        GEL = small(8).rearrange("p (r n) -> p r n", r=4)
        csil2 = small(8)
        ffst = lvl[:, 0:96]

        chunks = []

        def col_chunk(w, c0, w_cols, chan, job, k=KD):
            chunks.append((k * w_cols, w[:, c0:c0 + w_cols].rearrange("(k p) n -> p k n", p=P), k, chan, job))

        col_chunk(w_in, 0, 512, "a", FIRST_A["pm"] + 3)
        col_chunk(w_in, 512, 160, "d", FIRST_D["pm"] + 3)
        col_chunk(w_uq, 0, 768, "d", FIRST_D["q"] + 3, 3)
        chunks.append((1024, w_uk.rearrange("(k p) n -> p k n", p=P), 2, "d", FIRST_D["kv"] + 3))
        chunks.append((1024, w_uv.rearrange("(k p) n -> p k n", p=P), 2, "d", FIRST_D["kv"] + 3))
        for i, w in enumerate((512, 512, 512, 256)):
            col_chunk(w_in, MLA_COLS + 512 * i, w, "a", FIRST_A["pr"] + min(4 * i + 3, 13))
        chunks.append((1024, lora, 1, "a", FIRST_A["chain"] + 11))
        for i in range(2):
            col_chunk(w_o, 512 * i, 512, "d", FIRST_D["wo"] + 4 * i + 3)
        for i in range(4):
            col_chunk(w_pq, 512 * i, 512, "d", FIRST_D["pq"] + 2 * i + 1)
        chunks.append((2048, keys, 1, "a", FIRST_A["s"] + 15))
        for i in range(12):
            col_chunk(w_ada, 512 * i, 512, "a", FIRST_A["ada"] + i)
        in2_order = [1, 0, 2, 3, 4, 5, 6]
        in2_last = [("a", 3), ("d", 3), ("a", 7), ("a", 11), ("a", 15), ("a", 19), ("a", 23)]
        for i, (ch, j) in zip(in2_order, in2_last):
            col_chunk(w_in2, 512 * i, 512, ch, (FIRST_A if ch == "a" else FIRST_D)["in2"] + j)
        chunks.append((4096, w_pw.rearrange("(k p) n -> p k n", p=P), 4, "d", FIRST_D["pw"] + 7))
        chunks.append((1024, w_pool.rearrange("g p n -> p g n"), 4, "d", FIRST_D["yb"] + 7))
        for i in range(2):
            col_chunk(w_out, 512 * i, 512, "d", FIRST_D["wout"] + 4 * i + 3)
        for i in range(11):
            col_chunk(w_up, 512 * i, 512, "a", FIRST_A["up"] + 4 * i + 3)
        for i in range(6):
            k = min(4, NF - 4 * i)
            chunks.append((k * D, w_down[512 * i:512 * i + k * P, :].rearrange("(k p) n -> p k n", p=P), k, "down", i))
        s_down = ctx.enter_context(nc.semaphore("down_chunk"))
        CNUM = {}
        at = 0
        for nm, cnt in (("pm", 2), ("uq", 1), ("uk", 1), ("uv", 1), ("pr", 4), ("lora", 1), ("wo", 2), ("pq", 4),
                        ("keys", 1), ("ada", 12), ("in2", 7), ("pw", 1), ("pool", 1), ("wout", 2), ("up", 11),
                        ("down", 6)):
            CNUM[nm] = at
            at += cnt
        assert at == len(chunks)
        last_chunk = {"hT": 2, "pm": 2, "cT": 2, "q": 3, "kv": 5, "qkT": 5, "att": 5, "pr": 9}

        def chunk(pe, number, k=None):
            cols, _, kk, _, _ = chunks[number]
            pe.wait_ge(w_sem[number % NWR], 16 * (number // NWR + 1))
            return WR[:, number % NWR, 0:cols].rearrange("p (k n) -> p k n", k=k or kk)

        block = ctx.enter_context(nc.Block())

        @block.sync
        def _(sp):
            for t in range(NT):
                sp.dma_start(X[:, t, :], x[P * t:P * t + P, :]).then_inc(s["in_x"], 16)
            sp.dma_start(C[:, :], cst).then_inc(s["in_const"], 16)
            sp.dma_start(V[:, :], vec).then_inc(s["in_const"], 16)
            sp.dma_start(RW[:, 0:NROW1], row1).then_inc(s["in_const"], 16)
            sp.dma_start(posi[:, :], pos).then_inc(s["in_const"], 16)

            def load(i):
                cols, src, k, _, _ = chunks[i]
                if i >= NWR:
                    _, _, _, chan, job = chunks[i - NWR]
                    if chan == "down":
                        sp.wait_ge(s_down, job + 1)
                    else:
                        sp.wait_ge(s[chan + "_full"], job + 1)
                dst = WR[:, i % NWR, 0:cols]
                if len(src.shape) == 3:
                    dst = dst.rearrange("p (k n) -> p k n", k=k)
                sp.dma_start(dst, src).then_inc(w_sem[i % NWR], 16)

            stop = last_chunk.get(upto, len(chunks))
            if upto.startswith("inv") or upto == "chain" or upto in ("lora", "kn", "bonus", "tok"):
                stop = 10
            if upto in ("yT", "wo"):
                stop = 12
            if upto in ("hT2", "pq", "s"):
                stop = 17
            if upto in ("ada", "modc", "acc"):
                stop = 29
            if upto in ("hT3", "in2", "ln"):
                stop = 36
            for i in range(stop):
                load(i)
                if i == CNUM["pq"]:
                    sp.wait_ge(s["d_free"], FIRST_D["wo"])
                    sp.dma_start(GF, gffn).then_inc(s["in_gffn"], 16)
                if i == CNUM["wout"]:
                    sp.wait_ge(s["row2free"], 1)
                    sp.dma_start(R2, row2).then_inc(s["in_row2"], 16)
            if dbg is None:
                for t in range(NT):
                    sp.wait_ge(s["fin"], t + 1)
                    sp.dma_start(out[P * t:P * t + P, :], X[:, t, :]).then_inc(s["out_done"], 16)
                sp.wait_ge(s["out_done"], 16 * NT)
            else:
                sp.wait_ge(s["fin"], 3)
                n_out = 0
                flat = {"X": X, "HN": HN, "HT": HT}
                for nm, a_, b_ in dumps:
                    z = flat[nm][:, :, :].rearrange("p a b -> p (a b)") if nm in flat else {"AR": AR, "SC": SC, "C": C, "RW": RW}[nm]
                    sp.dma_start(dbg[:, n_out:n_out + b_ - a_], z[:, a_:b_]).then_inc(s["out_done"], 16)
                    n_out += b_ - a_
                sp.wait_ge(s["out_done"], 16 * len(dumps))

        @block.tensor
        def _(pe):
            cnt = {"a": 0, "d": 0}

            def bank(chan):
                j = cnt[chan]
                cnt[chan] += 1
                if j >= 4:
                    pe.wait_ge(s[chan + "_free"], j - 3)
                return (PA if chan == "a" else PD)[:, j % 4, :]

            def full(chan, ins):
                ins.then_inc(s[chan + "_full"], 1)

            def transposes(chan, srcs, rows=P, cols=P):
                b = bank(chan)
                for i, src in enumerate(srcs):
                    ins = nc.tensor.transpose(b[0:cols, rows * i:rows * i + rows], src, ident[0:rows, 0:rows])
                full(chan, ins)

            def product(chan, pairs, w=512, rows=P):
                b = bank(chan)[0:rows, 0:w]
                for i, (lhsT, rhs) in enumerate(pairs):
                    ins = nc.tensor.matmul(b, lhsT, rhs, start=(i == 0), stop=(i == len(pairs) - 1))
                full(chan, ins)

            def turn(ready, count=1):
                for k in range(KD):
                    if k == 0:
                        pe.wait_ge(s[ready], NT * count)
                    transposes("ad"[k % 2], [HN[:, t, P * k:P * k + P] for t in range(NT)])

            pe.wait_ge(s["in_const"], 64)
            turn("xn")

            pe.wait_ge(s["a_free"], FIRST_A["pm"])
            pe.wait_ge(s["d_free"], FIRST_D["pm"])
            if upon("pm"):
                w0_, w1_ = chunk(pe, 0), chunk(pe, 1)
                for t in range(NT):
                    product("a", [(HT[:, k, P * t:P * t + P], w0_[:, k, :]) for k in range(KD)])
                for t in range(NT):
                    product("d", [(HT[:, k, P * t:P * t + P], w1_[:, k, :]) for k in range(KD)], 160)
            if upon("cT"):
                pe.wait_ge(s["cn"], NT)
                for g in range(5):
                    transposes("ad"[g % 2], [PM[:, t, P * g:P * g + P] for t in range(NT)])
                pe.wait_ge(s["a_free"], FIRST_A["q"])
                pe.wait_ge(s["d_free"], FIRST_D["q"])
            if upon("q"):
                uq = chunk(pe, CNUM["uq"])
                for t in range(NT):
                    for half in range(2):
                        product("ad"[half], [(CT[:, k, P * t:P * t + P], uq[:, k, 384 * half:384 * half + 384])
                                             for k in range(3)], 384)
            if upon("kv"):
                uk, uvw = chunk(pe, CNUM["uk"]), chunk(pe, CNUM["uv"])
                for t in range(NT):
                    product("a", [(CT[:, 3 + k, P * t:P * t + P], uk[:, k, :]) for k in range(2)])
                    product("d", [(CT[:, 3 + k, P * t:P * t + P], uvw[:, k, :]) for k in range(2)])
            if upon("qkT"):
                pe.wait_ge(s["qk_normed"], NT)
                for g in range(2 * H):
                    transposes("ad"[g % 2], [QK[:, t, g, :] for t in range(NT)], P, DQK)
                pe.wait_ge(s["a_free"], FIRST_A["att"])
                pe.wait_ge(s["d_free"], FIRST_D["att"])
            if upon("att"):
                units = [(t, h) for t in range(NT) for h in range(H)]
                for u in range(len(units) + 2):
                    if u < len(units):
                        t, h = units[u]
                        nk = P * (t + 1)
                        b = bank("a")
                        nc.tensor.matmul(b[:, 0:nk], QKT[0:DQK, h, P * t:P * t + P], QKT[0:DQK, H + h, 0:nk],
                                         start=True, stop=False)
                        full("a", nc.tensor.matmul(b[:, nk - P:nk], cc("lowrow")[0:1, :], cc("negrow")[0:1, :],
                                                   start=False, stop=True))
                    if 1 <= u <= len(units):
                        t, h = units[u - 1]
                        pe.wait_ge(s["probs"], u)
                        transposes("d", [PB[:, (u - 1) % 2, P * j:P * j + P] for j in range(t + 1)])
                    if u >= 2:
                        t, h = units[u - 2]
                        pe.wait_ge(s["d_free"], FIRST_D["att"] + (1 if u == 2 else 2 * (u - 2)))
                        product("d", [(PT[:, (u - 2) % 2, P * j:P * j + P], VA[:, j, 64 * h:64 * h + 64])
                                      for j in range(t + 1)], 64)
            if upon("pr"):
                for m in range(14):
                    w = chunk(pe, CNUM["pr"] + m // 4)
                    product("a", [(w[:, k, P * (m % 4):P * (m % 4) + P], HT[:, k, :]) for k in range(KD)])
            if upon("lora"):
                lw = chunk(pe, CNUM["lora"], 1)[:, 0, :]
                pe.wait_ge(s["lora_in"], 2)
                pe.wait_ge(s["prt"], 14)
                for m in range(4):
                    product("a", [(lw[0:64, P * m:P * m + P], LT[0:64, 2, :])])
                for m in range(4):
                    product("a", [(lw[64:128, P * m:P * m + P], LT[64:128, 0, :])])
                for t in range(NT):
                    product("a", [(LT[:, 3, P * t:P * t + P], lw[:, 512:1024])])
            if upon("kn"):
                for m in range(4):
                    pe.wait_ge(s["kx_sq"], m + 1)
                    product("d", [(cc("heads"), E1[:, m, :])])
            if upon("bonus"):
                pe.wait_ge(s["rkk"], 1)
                b = bank("d")
                for t in range(NT):
                    for m in range(4):
                        o = 8 * t + 2 * m
                        ins = nc.tensor.matmul(b[:, o:o + 2], E1[:, m, P * t:P * t + P], cc("head2"),
                                               start=True, stop=True)
                full("d", ins)
            if upon("tok"):
                for t in range(NT):
                    transposes("d", [VT[:, m, P * t:P * t + P] for m in range(4)])
                pe.wait_ge(s["rhat"], 4)
                for t in range(NT):
                    transposes("a", [KT[:, m, P * t:P * t + P] for m in range(4)])
                    transposes("d", [AT[:, m, P * t:P * t + P] for m in range(4)])
            for grp in range(2):
                if not upon(f"inv{grp}"):
                    break
                fa, fd = FIRST_A[f"inv{grp}"], FIRST_D[f"inv{grp}"]
                if grp == 0:
                    pe.wait_ge(s["a_free"], fa)
                    pe.wait_ge(s["d_free"], fd)
                for q in range(4):
                    h = 4 * grp + q
                    o = 64 * (h % 2)
                    b = bank("d")
                    for c in range(NT):
                        sl = slice(P * c, P * c + P)
                        ins = nc.tensor.matmul(b[:, sl], AT[o:o + 64, h // 2, sl], KK[o:o + 64, h // 2, sl],
                                               start=True, stop=True)
                    full("d", ins)
                for q in range(4):
                    pe.wait_ge(s["x1t"], 4 * grp + q + 1)
                    transposes("a", [XT(4 * grp + q)[:, P * c:P * c + P] for c in range(NT)])
                for lev in range(1, LEVELS):
                    last = lev == LEVELS - 1
                    for q in range(4):
                        if lev == 1:
                            pe.wait_ge(s["a_free"], fa + q + 1)
                        else:
                            pe.wait_ge(s["d_free"], fd + 4 + 8 * (lev - 2) + 2 * q + 2)
                        pe.wait_ge(s["ct"], 24 * grp + 4 * (lev - 1) + q + 1)
                        b = bank("a")
                        for c in range(NT):
                            sl = slice(P * c, P * c + P)
                            ins = nc.tensor.matmul(b[:, sl], CTL[:, q, sl], XI[:, q, sl], start=True, stop=True)
                        full("a", ins)
                    for q in range(4):
                        xt = XT(4 * grp + q)
                        pe.wait_ge(s["a_free"], fa + 4 * lev + q + 1)
                        b = bank("d")
                        for c in range(NT):
                            sl = slice(P * c, P * c + P)
                            ins = nc.tensor.matmul(b[:, sl], ZI[:, q, sl], xt[:, sl], start=True, stop=True)
                        full("d", ins)
                        if not last:
                            b = bank("d")
                            for c in range(NT):
                                sl = slice(P * c, P * c + P)
                                ins = nc.tensor.matmul(b[:, sl], xt[:, sl], ZI[:, q, sl], start=True, stop=True)
                            full("d", ins)
            if upon("chain"):
                fa, fd = FIRST_A["chain"], FIRST_D["chain"]

                def matrices(c):
                    sl = slice(P * c, P * c + P)
                    for left, right in ((KT, KK), (KT, RT), (AT, RT)):
                        for odd in range(2):
                            b = bank("d")
                            o = 64 * odd
                            for q in range(4):
                                ins = nc.tensor.matmul(b[:, P * q:P * q + P], left[o:o + 64, q, sl],
                                                       right[o:o + 64, q, sl], start=True, stop=True)
                            full("d", ins)

                matrices(0)
                pe.wait_ge(s["d_free"], fd)
                pe.wait_ge(s["tmid"], 1)
                for c in range(NT):
                    sl = slice(P * c, P * c + P)
                    mat, f_, sk_ = MATS[c % 2], FS[c % 2][:, 0, :], FS[c % 2][:, 1, :]
                    heads = [(h, slice(64 * h, 64 * h + 64)) for h in range(H)]
                    pe.wait_ge(s["d_free"], fd + 7 * c + 6)
                    b = bank("a")
                    for h, hv in heads:
                        nc.tensor.matmul(b[:, hv], KK[:, h // 2, sl], tmid[:, hv], start=True, stop=False)
                        ins = nc.tensor.matmul(b[:, hv], mat[:, 0, h, :], VTOK[:, c, hv], start=False, stop=True)
                    full("a", ins)
                    if c + 1 < NT:
                        matrices(c + 1)
                    pe.wait_ge(s["a_free"], fa + 3 * c + 1)
                    b = bank("a")
                    for h, hv in heads:
                        ins = nc.tensor.matmul(b[:, hv], XT(h)[:, sl], f_[:, hv], start=True, stop=True)
                    full("a", ins)
                    pe.wait_ge(s["a_free"], fa + 3 * c + 2)
                    b = bank("d")
                    for pr in range(4):
                        f2 = slice(P * pr, P * pr + P)
                        nc.tensor.matmul(b[:, f2], ident, tmid[:, f2], start=True, stop=False)
                        nc.tensor.matmul(b[:, f2], KTOK[:, c, f2], VTOK[:, c, f2], start=False, stop=False)
                        ins = nc.tensor.matmul(b[:, f2], BTOK[:, c, f2], sk_[:, f2], start=False, stop=True)
                    full("d", ins)
                    b = bank("a")
                    for h, hv in heads:
                        nc.tensor.matmul(b[:, hv], RT[:, h // 2, sl], tmid[:, hv], start=True, stop=False)
                        nc.tensor.matmul(b[:, hv], mat[:, 1, h, :], VTOK[:, c, hv], start=False, stop=False)
                        ins = nc.tensor.matmul(b[:, hv], mat[:, 2, h, :], sk_[:, hv], start=False, stop=True)
                    full("a", ins)
            if upon("yT"):
                turn("ycomb")
            if upon("wo"):
                pe.wait_ge(s["a_free"], FIRST_A["wo"])
                pe.wait_ge(s["d_free"], FIRST_D["wo"])
                for half in range(2):
                    w = chunk(pe, CNUM["wo"] + half)
                    for t in range(NT):
                        product("d", [(HT[:, k, P * t:P * t + P], w[:, k, :]) for k in range(KD)])
            if upon("hT2"):
                turn("xn2")
            if upon("pq"):
                pe.wait_ge(s["a_free"], FIRST_A["pq"])
                pe.wait_ge(s["d_free"], FIRST_D["pq"])
                for m in range(16):
                    w = chunk(pe, CNUM["pq"] + m // 4)
                    product("ad"[m % 2], [(w[:, k, P * (m % 4):P * (m % 4) + P], HT[:, k, :]) for k in range(KD)])
            if upon("s"):
                pe.wait_ge(s["a_free"], FIRST_A["s"])
                pe.wait_ge(s["d_free"], FIRST_D["ada"])
                kw = chunk(pe, CNUM["keys"], 16)
                for t in range(NT):
                    for g4 in range(4):
                        b = bank("a")
                        for i in range(4):
                            g = 4 * g4 + i
                            ins = nc.tensor.matmul(b[:, P * i:P * i + P], QPT[:, g, P * t:P * t + P], kw[:, g, :],
                                                   start=True, stop=True)
                        full("a", ins)
            if upon("ada"):
                pe.wait_ge(s["csil"], 8)
                for i in range(12):
                    w = chunk(pe, CNUM["ada"] + i)
                    b = bank("a")
                    for k in range(KD):
                        ins = nc.tensor.matmul(b, SILU[:, k, :], w[:, k, :], start=(k == 0), stop=(k == KD - 1))
                    full("a", ins)
            if upon("modc"):
                pe.wait_ge(s["a_free"], FIRST_A["hT3"])
                b = bank("d")
                for i in range(32):
                    ins = nc.tensor.matmul(b[:, i:i + 1], MODROW[0:1, P * i:P * i + P], cc("ones")[0:1, 0:1],
                                           start=True, stop=True)
                full("d", ins)
            if upon("acc"):
                fours = cc("ones")[0:1, :].unsqueeze(1).broadcast_to([1, 4, P])
                for t in range(NT):
                    acc = [bank("d"), bank("d")]
                    for half in range(2):
                        nc.tensor.matmul(acc[half], cc("zero")[0:1, :], fours, start=True, stop=False)
                    with pe.Fori(0, NSEL // RING) as it:
                        for j in range(RING):
                            pe.wait_ge(s["diag"], it * RING + (NSEL * t + j + 1))
                            for half in range(2):
                                ins = nc.tensor.matmul(acc[half], DG[:, j, :],
                                                       UV[:, j, D + 512 * half:D + 512 * half + 512],
                                                       start=False, stop=False)
                            ins.then_inc(s["uv_used"], 1)
                    for half in range(2):
                        full("d", nc.tensor.matmul(acc[half], cc("zero")[0:1, :], fours, start=False,
                                                   stop=True))
            if upon("hT3"):
                turn("xn3")
            if upon("in2"):
                pe.wait_ge(s["a_free"], FIRST_A["in2"])
                pe.wait_ge(s["d_free"], FIRST_D["in2"])
                for i in range(7):
                    w = chunk(pe, CNUM["in2"] + i)
                    for m in range(4):
                        product("d" if i == 1 else "a",
                                [(w[:, k, P * m:P * m + P], HT[:, k, :]) for k in range(KD)])
            if upon("ln"):
                pe.wait_ge(s["conv"], 4)
                product("d", [(cc("ones"), CV[:, m, :]) for m in range(4)])
                pe.wait_ge(s["convsq"], 4)
                product("d", [(cc("ones"), HN[:, m, 0:512]) for m in range(4)])
            if upon("pw"):
                pe.wait_ge(s["silu"], 4)
                w = chunk(pe, CNUM["pw"])
                for m in range(8):
                    product("d", [(w[:, k, P * m:P * m + P], CV[:, k, :]) for k in range(4)])
            if upon("yb"):
                w = chunk(pe, CNUM["pool"])
                pe.wait_ge(s["pooled"], 4)
                for m in range(8):
                    product("d", [(w[:, m // 2, P * (m % 2):P * (m % 2) + P], PO[:, m // 2, :])])
            if upon("wout"):
                pe.wait_ge(s["merged"], 8)
                for half in range(2):
                    w = chunk(pe, CNUM["wout"] + half)
                    for t in range(NT):
                        product("d", [(MG[:, k, P * t:P * t + P], w[:, k, :]) for k in range(KD)])
            if upon("hT4"):
                turn("xn4")
            if upon("up"):
                pe.wait_ge(s["a_free"], FIRST_A["up"])
                pe.wait_ge(s["d_free"], FIRST_D["up"])
                for i in range(11):
                    w = chunk(pe, CNUM["up"] + i)
                    for m in range(4):
                        product("a", [(w[:, k, P * m:P * m + P], HT[:, k, :]) for k in range(KD)])
            if upon("down"):
                banks = [[bank("a") for _ in range(NT)], [bank("d") for _ in range(NT)]]
                for i in range(6):
                    w = chunk(pe, CNUM["down"] + i)
                    nk = w.shape[1]
                    for kk in range(nk):
                        k = 4 * i + kk
                        pe.wait_ge(s["ff"], k + 1)
                        for half in range(2):
                            for t in range(NT):
                                ins = nc.tensor.matmul(banks[half][t], FT[:, k, P * t:P * t + P],
                                                       w[:, kk, 512 * half:512 * half + 512],
                                                       start=(k == 0), stop=(k == NF - 1))
                                if k == NF - 1:
                                    full("ad"[half], ins)
                    if i < 3:
                        pe.drain().then_inc(s_down, 1)
            if dbg is not None:
                tell(pe.drain(), "fin")

        @block.scalar
        def _(act):
            A = nc.scalar.activation

            def take():
                j = n["a_free"]
                act.wait_ge(s["a_full"], j + 1)
                return PA[:, j % 4, :]

            def link():
                act.wait_ge(s["act"], n["act"])

            def turned(dst, scale=None, bias=None):
                for k in range(0, KD, 2):
                    tell(A(dst[:, k, :], take(), ACT.Identity, scale=scale(k) if scale else 1.0,
                           bias=bias(k) if bias else 0.0), "a_free")

            def roots(*tiles):
                for v in tiles:
                    act.wait_ge(s["var"], n["rstd"] + 1)
                    tell(A(v, v, ACT.Sqrt), "rstd")

            def ffv(t):
                return ffst[:, 24 * t + 13:24 * t + 14]

            roots(st_a[:, 0:4])
            act.wait_ge(s["in_const"], 64)
            turned(HT, lambda k: vv("g_mix", k))
            if upon("pm"):
                for t in range(NT):
                    tell(nc.scalar.copy(PM[:, t, 0:512], take()), "a_free")
                act.wait_ge(s["sscan"], 1)
                tell(A(sinb[:, :], ang[:, :], ACT.Sin), "act")
                act.wait_ge(s["sscan"], 2)
                tell(A(cosb[:, :], kint[:, :], ACT.Sin), "act")
            if upon("cT"):
                roots(st_a[:, 8:16])
                for g in (0, 2, 4):
                    sc_ = vv("g_cq", g) if g < 3 else vv("g_ckv", g - 3)
                    tell(A(CT[:, g, :], take(), ACT.Copy, scale=sc_), "a_free")
            if upon("q"):
                for t in range(NT):
                    tell(nc.scalar.copy(QK[:, t, 0:4, :].rearrange("p g d -> p (g d)"), take()[:, 0:384]), "a_free")
            if upon("kv"):
                for t in range(NT):
                    tell(nc.scalar.copy(QK[:, t, H:2 * H, 0:DN], take().rearrange("p (h d) -> p h d", h=H)), "a_free")
            if upon("qkT"):
                roots(*[st_a[:, 16:32]] * NT)
                for g in range(0, 2 * H, 2):
                    tell(nc.scalar.copy(QKT[0:DQK, g, :], take()[0:DQK, :]), "a_free")
            if upon("att"):
                u = 0
                for t in range(NT):
                    for h in range(H):
                        b = take()
                        nk = P * (t + 1)
                        act.wait_ge(s["smax"], u + 1)
                        if u >= 2:
                            act.wait_ge(s["d_full"], FIRST_D["att"] + (1 if u == 2 else 2 * u - 4))
                        tell(A(PB[:, u % 2, 0:nk], b[:, 0:nk], ACT.Exp, bias=nmax[:, u:u + 1], scale=DQK ** -0.5,
                               accum_out=rsum[:, u:u + 1]), "probs")
                        act.wait_ge(s["probs"], u + 1)
                        tell(nc.scalar.copy(st_a[:, 63:64], rsum[:, u:u + 1]), "a_free")
                        u += 1
                roots(*[st_a[:, 16:24]] * NT)
            if upon("pr"):
                for m in range(14):
                    b = take()
                    if m == 0:
                        act.wait_ge(s["raw_used"], 1)
                    if m >= 4:
                        act.wait_ge(s["raw_used"], m - 2)
                    tell(nc.scalar.copy(RAW[:, m % 4, 1:513], b), "a_free")
            if upon("lora"):
                act.wait_ge(s["prt"], 14)
                tell(A(LT[0:64, 2, :], LT[0:64, 0, :], ACT.Tanh), "lora_in")
                tell(A(LT[:, 3, :], LT[:, 1, :], ACT.Sigmoid), "lora_in")
                for m in range(4):
                    tell(A(SG[:, m, :], take(), ACT.Sigmoid, bias=vv("w0", m)), "a_free")
                for m in range(4):
                    tell(A(AT[:, m, :], take(), ACT.Sigmoid, bias=vv("a0", m)), "a_free")
                for t in range(NT):
                    tell(nc.scalar.copy(GT[:, t, :], take()), "a_free")
            if upon("kn"):
                roots(*[E2[:, m, :] for m in range(4)])
            if upon("tok"):
                act.wait_ge(s["Lm"], 1)
                tell(A(fdec[:, :], fdec[:, :], ACT.Exp, scale=-KAPPA), "rexp")
                act.wait_ge(s["Lm"], 2)
                act.wait_ge(s["d_full"], FIRST_D["tok"])
                tell(A(E1[:, :, :], CS[:, :, :], ACT.Exp, scale=-KAPPA), "rexp")
                tell(A(E2[:, :, :], CS[:, :, :], ACT.Exp, scale=KAPPA), "rexp")
                act.wait_ge(s["Lm"], 3)
                act.wait_ge(s["d_full"], FIRST_D["tok"] + 4)
                tell(A(EQ[:, :, :], SG[:, :, :], ACT.Exp, scale=-KAPPA), "rexp")
                act.wait_ge(s["rexp"], n["rexp"])
                for t in range(NT):
                    tell(nc.scalar.copy(KTOK[:, t, :], take()), "a_free")
            for grp in range(2):
                if not upon(f"inv{grp}"):
                    break
                for q in range(4):
                    tell(nc.scalar.copy(XI[:, q, :], take()), "a_free")
                for lev in range(1, LEVELS):
                    for q in range(4):
                        b = take()
                        if lev > 1:
                            act.wait_ge(s["d_full"], FIRST_D[f"inv{grp}"] + 4 + 8 * (lev - 2) + 2 * q + 2)
                        tell(nc.scalar.copy(ZI[:, q, :], b), "a_free")
            if upon("chain"):
                for c in range(NT):
                    for dst in (FS[c % 2][:, 0, :], FS[c % 2][:, 1, :], HN[:, c, 512:1024]):
                        tell(nc.scalar.copy(dst, take()), "a_free")
            if upon("yT"):
                roots(*[st_a[:, 16:24]] * NT)
                turned(HT)
            if upon("hT2"):
                roots(st_a[:, 0:4])
                turned(HT)
            if upon("pq"):
                for m in range(0, 16, 2):
                    tell(nc.scalar.copy(QPT[:, m, :], take()), "a_free")
            if upon("s"):
                for t in range(NT):
                    for g4 in range(4):
                        tell(nc.scalar.copy(SS[t][:, 512 * g4:512 * g4 + 512], take()), "a_free")
            if upon("ada"):
                tell(A(csil2, vv("c"), ACT.Silu), "act")
                link()
                act.wait_ge(s["a_full"], FIRST_A["ada"])
                for k in range(KD):
                    tell(A(SILU[:, k, :], cc("ones"), ACT.Copy, scale=csil2[:, k:k + 1]), "csil")
                for i in range(12):
                    b = take()
                    if i // 2 in (2, 5):
                        g = (0 if i < 6 else 1024) + 512 * (i % 2)
                        tell(nc.scalar.copy(RW[:, g:g + 512], b), "a_free")
                    else:
                        r = i if i < 4 else i - 2
                        tell(nc.scalar.copy(MODROW[0:1, 512 * r:512 * r + 512], b[0:1, :]), "a_free")
            if upon("acc"):
                def gate_exp(t):
                    act.wait_ge(s["topk"], t + 1)
                    tell(A(GATE[:, t % 2, :], GATE[:, t % 2, :], ACT.Exp), "geluv")

                for t in range(NT):
                    gate_exp(t)
                    with act.Fori(0, NSEL // RING) as it:
                        for g in range(RING // GRP):
                            act.wait_ge(s["dots"], it * RING + (NSEL * t + GRP * (g + 1)))
                            A(GEL[:, g, :], DOT[:, g, :], ACT.Gelu).then_inc(s["gelu"], 1)
            if upon("hT3"):
                roots(*[ffv(t) for t in range(NT)])
                turned(HT, lambda k: modc[:, 8 + k:9 + k], lambda k: modc[:, k:k + 1])
            if upon("in2"):
                for m in range(4):
                    tell(A(SGA[:, m, :], take(), ACT.Sigmoid), "a_free")
                for m in range(4):
                    tell(nc.scalar.copy(UP[:, m, 16:528], take()), "a_free")
                for m in range(8):
                    tell(A(GA[:, m, :], take(), ACT.Sigmoid), "a_free")
                for m in range(8):
                    tell(A(GB[:, m, :], take(), ACT.Sigmoid), "a_free")
            if upon("ln"):
                roots(HN[:, 0, 512:1024])
                for m in range(4):
                    act.wait_ge(s["silu_in"], m + 1)
                    tell(A(CV[:, m, :], CV[:, m, :], ACT.Silu, scale=vv("ln_a_g", m), bias=vv("ln_a_b", m)), "silu")
            if upon("hT4"):
                roots(*[ffv(t) for t in list(range(NT)) * 2])
                turned(HT, lambda k: modc[:, 24 + k:25 + k], lambda k: modc[:, 16 + k:17 + k])
            if upon("up"):
                for j in range(NF):
                    for i in range(2):
                        b = take()
                        q = 2 * (j % 2) + i
                        act.wait_ge(s["upraw_used"], max(1, 2 * (j - 2) + i + 2))
                        tell(nc.scalar.copy(UR[:, q, 2:514], b), "a_free")
                    if j >= 1:
                        act.wait_ge(s["gelu_in"], j)
                        tell(A(UC[:, 2 * ((j - 1) % 2) + 1, :], UC[:, 2 * ((j - 1) % 2) + 1, :],
                               ACT.Gelu_apprx_tanh), "ffgelu")
                act.wait_ge(s["gelu_in"], NF)
                tell(A(UC[:, 2 * ((NF - 1) % 2) + 1, :], UC[:, 2 * ((NF - 1) % 2) + 1, :],
                       ACT.Gelu_apprx_tanh), "ffgelu")
            if upon("down"):
                for t in range(NT):
                    tell(nc.scalar.copy(HN[:, t, 0:512], take()), "a_free")
                roots(*[ffv(t) for t in range(NT)])
            if dbg is not None:
                act.wait_ge(s["a_free"], n["a_free"])
                tell(act.drain(), "fin")

        @block.vector
        def _(dve):
            tt, ts, stt = nc.vector.tensor_tensor, nc.vector.tensor_scalar, nc.vector.scalar_tensor_tensor
            ttr = nc.vector.tensor_tensor_reduce

            def take():
                j = n["d_free"]
                dve.wait_ge(s["d_full"], j + 1)
                return PD[:, j % 4, :]

            def link(ins=None, name="dve"):
                if ins is not None:
                    tell(ins, name)
                dve.wait_ge(s[name], n[name])

            def rstd(dst, scale, eps):
                w = dst.shape[-1]
                r_, v_ = root[:, 0:w], root[:, 16:16 + w]
                link(ts(v_, dst, scale, eps, ALU.mult, ALU.add))
                tell(nc.vector.tensor_copy(dst, v_), "var")
                dve.wait_ge(s["rstd"], n["var"])
                link(nc.vector.reciprocal(r_, dst))
                link(tt(v_, v_, r_, ALU.mult))
                link(stt(v_, v_, -0.5, r_, ALU.mult, ALU.mult))
                link(stt(dst, v_, 1.5, r_, ALU.add, ALU.mult))

            def turned(dst, scale=None, bias=None):
                for k in range(1, KD, 2):
                    b = take()
                    if bias:
                        tell(ts(dst[:, k, :], b, scale(k), bias(k), ALU.mult, ALU.add), "d_free")
                    elif scale:
                        tell(ts(dst[:, k, :], b, scale(k), None, ALU.mult), "d_free")
                    else:
                        tell(nc.vector.tensor_copy(dst[:, k, :], b), "d_free")

            def rms_rows(ready, gain=None):
                for t in range(NT):
                    link(ttr(HN[:, t, :], X[:, t, :], X[:, t, :], 1.0, 0.0, ALU.mult, ALU.add, st_a[:, t:t + 1]))
                rstd(st_a[:, 0:NT], 1.0 / D, EPS)
                for t in range(NT):
                    if gain is None:
                        tell(ts(HN[:, t, :], X[:, t, :], st_a[:, t:t + 1], None, ALU.mult), ready)
                    else:
                        tell(stt(HN[:, t, :], X[:, t, :], st_a[:, t:t + 1], gain, ALU.mult, ALU.mult), ready)

            dve.wait_ge(s["in_x"], 64)
            rms_rows("xn")
            dve.wait_ge(s["in_const"], 64)
            if upon("pm"):
                TWO_PI = [6.28125, 0.0019350051879882812, 3.0199159819567e-07]
                MAGIC = 12582912.0
                link(nc.vector.tensor_copy(posf[:, :], posi[:, :]))
                a3 = ang.rearrange("p (t i) -> p t i", t=NT)
                k3 = kint.rearrange("p (t i) -> p t i", t=NT)
                link(tt(a3, posf.unsqueeze(2).broadcast_to([P, NT, HALF]),
                        cc("invfreq").unsqueeze(1).broadcast_to([P, NT, HALF]), ALU.mult))
                link(ts(kint[:, :], ang[:, :], 1.0 / (2 * np.pi), 0.25, ALU.mult, ALU.add))
                link(ts(kint[:, :], kint[:, :], MAGIC, -MAGIC, ALU.add, ALU.add))
                link(stt(cosb[:, :], kint[:, :], -TWO_PI[0], ang[:, :], ALU.mult, ALU.add))
                link(stt(cosb[:, :], kint[:, :], -TWO_PI[1], cosb[:, :], ALU.mult, ALU.add))
                link(stt(cosb[:, :], kint[:, :], -TWO_PI[2], cosb[:, :], ALU.mult, ALU.add))
                link(ts(cosb[:, :], cosb[:, :], np.pi / 2, 3.1415925, ALU.add, ALU.min))
                link(ts(cosb[:, :], cosb[:, :], -3.1415925, None, ALU.max))
                link(ts(sinb[:, :], ang[:, :], 1.0 / (2 * np.pi), None, ALU.mult))
                link(ts(sinb[:, :], sinb[:, :], MAGIC, -MAGIC, ALU.add, ALU.add))
                for c_ in TWO_PI:
                    link(stt(ang[:, :], sinb[:, :], -c_, ang[:, :], ALU.mult, ALU.add))
                link(ts(ang[:, :], ang[:, :], 3.1415925, -3.1415925, ALU.min, ALU.max), "sscan")
                link(nc.vector.tensor_copy(kint[:, :], cosb[:, :]), "sscan")
            turned(HT, lambda k: vv("g_mix", k))
            if upon("pm"):
                for t in range(NT):
                    tell(nc.vector.tensor_copy(PM[:, t, 512:672], take()[:, 0:160]), "d_free")
                dve.wait_ge(s["a_free"], FIRST_A["cT"])
                dve.wait_ge(s["d_free"], n["d_free"])
            TMP = HN[:, 0:2, :].rearrange("p a b -> p (a b)")
            if upon("cT"):
                dve.wait_ge(s["a_full"], FIRST_A["pm"])
                dve.wait_ge(s["d_full"], FIRST_D["pm"])
                st = st_a[:, 8:16]
                for t in range(NT):
                    link(ttr(TMP[:, 0:QR], PM[:, t, 0:QR], PM[:, t, 0:QR], 1.0 / QR, 0.0, ALU.mult, ALU.add,
                             st[:, 2 * t:2 * t + 1]))
                    link(ttr(TMP[:, QR:QR + KVR], PM[:, t, QR:QR + KVR], PM[:, t, QR:QR + KVR], 1.0 / KVR, 0.0,
                             ALU.mult, ALU.add, st[:, 2 * t + 1:2 * t + 2]))
                rstd(st, 1.0, EPS)
                for t in range(NT):
                    link(ts(PM[:, t, 0:QR], PM[:, t, 0:QR], st[:, 2 * t:2 * t + 1], None, ALU.mult))
                    tell(ts(PM[:, t, QR:QR + KVR], PM[:, t, QR:QR + KVR], st[:, 2 * t + 1:2 * t + 2], None,
                            ALU.mult), "cn")
                for t in range(NT):
                    link(nc.vector.tensor_copy(QK[:, t, H:2 * H, DN:DQK],
                                               PM[:, t, QR + KVR:MLA_COLS].unsqueeze(1).broadcast_to([P, H, DR])))
                for g in (1, 3):
                    sc_ = vv("g_cq", g) if g < 3 else vv("g_ckv", g - 3)
                    tell(ts(CT[:, g, :], take(), sc_, None, ALU.mult), "d_free")
            if upon("q"):
                for t in range(NT):
                    tell(nc.vector.tensor_copy(QK[:, t, 4:8, :].rearrange("p g d -> p (g d)"), take()[:, 0:384]),
                         "d_free")
            if upon("kv"):
                for t in range(NT):
                    tell(nc.vector.tensor_copy(VA[:, t, :], take()), "d_free")
                dve.wait_ge(s["d_free"], n["d_free"])
            if upon("qkT"):
                dve.wait_ge(s["a_free"], FIRST_A["qkT"])
                dve.wait_ge(s["act"], 2)
                tmp3 = TMP[:, 0:1536].rearrange("p (g d) -> p g d", g=2 * H)
                ro = [TMP[:, 256 * i:256 * i + 256].rearrange("p (g i) -> p g i", g=2 * H) for i in range(4)]
                for t in range(NT):
                    st = st_a[:, 16:32]
                    q3 = QK[:, t, :, :]
                    link(tt(tmp3, q3, q3, ALU.mult))
                    link(nc.vector.tensor_reduce(st, tmp3, AX, ALU.add))
                    rstd(st, 1.0 / DQK, EPS)
                    link(tt(q3, q3, st.unsqueeze(2).broadcast_to([P, 2 * H, DQK]), ALU.mult))
                    link(tt(q3[:, 0:H, :], q3[:, 0:H, :], r1("g_q").unsqueeze(1).broadcast_to([P, H, DQK]), ALU.mult))
                    link(tt(q3[:, H:2 * H, :], q3[:, H:2 * H, :], r1("g_k").unsqueeze(1).broadcast_to([P, H, DQK]),
                            ALU.mult))
                    co = cosb[:, HALF * t:HALF * t + HALF].unsqueeze(1).broadcast_to([P, 2 * H, HALF])
                    si = sinb[:, HALF * t:HALF * t + HALF].unsqueeze(1).broadcast_to([P, 2 * H, HALF])
                    t1, t2 = q3[:, :, DN:DN + HALF], q3[:, :, DN + HALF:DQK]
                    tell(tt(ro[0], t1, co, ALU.mult), "dve")
                    tell(tt(ro[1], t2, si, ALU.mult), "dve")
                    tell(tt(ro[2], t1, si, ALU.mult), "dve")
                    link(tt(ro[3], t2, co, ALU.mult))
                    tell(tt(t1, ro[0], ro[1], ALU.subtract), "dve")
                    link(tt(t2, ro[2], ro[3], ALU.add), "qk_normed")
                    link()
                for g in range(1, 2 * H, 2):
                    tell(nc.vector.tensor_copy(QKT[0:DQK, g, :], take()[0:DQK, :]), "d_free")
            if upon("att"):
                units = [(t, h) for t in range(NT) for h in range(H)]
                for u in range(len(units) + 2):
                    if u < len(units):
                        t, h = units[u]
                        nk = P * (t + 1)
                        dve.wait_ge(s["a_full"], FIRST_A["att"] + u + 1)
                        b = PA[:, (FIRST_A["att"] + u) % 4, 0:nk]
                        link(nc.vector.tensor_reduce(nmax[:, u:u + 1], b, AX, ALU.max))
                        tell(ts(nmax[:, u:u + 1], nmax[:, u:u + 1], -DQK ** -0.5, None, ALU.mult), "smax")
                    if 1 <= u <= len(units):
                        t, h = units[u - 1]
                        b = take()
                        if u >= 3:
                            dve.wait_ge(s["d_full"], FIRST_D["att"] + 2 * (u - 3) + 3)
                        tell(nc.vector.tensor_copy(PT[:, (u - 1) % 2, 0:P * (t + 1)], b[:, 0:P * (t + 1)]), "d_free")
                    if u >= 2:
                        t, h = units[u - 2]
                        b = take()
                        dve.wait_ge(s["a_free"], FIRST_A["att"] + u - 1)
                        link(nc.vector.reciprocal(st_a[:, 32:33], rsum[:, u - 2:u - 1]))
                        link(ts(HN[:, t, 64 * h:64 * h + 64], b[:, 0:64], st_a[:, 32:33], None, ALU.mult), "d_free")
                dve.wait_ge(s["d_free"], n["d_free"])
                tmp8 = TMP[:, 1536:2048].rearrange("p (h d) -> p h d", h=H)
                for t in range(NT):
                    o3 = HN[:, t, 0:512].rearrange("p (h d) -> p h d", h=H)
                    t3 = AR[:, 0:512].rearrange("p (h d) -> p h d", h=H)
                    st = st_a[:, 16:24]
                    link(tt(t3, o3, o3, ALU.mult))
                    link(nc.vector.tensor_reduce(st, t3, AX, ALU.add))
                    rstd(st, 1.0 / 64, EPS)
                    link(tt(o3, o3, st.unsqueeze(2).broadcast_to([P, H, 64]), ALU.mult))
                    link(tt(HN[:, t, 0:512], HN[:, t, 0:512], r1("g_attn"), ALU.mult), "o_normed")
            if upon("pr"):
                dve.wait_ge(s["dve"], n["dve"])
                tell(nc.vector.memset(RAW[:, :, 0:1], 0.0), "raw_used")
                for m in range(14):
                    dst = (RT, KT, VT, LT)[m // 4][:, m % 4, :]
                    dve.wait_ge(s["a_free"], FIRST_A["pr"] + m + 1)
                    raw = RAW[:, m % 4, :]
                    link(tt(dst, raw[:, 0:512], raw[:, 1:513], ALU.subtract))
                    link(stt(dst, dst, vv("mu", m), raw[:, 1:513], ALU.mult, ALU.add), "raw_used")
                    tell(dve.nop(), "prt")
            if upon("kn"):
                for m in range(4):
                    link(ts(KK[:, m, :], KT[:, m, :], vv("k_k", m), None, ALU.mult))
                    tell(tt(E1[:, m, :], KK[:, m, :], KK[:, m, :], ALU.mult), "kx_sq")
                for m in range(4):
                    b = take()
                    link(ts(E2[:, m, :], b, 1e-24, None, ALU.max), "d_free")
                    tell(dve.nop(), "var")
                for m in range(4):
                    dve.wait_ge(s["rstd"], n["var"] - 3 + m)
                    link(nc.vector.reciprocal(E2[:, m, :], E2[:, m, :]))
                    link(tt(KK[:, m, :], KK[:, m, :], E2[:, m, :], ALU.mult))
            if upon("bonus"):
                dve.wait_ge(s["a_free"], FIRST_A["lora"] + 12)
                omk = st_a[:, 40:44]
                link(ts(omk, vv("k_a"), -1.0, 1.0, ALU.mult, ALU.add))
                for m in range(4):
                    link(ts(E2[:, m, :], AT[:, m, :], vv("k_a", m), omk[:, m:m + 1], ALU.mult, ALU.add))
                    link(tt(KT[:, m, :], KT[:, m, :], E2[:, m, :], ALU.mult))
                    link(stt(E1[:, m, :], RT[:, m, :], vv("r_k", m), KT[:, m, :], ALU.mult, ALU.mult))
                tell(dve.nop(), "rkk")
                b = take()
                tell(nc.vector.tensor_copy(bon[:, :], b[:, 0:32]), "d_free")
            if upon("tok"):
                for m in range(4):
                    for c in range(NT):
                        sl = slice(P * c, P * c + P)
                        tell(nc.vector.tensor_tensor_scan(CS[:, m, sl], cc("ones"), SG[:, m, sl], 0.0,
                                                          ALU.mult, ALU.add), "dve")
                link()
                cs4 = CS.rearrange("p m (c n) -> p m c n", c=NT)
                f4 = fdec.rearrange("p (m c) -> p m c", m=4)
                mid, end = cs4[:, :, :, 63:64].squeeze(3), cs4[:, :, :, 127:128].squeeze(3)
                md = st_a[:, 44:60].rearrange("p (m c) -> p m c", m=4)
                link(nc.vector.tensor_copy(md, mid))
                link(tt(f4, end, md, ALU.subtract))
                link(tt(f4[:, :, 0:3], f4[:, :, 0:3], md[:, :, 1:4], ALU.add), "Lm")
                link()
                for m in range(4):
                    tell(tt(cs4[:, m, :, :], cs4[:, m, :, :], md[:, m, :].unsqueeze(2).broadcast_to([P, NT, P]),
                            ALU.subtract), "dve")
                link()
                tell(dve.nop(), "Lm")
                link(tt(SG[:, :, :], CS[:, :, :], SG[:, :, :], ALU.subtract), "Lm")
                for t in range(NT):
                    tell(nc.vector.tensor_copy(VTOK[:, t, :], take()), "d_free")
                dve.wait_ge(s["rexp"], 2)
                link(tt(RT[:, :, :], RT[:, :, :], E1[:, :, :], ALU.mult), "rhat")
                dve.wait_ge(s["rexp"], 3)
                link(tt(KT[:, :, :], KT[:, :, :], E2[:, :, :], ALU.mult), "rhat")
                link(stt(AT[:, :, :], AT[:, :, :], -1.0, KK[:, :, :], ALU.mult, ALU.mult))
                link(tt(AT[:, :, :], AT[:, :, :], E2[:, :, :], ALU.mult), "rhat")
                dve.wait_ge(s["rexp"], 4)
                link(tt(KK[:, :, :], KK[:, :, :], EQ[:, :, :], ALU.mult), "rhat")
                for t in range(NT):
                    tell(nc.vector.tensor_copy(BTOK[:, t, :], take()), "d_free")
            def by_chunk(z):
                return z.rearrange("p (c n) -> p c n", c=NT)

            def mask(m_):
                return m_.unsqueeze(1).broadcast_to([P, NT, P])

            for grp in range(2):
                if not upon(f"inv{grp}"):
                    break
                fa = FIRST_A[f"inv{grp}"]
                dve.wait_ge(s["a_free"], fa)
                dve.wait_ge(s["d_free"], n["d_free"])
                if grp == 0:
                    dve.wait_ge(s["rhat"], 4)
                    tell(nc.vector.memset(tmid[:, :], 0.0), "tmid")
                for q in range(4):
                    b = take()
                    tell(tt(by_chunk(MT[:, q, :]), by_chunk(b), mask(cc("strict")), ALU.mult), "d_free")
                dve.wait_ge(s["d_free"], n["d_free"])
                for q in range(4):
                    xt = by_chunk(XT(4 * grp + q))
                    link(tt(xt, by_chunk(MT[:, q, :]), mask(LV[:, 0, :]), ALU.mult))
                    link(tt(xt, xt, mask(ident), ALU.add), "x1t")
                for q in range(4):
                    tell(tt(by_chunk(CTL[:, q, :]), by_chunk(MT[:, q, :]), mask(LV[:, 1, :]), ALU.mult), "ct")
                for lev in range(1, LEVELS):
                    for q in range(4):
                        xt = XT(4 * grp + q)
                        b = take()
                        if lev < LEVELS - 1:
                            dve.wait_ge(s["d_full"], n["d_free"] + 2)
                        tell(tt(xt, xt, b, ALU.add), "d_free")
                        if lev < LEVELS - 1:
                            b = take()
                            tell(tt(XI[:, q, :], XI[:, q, :], b, ALU.add), "d_free")
                            dve.wait_ge(s["a_full"], fa + 4 * lev + q + 1)
                            tell(tt(by_chunk(CTL[:, q, :]), by_chunk(MT[:, q, :]), mask(LV[:, lev + 1, :]),
                                    ALU.mult), "ct")
            if upon("chain"):
                def matrices(c):
                    for m, mk in enumerate(("strict", "incl", "incl")):
                        for odd in range(2):
                            b = take()
                            tell(tt(MATS[c % 2][:, m, odd:H:2, :], by_chunk(b), mask(cc(mk)), ALU.mult),
                                 "d_free")

                dve.wait_ge(s["d_free"], n["d_free"])
                matrices(0)
                for c in range(NT):
                    if c + 1 < NT:
                        matrices(c + 1)
                    b = take()
                    dve.wait_ge(s["a_full"], FIRST_A["chain"] + 3 * c + 3)
                    for pr in range(4):
                        f2 = slice(P * pr, P * pr + P)
                        ins = stt(tmid[:, f2], b[:, f2], fdec[:, 4 * pr + c:4 * pr + c + 1], cc("heads"),
                                  ALU.mult, ALU.mult)
                        tell(ins, "d_free" if pr == 3 else "dve")
            if upon("yT"):
                dve.wait_ge(s["a_free"], FIRST_A["yT"])
                dve.wait_ge(s["d_full"], FIRST_D["yT"])
                dve.wait_ge(s["d_free"], n["d_free"])
                g1_, g2_ = AR[:, 18432:18944], AR[:, 18944:19456]
                h3 = lambda z: z.rearrange("p (h d) -> p h d", h=H)
                for t in range(NT):
                    y = HN[:, t, 512:1024]
                    st = st_a[:, 16:24]
                    bc = lambda z: z.unsqueeze(2).broadcast_to([P, H, 64])
                    link(nc.vector.tensor_reduce(st, h3(y), AX, ALU.add))
                    link(ts(st, st, 1.0 / 64, None, ALU.mult))
                    link(tt(h3(y), h3(y), bc(st), ALU.subtract))
                    link(tt(g1_, y, y, ALU.mult))
                    link(nc.vector.tensor_reduce(st, h3(g1_), AX, ALU.add))
                    rstd(st, 1.0 / 64, LN_X_EPS)
                    link(tt(h3(y), h3(y), bc(st), ALU.mult))
                    link(tt(y, y, r1("ln_x_w"), ALU.mult))
                    link(tt(y, y, r1("ln_x_b"), ALU.add))
                    link(tt(h3(g2_), h3(VTOK[:, t, :]), bc(bon[:, 8 * t:8 * t + 8]), ALU.mult))
                    link(tt(y, y, g2_, ALU.add))
                    link(tt(y, y, GT[:, t, :], ALU.mult), "ycomb")
                turned(HT)
            if upon("wo"):
                for half in range(2):
                    for t in range(NT):
                        b = take()
                        xs = X[:, t, 512 * half:512 * half + 512]
                        link(tt(xs, xs, b, ALU.add), "d_free")
            if upon("hT2"):
                dve.wait_ge(s["in_gffn"], 16)
                rms_rows("xn2", GF)
                turned(HT)
            if upon("pq"):
                for m in range(1, 16, 2):
                    tell(nc.vector.tensor_copy(QPT[:, m, :], take()), "d_free")

            def top_sixteen(vals, idx, src, width, first, last):
                for g in range(first, last):
                    tell(nc.vector.max(vals[:, 16 * g:16 * g + 8], src[:, width * g:width * g + width]), "dve")
                link()
                for g in range(first, last):
                    tell(nc.vector.max_index(idx[:, 16 * g:16 * g + 8], vals[:, 16 * g:16 * g + 8],
                                             src[:, width * g:width * g + width]), "dve")
                link()
                for g in range(first, last):
                    sg_ = src[:, width * g:width * g + width]
                    tell(nc.vector.match_replace(sg_, vals[:, 16 * g:16 * g + 8], sg_, -3e38), "dve")
                link()
                for g in range(first, last):
                    tell(nc.vector.max(vals[:, 16 * g + 8:16 * g + 16], src[:, width * g:width * g + width]), "dve")
                link()
                for g in range(first, last):
                    tell(nc.vector.max_index(idx[:, 16 * g + 8:16 * g + 16], vals[:, 16 * g + 8:16 * g + 16],
                                             src[:, width * g:width * g + width]), "dve")
                link()

            STEPS = 8

            def select(t, step):
                c4 = CAND.rearrange("p (h a b) -> p h a b", h=H, a=TOPK)
                halves = s1v.rearrange("p (h q k) -> p h q k", h=H, q=2)
                pa_, pb_ = i1u[:, 0:128], i1u[:, 128:256]
                acc_ = [SS[t][:, 0:NSEL], SS[t][:, NSEL:2 * NSEL]]
                if step == 0:
                    dve.wait_ge(s["a_free"], FIRST_A["s"] + 4 * t + 4)
                    top_sixteen(s1v, i1u, SS[t], NK, 0, 8)
                elif step == 1:
                    top_sixteen(s1v, i1u, SS[t], NK, 8, 16)
                elif step == 2:
                    for h in range(H):
                        tell(tt(c4[:, h, :, :], halves[:, h, 0, :].unsqueeze(2).broadcast_to([P, TOPK, TOPK]),
                                halves[:, h, 1, :].unsqueeze(1).broadcast_to([P, TOPK, TOPK]), ALU.add), "dve")
                    link()
                elif step == 3:
                    top_sixteen(tpv, tpu, CAND, TOPK * TOPK, 0, 4)
                elif step == 4:
                    top_sixteen(tpv, tpu, CAND, TOPK * TOPK, 4, 8)
                elif step == 5:
                    g3 = GATE[:, t % 2, :].rearrange("p (h k) -> p h k", h=H)
                    p3 = tpv.rearrange("p (h k) -> p h k", h=H)
                    if t >= 2:
                        dve.wait_ge(s["uv_used"], NSEL * (t - 1))
                    link(tt(g3, p3, p3[:, :, 0:1].broadcast_to([P, H, TOPK]), ALU.subtract), "topk")
                    link(nc.vector.tensor_copy(s1v[:, :], i1u[:, :]))
                    tell(ts(pa_, tpu[:, :], 4, None, ALU.logical_shift_right), "dve")
                    link(ts(pb_, tpu[:, :], 15, None, ALU.bitwise_and))
                if step in (6, 7):
                    q = step - 6
                    link(nc.vector.tensor_copy(tpv[:, :], (pa_, pb_)[q]))
                    eq = CAND.rearrange("p (k a) -> p k a", k=NSEL)
                    link(tt(eq, tpv.unsqueeze(2).broadcast_to([P, NSEL, TOPK]),
                            cc("iota").unsqueeze(1).broadcast_to([P, NSEL, TOPK]), ALU.is_equal))
                    for h in range(H):
                        e3 = c4[:, h, :, :]
                        tell(tt(e3, e3, halves[:, h, q, :].unsqueeze(1).broadcast_to([P, TOPK, TOPK]), ALU.mult), "dve")
                    link()
                    link(nc.vector.tensor_reduce(acc_[q], eq, AX, ALU.add))
                if step == 7:
                    link(stt(acc_[0], acc_[0], float(NK), acc_[1], ALU.mult, ALU.add))
                    link(nc.vector.tensor_copy(IDX[:, t % 2, :], acc_[0]), "idx")

            def gates(t):
                dve.wait_ge(s["geluv"], t + 1)
                g3 = GATE[:, t % 2, :].rearrange("p (h k) -> p h k", h=H)
                link(nc.vector.tensor_reduce(gmx[:, 0:8], g3, AX, ALU.add))
                link(nc.vector.reciprocal(gmx[:, 8:16], gmx[:, 0:8]))
                link(tt(g3, g3, gmx[:, 8:16].unsqueeze(2).broadcast_to([P, H, TOPK]), ALU.mult))

            if upon("modc"):
                if upon("acc"):
                    for step in range(STEPS):
                        select(0, step)
                b = take()
                link(tt(modc[:, :], b[:, 0:32], vv("b_mod"), ALU.add), "d_free")
                for o in (8, 24):
                    link(ts(modc[:, o:o + 8], modc[:, o:o + 8], 1.0, None, ALU.add))
                tell(dve.nop(), "peer_clear")
            if upon("acc"):
                for t in range(NT):
                    gates(t)
                    turns = NSEL // RING
                    cuts = [turns * i // (STEPS + 1) for i in range(STEPS + 2)] if t + 1 < NT else [0, turns]
                    for step, (first, last) in enumerate(zip(cuts[:-1], cuts[1:])):
                        if step > 0:
                            select(t + 1, step - 1)
                        with dve.Fori(first, last) as it:
                            for g in range(RING // GRP + 1):
                                if g < RING // GRP:
                                    for j in range(GRP * g, GRP * g + GRP):
                                        dve.wait_ge(uv_full[j], it * 16 + 16 * (NSEL // RING * t + 1))
                                        ttr(UV[:, j, 0:D], UV[:, j, 0:D], HN[:, t, :], 1.0, 0.0, ALU.mult, ALU.add,
                                            DOT[:, g, j % GRP:j % GRP + 1]).then_inc(s["dots"], 1)
                                if g >= 1:
                                    dve.wait_ge(s["gelu"], it * (RING // GRP) + (NSEL // GRP * t + g))
                                    for j in range(GRP * (g - 1), GRP * g):
                                        sel_ = GATE[:, t % 2, bass.ds(it * RING + j, 1)]
                                        ts(DG[:, j, :], ident, GEL[:, g - 1, j % GRP:j % GRP + 1], sel_,
                                           ALU.mult, ALU.mult).then_inc(s["diag"], 1)
                    for half in range(2):
                        b = take()
                        xs = X[:, t, 512 * half:512 * half + 512]
                        link(tt(xs, xs, b, ALU.add), "d_free")

            def layer_rows(ready, t, src, dst, gain=None, shift=None):
                st = ffst[:, 24 * t:24 * t + 24]
                for i in range(2):
                    tell(nc.vector.bn_stats(st[:, 6 * i:6 * i + 6], src[:, 512 * i:512 * i + 512]), "dve")
                link()
                link(nc.vector.bn_aggr(st[:, 12:14], st[:, 0:12]))
                rstd(st[:, 13:14], 1.0, LN_EPS)
                if gain is None:
                    tell(ts(dst, src, st[:, 12:13], st[:, 13:14], ALU.subtract, ALU.mult), ready)
                else:
                    link(ts(dst, src, st[:, 12:13], st[:, 13:14], ALU.subtract, ALU.mult))
                    link(tt(dst, dst, gain, ALU.mult))
                    link(tt(dst, dst, shift, ALU.add), ready)

            if upon("hT3"):
                tell(dve.nop(), "row2free")
                for t in range(NT):
                    layer_rows("xn3", t, X[:, t, :], HN[:, t, :])
                turned(HT, lambda k: modc[:, 8 + k:9 + k], lambda k: modc[:, k:k + 1])
            if upon("in2"):
                tell(nc.vector.memset(YAP[:, :, 0:30], 0.0), "bufs")
                link(nc.vector.memset(UP[:, :, 0:16], 0.0), "bufs")
                dve.wait_ge(s["a_free"], FIRST_A["in2"] + 4)
                for m in range(4):
                    b = take()
                    link(tt(YAP[:, m, 30:542], b, SGA[:, m, :], ALU.mult), "d_free")
            if upon("ln"):
                for m in range(4):
                    w = vv("w_conv")[:, CONV_K * m:CONV_K * m + CONV_K]
                    link(ts(CV[:, m, :], YAP[:, m, 0:512], w[:, 0:1], vv("b_conv", m), ALU.mult, ALU.add))
                    for j in range(1, CONV_K):
                        link(stt(CV[:, m, :], YAP[:, m, j:j + 512], w[:, j:j + 1], CV[:, m, :], ALU.mult, ALU.add))
                    tell(dve.nop(), "conv")
                b = take()
                for m in range(4):
                    ins = stt(CV[:, m, :], b, -1.0 / RD, CV[:, m, :], ALU.mult, ALU.add)
                    if m < 3:
                        tell(ins, "dve")
                    else:
                        tell(ins, "d_free")
                dve.wait_ge(s["d_free"], n["d_free"])
                link()
                dve.wait_ge(s["a_full"], FIRST_A["in2"])
                for m in range(4):
                    tell(tt(HN[:, m, 0:512], CV[:, m, :], CV[:, m, :], ALU.mult), "convsq")
                b = take()
                link(ts(HN[:, 0, 512:1024], b, 1.0 / RD, LN_EPS, ALU.mult, ALU.add), "d_free")
                tell(dve.nop(), "var")
                dve.wait_ge(s["rstd"], n["var"])
                link(nc.vector.reciprocal(HN[:, 0, 512:1024], HN[:, 0, 512:1024]))
                for m in range(4):
                    tell(tt(CV[:, m, :], CV[:, m, :], HN[:, 0, 512:1024], ALU.mult), "silu_in")
            if upon("yb"):
                for m, w in enumerate(POOL):
                    if m == 0:
                        dve.wait_ge(s["a_free"], FIRST_A["in2"] + 8)
                    u = UP[:, m, :]
                    src = u
                    step = 1
                    bufs_ = [HN[:, 1, 0:528], HN[:, 2, 0:528]]
                    i = 0
                    while step < w:
                        dst = bufs_[i % 2]
                        if 2 * step == w:
                            link(tt(dst[:, 16:528], src[:, 16:528], src[:, 16 - step:528 - step], ALU.add))
                        else:
                            link(nc.vector.memset(dst[:, 0:16], 0.0))
                            link(tt(dst[:, 16:528], src[:, 16:528], src[:, 16 - step:528 - step], ALU.add))
                        src = dst
                        step *= 2
                        i += 1
                    cn_ = cc("cnt")[:, 16 * m:16 * m + 16]
                    link(tt(src[:, 16:32], src[:, 16:32], cn_, ALU.mult))
                    link(ts(src[:, 32:528], src[:, 32:528], 1.0 / w, None, ALU.mult))
                    link(tt(PO[:, m, :], src[:, 16:528], u[:, 16:528], ALU.subtract), "pooled")
            if upon("pw"):
                dve.wait_ge(s["a_free"], FIRST_A["in2"] + 24)
                for m in range(8):
                    b = take()
                    link(tt(MG[:, m, :], b, GA[:, m, :], ALU.mult), "d_free")
            if upon("yb"):
                dve.wait_ge(s["a_free"], FIRST_A["in2"] + 24)
                for m in range(8):
                    b = take()
                    q = HN[:, 3, 512 * (m % 2):512 * (m % 2) + 512]
                    link(stt(q, b, vv("pool_scale", m), GB[:, m, :], ALU.mult, ALU.mult), "d_free")
                    link(tt(MG[:, m, :], MG[:, m, :], q, ALU.add), "merged")
            if upon("wout"):
                dve.wait_ge(s["in_row2"], 16)

                def r2(name):
                    return R2[:, ROW2[name][0]:ROW2[name][1]]
                link(tt(RW[:, 0:2048], RW[:, 0:2048], R2[:, 0:2048], ALU.add))
                for half in range(2):
                    sl = slice(512 * half, 512 * half + 512)
                    for t in range(NT):
                        b = take()
                        q = HN[:, t, sl]
                        link(tt(q, b, RW[:, sl], ALU.mult), "d_free")
                        link(stt(X[:, t, sl], X[:, t, sl], ALPHA, q, ALU.mult, ALU.add))
                for t in range(NT):
                    layer_rows("lnx", t, X[:, t, :], X[:, t, :], r2("ln1_g"), r2("ln1_b"))
            if upon("hT4"):
                for t in range(NT):
                    layer_rows("xn4", t, X[:, t, :], HN[:, t, :])
                turned(HT, lambda k: modc[:, 24 + k:25 + k], lambda k: modc[:, 16 + k:17 + k])
            if upon("up"):
                link(nc.vector.memset(UR[:, :, 0:2], 0.0), "upraw_used")

                def gated(j):
                    dve.wait_ge(s["ffgelu"], j + 1)
                    v_ = UC[:, 2 * (j % 2), :]
                    link(tt(FT[:, j, :], v_, UC[:, 2 * (j % 2) + 1, :], ALU.mult), "ff")
                for j in range(NF):
                    for i in range(2):
                        f = j + NF * i
                        q = 2 * (j % 2) + i
                        w = vv("w_ff")[:, 3 * f:3 * f + 3]
                        dve.wait_ge(s["a_free"], FIRST_A["up"] + 2 * j + i + 1)
                        u, o = UR[:, q, :], UC[:, q, :]
                        link(ts(o, u[:, 0:512], w[:, 0:1], vv("b_ff", f), ALU.mult, ALU.add))
                        link(stt(o, u[:, 1:513], w[:, 1:2], o, ALU.mult, ALU.add))
                        link(stt(o, u[:, 2:514], w[:, 2:3], o, ALU.mult, ALU.add), "upraw_used")
                        if i == 1:
                            tell(dve.nop(), "gelu_in")
                    if j >= 1:
                        gated(j - 1)
                gated(NF - 1)
            if upon("down"):
                for t in range(NT):
                    b = take()
                    link(tt(HN[:, t, 512:1024], b, RW[:, 1536:2048], ALU.mult), "d_free")
                dve.wait_ge(s["a_free"], FIRST_A["end"])
                for t in range(NT):
                    link(tt(HN[:, t, 0:512], HN[:, t, 0:512], RW[:, 1024:1536], ALU.mult))
                    link(stt(X[:, t, :], X[:, t, :], ALPHA, HN[:, t, :], ALU.mult, ALU.add))
                    layer_rows("fin", t, X[:, t, :], X[:, t, :], r2("ln2_g"), r2("ln2_b"))
            if dbg is not None:
                tell(dve.drain(), "fin")

        @block.gpsimd
        def _(pool):
            if upon("acc"):
                pool.wait_ge(s["a_full"], FIRST_A["ada"])

                for t in range(NT):
                    pool.wait_ge(s["idx"], t + 1)
                    for i in range(NSEL):
                        turn = NSEL * t + i
                        if turn == 4:
                            pool.wait_ge(s["peer_clear"], 1)
                        if turn >= RING:
                            pool.wait_ge(s["uv_used"], turn - RING + 1)
                        nc.gpsimd.indirect_dma_start(
                            UV[:, turn % RING, :], None, uv,
                            bass.IndirectOffsetOnAxis(ap=IDX[:, t % 2, i:i + 1], axis=0),
                        ).then_inc(uv_full[turn % RING], 16)


def kernel(**inputs):
    import numpy as _np
    import concourse.bacc as _bacc
    from concourse import mybir as _mybir
    from concourse.bass_utils import run_bass_kernel_spmd as _run

    def f(name):
        return _np.asarray(inputs[name])

    def cols(v):
        return _np.ascontiguousarray(_np.asarray(v).reshape(-1, P).T)

    def rows(*vs):
        return _np.ascontiguousarray(_np.broadcast_to(_np.concatenate([_np.asarray(v).reshape(-1) for v in vs])[None], (P, sum(_np.asarray(v).size for v in vs))))

    b_ada = f("b_ada_2")[0].reshape(6, D)
    w_conv = f("w_dw_a_2")[0].reshape(CONV_K, 4, P).transpose(2, 1, 0).reshape(P, 4 * CONV_K)
    w_ff = f("w_dw_f_2")[0].reshape(3, 44, P).transpose(2, 1, 0).reshape(P, 44 * 3)
    vec = _np.concatenate([
        cols(f("g_mix")[0]), cols(f("rwkv_mu")[0]), cols(f("g_cq")[0]), cols(f("g_ckv")[0]), cols(f("w0")[0]),
        cols(f("a0")[0]), cols(f("k_k")[0]), cols(f("k_a")[0]), cols(f("r_k")[0]), cols(f("c_2")[0]),
        cols(b_ada[0]), cols(b_ada[1]), cols(b_ada[3]), cols(b_ada[4]), w_conv, cols(f("b_dw_a_2")[0]),
        cols(f("ln_a_g_2")[0]), cols(f("ln_a_b_2")[0]), cols(f("pool_scale_2")[0]), w_ff,
        cols(f("b_dw_f_2")[0])], 1)
    lora = _np.concatenate([_np.concatenate([f("w2")[0], f("a2")[0]], 0), f("g2")[0]], 1)
    keys = f("sub_keys")[0].transpose(3, 0, 1, 2).reshape(P, 16 * NK)
    uv = _np.concatenate([f("expert_u")[0], f("expert_v")[0]], 1)
    w_up = f("w_up_2")[0].reshape(D, 2, NF, P).transpose(0, 2, 1, 3).reshape(D, 2 * D_FF)
    arrays = {
        "x": f("x")[0], "pos": _np.ascontiguousarray(f("positions")[0].reshape(NT, P).T), "cst": constants(),
        "vec": vec, "row1": rows(f("g_qnorm"), f("g_knorm"), f("g_attn_out"), f("ln_x_w"), f("ln_x_b")),
        "gffn": rows(f("g_ffn")),
        "row2": rows(b_ada[2], b_ada[5], f("ln1_g_2"), f("ln1_b_2"), f("ln2_g_2"), f("ln2_b_2")),
        "w_in": f("w_in")[0], "w_uq": f("w_uq")[0], "w_uk": f("w_uk")[0], "w_uv": f("w_uv")[0], "lora": lora,
        "w_o": f("w_o")[0], "w_pq": f("w_pq")[0], "keys": keys, "uv": uv, "w_ada": f("w_ada_2")[0],
        "w_in2": f("w_in_2")[0], "w_pw": f("w_pw_a_2")[0], "w_pool": f("w_pool_2")[0], "w_out": f("w_out_2")[0],
        "w_up": w_up, "w_down": f("w_down_2")[0],
    }
    nc = _bacc.Bacc("TRN2", target_bir_lowering=False, num_devices=1)
    arrays = {f"in_{k}": _np.ascontiguousarray(v) for k, v in arrays.items()}
    args = [nc.dram_tensor(k, v.shape, _mybir.dt.from_np(v.dtype), kind="ExternalInput").ap()
            for k, v in arrays.items()]
    out = nc.dram_tensor("out_0", (S, D), F32, kind="ExternalOutput").ap()
    build(nc, *args, out)
    r = _run(nc, [arrays], core_ids=[0])
    return r.results[0]["out_0"].reshape(1, S, D)
```

```python
from contextlib import ExitStack

import numpy as np

import concourse.bass as bass
from concourse import mybir

ALU = mybir.AluOpType
ACT = mybir.ActivationFunctionType
F32 = mybir.dt.float32
I32 = mybir.dt.int32
U32 = mybir.dt.uint32
AX = mybir.AxisListType.X

P = 128
S = 512
NT = S // P
D = 1024
KD = D // P
EPS = 1e-6
LN_EPS = 1e-5

H = 8
DQK = 96
DN = 64
DR = 32
HALF = DR // 2
QR = 384
KVR = 256
MLA_COLS = QR + KVR + DR
RD = 512
RM = RD // P
LN_X_EPS = 64e-5
KAPPA = float(np.exp(-0.5))
LEVELS = 7
NK = 128
TOPK = 16
NSEL = H * TOPK
RING = 8
GRP = 2
CONV_K = 31
POOL = (2, 4, 8, 16)
D_FF = 2816
NF = D_FF // P
ALPHA = 2.0 ** 0.25

ADA_EARLY = 4
TURNS = NSEL // RING
NORM_AT, TURN_AT = 2, 4
SELECT_AT = (3, 5, 7, 8, 10, 11, 13, 14)

CH = 4096
NWR = 3

JOBS = [
    ("hT", 4, 4), ("pm", 4, 4), ("cT", 3, 2), ("q", 4, 4), ("kv", 4, 4), ("qkT", 12, 8),
    ("att", 40, 64), ("pr", 2, 0), ("lora", 12, 0), ("kn", 0, 4), ("bonus", 0, 1),
    ("tok", 4, 8),
    ("inv0", 28, 48), ("inv1", 28, 48), ("chain", 12, 28),
    ("yT", 8, 4), ("wo", 4, 12), ("pq", 8, 8), ("s", 16, 0), ("ada", 8, 0),
    ("modc", 0, 1), ("acc", 8, 8), ("in2", 24, 4), ("ln", 0, 2), ("pw", 0, 8),
    ("yb", 0, 8), ("wout", 4, 12), ("up", 44, 0), ("down", 4, 4), ("end", 0, 0),
]
FIRST_A, FIRST_D = {}, {}
_a = _d = 0
for _name, _na, _nd in JOBS:
    FIRST_A[_name], FIRST_D[_name] = _a, _d
    _a, _d = _a + _na, _d + _nd


PR_EARLY, PR_IN_ATT = 4, 12


def pr_after(u):
    m = PR_EARLY + (u - 2) // 3
    return m if (u - 2) % 3 == 0 and PR_EARLY <= m < PR_IN_ATT else None


def unit_job(u):
    return FIRST_A["att"] + u + sum(pr_after(v) is not None for v in range(u))


def pr_job(m):
    if m < PR_EARLY:
        return FIRST_A["qkT"] + m
    return FIRST_A["att"] + 4 * (m - PR_EARLY) + 3 if m < PR_IN_ATT else FIRST_A["pr"] + m - PR_IN_ATT


def _cols(items):
    at, n = {}, 0
    for name, w in items:
        at[name] = (n, n + w)
        n += w
    return at, n


CONST, NCONST = _cols([("ident", P), ("ones", P), ("zero", P), ("lowrow", P), ("negrow", P),
                       ("level", LEVELS * P), ("strict", P), ("incl", P), ("heads", P), ("head2", 2),
                       ("invfreq", HALF), ("iota", TOPK), ("cnt", 4 * 16)])
VECS = [("g_mix", 8), ("mu", 14), ("g_cq", 3), ("g_ckv", 2), ("w0", 4), ("a0", 4), ("k_k", 4), ("k_a", 4),
        ("r_k", 4), ("c", 8), ("b_mod", 32), ("w_conv", 4 * CONV_K), ("b_conv", 4), ("ln_a_g", 4),
        ("ln_a_b", 4), ("pool_scale", 8), ("w_ff", 44 * 3), ("b_ff", 44)]
VEC, NVEC = _cols(VECS)
ROW1, NROW1 = _cols([("g_q", DQK), ("g_k", DQK), ("g_attn", RD), ("ln_x_w", RD), ("ln_x_b", RD)])
ROW2, NROW2 = _cols([("b_g1", D), ("b_g2", D), ("ln1_g", D), ("ln1_b", D), ("ln2_g", D), ("ln2_b", D)])


def constants():
    c = np.zeros((P, NCONST), np.float32)

    def put(name, v):
        a, b = CONST[name]
        c[:, a:b] = v

    i, j = np.arange(P)[:, None], np.arange(P)[None, :]
    put("ident", i == j)
    put("ones", 1.0)
    lev = [((j & (1 << l)) > 0) & ((i & (1 << l)) == 0) & ((i >> (l + 1)) == (j >> (l + 1)))
           for l in range(LEVELS)]
    put("level", np.concatenate(lev, 1))
    put("strict", i < j)
    put("incl", i <= j)
    put("heads", (i // 64) == (j // 64))
    put("head2", (i // 64) == np.arange(2)[None, :])
    put("lowrow", (j < 64) & (i == 0))
    put("negrow", np.where((j >= 64) & (i == 0), np.float32(-1e30), np.float32(0)))
    put("invfreq", (np.float32(10000.0) ** (-np.arange(HALF, dtype=np.float32) / np.float32(HALF)))[None, :])
    put("iota", np.arange(TOPK)[None, :])
    cnt = [1.0 / np.minimum(np.arange(16) + 1, w) for w in POOL]
    put("cnt", np.concatenate(cnt)[None, :])
    return c


def build(nc, x, pos, cst, vec, row1, gffn, row2, w_in, w_uq, w_uk, w_uv, lora, w_o, w_pq, keys, uv,
          w_ada, w_in2, w_pw, w_pool, w_out, w_up, w_down, out):
    with ExitStack() as ctx:
        def sb(name, shape, dt=F32):
            return ctx.enter_context(nc.sbuf_tensor(name, shape, dt))

        X = sb("X", [P, NT, D])
        HN = sb("HN", [P, NT, D])
        HT = sb("HT", [P, KD, S])
        WR = sb("WR", [P, NWR, CH])
        AR = sb("AR", [P, 22784])
        C = sb("C", [P, NCONST])
        V = sb("V", [P, NVEC])
        RW = sb("RW", [P, 2048])
        SC = sb("SC", [P, 1240])
        PA = ctx.enter_context(nc.psum_tensor("PA", [P, 4, 512], F32))
        PD = ctx.enter_context(nc.psum_tensor("PD", [P, 4, 512], F32))

        def cc(name):
            return C[:, CONST[name][0]:CONST[name][1]]

        def vv(name, m=None):
            a, b = VEC[name]
            return V[:, a:b] if m is None else V[:, a + m:a + m + 1]

        def r1(name):
            return RW[:, ROW1[name][0]:ROW1[name][1]]

        def ar(a, n, *dims):
            v = AR[:, a:a + n]
            if len(dims) == 1:
                return v.rearrange("p (a b) -> p a b", a=dims[0])
            if len(dims) == 2:
                return v.rearrange("p (a b c) -> p a b c", a=dims[0], b=dims[1])
            return v

        ident = cc("ident")
        LV = cc("level").rearrange("p (l n) -> p l n", l=LEVELS)

        names = ["a_full", "a_free", "d_full", "d_free", "dve", "act",
                 "in_x", "in_const", "in_gffn", "in_row2", "out_done",
                 "xn", "xn2", "xn3", "xn4",
                 "cn", "qk_normed", "smax", "probs", "raw_used", "lora_in", "prt",
                 "kx_sq", "rkk", "rexp", "rhat",
                 "ct", "x1t", "tmid", "ycomb",
                 "topk", "idx", "dots", "geluv", "diag", "uv_used", "csil",
                 "bufs", "conv", "convsq", "silu_in", "silu", "pooled", "merged",
                 "lnx", "upraw_used", "gelu_in", "gelu", "ff", "fin", "row2free",
                 "peer_clear", "sscan", "Lm", "ffgelu", "var", "rstd"]
        s = {}
        for nm in names:
            s[nm] = ctx.enter_context(nc.semaphore(nm))
        w_sem = [ctx.enter_context(nc.semaphore(f"w_slot{i}")) for i in range(NWR)]
        uv_full = [ctx.enter_context(nc.semaphore(f"uv_full{i}")) for i in range(RING)]
        n = {nm: 0 for nm in names}

        def tell(ins, name):
            n[name] += 1
            ins.then_inc(s[name], 1)


        QK = ar(0, 6144).rearrange("p (t g d) -> p t g d", t=NT, g=2 * H)
        QKT = ar(6144, 8192, 2 * H)
        VA = ar(14336, 2048, NT)
        CT = ar(16384, 2560, 5)
        PM = ar(18944, 2688, NT)
        PB = ar(18944, 1024, 2)
        PT = ar(19968, 1024, 2)
        RT, KT, VT, LT = (ar(2048 * i, 2048, 4) for i in range(4))
        SG, CS, AT, KK, GT, E1, E2 = (ar(2048 * i, 2048, 4) for i in range(4, 11))
        RAW = ar(16384, 4 * 513, 4)
        VTOK = HT[:, 0:4, :]
        KTOK, BTOK = SG, CS
        MT, CTL, XI, ZI = VT, LT, E1, E2

        def XT(h):
            return HT[:, 4 + h, :] if h < 4 else WR[:, 0, 512 * (h - 4):512 * (h - 4) + 512]

        MATS = [ar(4096, 3072).rearrange("p (m h n) -> p m h n", m=3, h=H),
                ar(18432, 3072).rearrange("p (m h n) -> p m h n", m=3, h=H)]
        FS = [ar(4096 + 3072, 1024, 2), ar(18432 + 3072, 1024, 2)]
        UV = AR[:, 0:RING * 2048].rearrange("p (r n) -> p r n", r=RING)
        QPT = ar(0, 8192, 16)
        SS = [HT[:, 0:4, :].rearrange("p a b -> p (a b)"), HT[:, 4:8, :].rearrange("p a b -> p (a b)"),
              ar(16384, 2048), ar(18432, 2048)]
        CAND = ar(20480, 2048)
        GF = ar(20480, 1024)
        SGA = ar(0, 2048, 4)
        PO = ar(0, 2048, 4)
        YAP = ar(2048, 4 * 542, 4)
        UP = ar(4216, 4 * 528, 4)
        CV = ar(6328, 2048, 4)
        GA = ar(8376, 4096, 8)
        GB = ar(12472, 4096, 8)
        R2 = ar(16600, NROW2)
        MG = HT
        EQ = VT
        SILU = ar(8192, 1024, 8)
        MODROW = ar(9216, 4096)
        FT = ar(0, NF * S, NF)
        HT4 = ar(11264, 4096, 8)
        UR = HN.rearrange("p a b -> p (a b)")[:, 0:4 * 514].rearrange("p (a b) -> p a b", a=4)
        UC = HT[:, 0:4, :]

        sc_at = [0]

        def small(w, dt=F32):
            a = sc_at[0]
            sc_at[0] += w
            assert sc_at[0] <= 1240, sc_at[0]
            v = SC[:, a:a + w]
            return v if dt is F32 else v.bitcast(dt)

        st_a = small(64)
        rsum = small(32)
        nmax = small(32)
        cosb = small(64)
        sinb = small(64)
        bon = small(32)
        fdec = small(16)
        modc = small(32)
        root = small(32)
        t_end = sc_at[0]
        posf = small(4)
        posi = small(4, I32)
        ang = small(64)
        kint = small(64)
        tmid = small(512)
        sc_at[0] = t_end
        s1v = small(256)
        i1u = small(256, U32)
        tpv = small(128)
        tpu = small(128, U32)
        gmx = small(24)
        lvl = C[:, CONST["level"][0]:CONST["level"][0] + 1280]
        DG = lvl[:, 0:1024].rearrange("p (r n) -> p r n", r=RING)
        GATE = lvl[:, 1024:1280].rearrange("p (r n) -> p r n", r=2)
        IDX = C[:, CONST["lowrow"][0]:CONST["negrow"][1]].rearrange("p (r n) -> p r n", r=2).bitcast(U32)
        DOT = small(8).rearrange("p (r n) -> p r n", r=4)
        GEL = small(8).rearrange("p (r n) -> p r n", r=4)
        csil2 = small(8)
        ffst = small(14 * NT)

        chunks = []

        def col_chunk(w, c0, w_cols, chan, job, k=KD):
            chunks.append((k * w_cols, w[:, c0:c0 + w_cols].rearrange("(k p) n -> p k n", p=P), k, chan, job))

        col_chunk(w_in, 0, 512, "a", FIRST_A["pm"] + 3)
        col_chunk(w_in, 512, 160, "d", FIRST_D["pm"] + 3)
        col_chunk(w_uq, 0, 768, "d", FIRST_D["q"] + 3, 3)
        chunks.append((1024, w_uk.rearrange("(k p) n -> p k n", p=P), 2, "d", FIRST_D["kv"] + 3))
        chunks.append((1024, w_uv.rearrange("(k p) n -> p k n", p=P), 2, "d", FIRST_D["kv"] + 3))
        for i, w in enumerate((512, 512, 512, 256)):
            col_chunk(w_in, MLA_COLS + 512 * i, w, "a", pr_job(min(4 * i + 3, 13)))
        chunks.append((1024, lora, 1, "a", FIRST_A["chain"] + 11))
        for i in range(ADA_EARLY):
            col_chunk(w_ada, 512 * i, 512, "a", FIRST_A["yT"] + i)
        for i in range(2):
            col_chunk(w_o, 512 * i, 512, "d", FIRST_D["wo"] + 8 + i)
        for i in range(4):
            col_chunk(w_pq, 512 * i, 512, "d", FIRST_D["pq"] + 2 * i + 1)
        chunks.append((2048, keys, 1, "a", FIRST_A["s"] + 15))
        for i in range(ADA_EARLY, 12):
            col_chunk(w_ada, 512 * i, 512, "a", FIRST_A["ada"] + i - ADA_EARLY)
        in2_order = [1, 0, 2, 3, 4, 5, 6]
        in2_last = [("a", 3), ("d", 3), ("a", 7), ("a", 11), ("a", 15), ("a", 19), ("a", 23)]
        for i, (ch, j) in zip(in2_order, in2_last):
            col_chunk(w_in2, 512 * i, 512, ch, (FIRST_A if ch == "a" else FIRST_D)["in2"] + j)
        chunks.append((4096, w_pw.rearrange("(k p) n -> p k n", p=P), 4, "d", FIRST_D["pw"] + 7))
        chunks.append((1024, w_pool.rearrange("g p n -> p g n"), 4, "d", FIRST_D["yb"] + 7))
        for i in range(2):
            col_chunk(w_out, 512 * i, 512, "d", FIRST_D["wout"] + 8 + i)
        for i in range(11):
            col_chunk(w_up, 512 * i, 512, "a", FIRST_A["up"] + 4 * i + 3)
        for i in range(6):
            k = min(4, NF - 4 * i)
            chunks.append((k * D, w_down[512 * i:512 * i + k * P, :].rearrange("(k p) n -> p k n", p=P), k, "down", i))
        s_down = ctx.enter_context(nc.semaphore("down_chunk"))
        CNUM = {}
        at = 0
        for nm, cnt in (("pm", 2), ("uq", 1), ("uk", 1), ("uv", 1), ("pr", 4), ("lora", 1), ("ada_early", ADA_EARLY),
                        ("wo", 2), ("pq", 4), ("keys", 1), ("ada", 12 - ADA_EARLY), ("in2", 7), ("pw", 1), ("pool", 1), ("wout", 2), ("up", 11),
                        ("down", 6)):
            CNUM[nm] = at
            at += cnt
        assert at == len(chunks)

        def chunk(pe, number, k=None):
            cols, _, kk, _, _ = chunks[number]
            pe.wait_ge(w_sem[number % NWR], 16 * (number // NWR + 1))
            return WR[:, number % NWR, 0:cols].rearrange("p (k n) -> p k n", k=k or kk)

        block = ctx.enter_context(nc.Block())

        @block.sync
        def _(sp):
            for t in range(NT):
                sp.dma_start(X[:, t, :], x[P * t:P * t + P, :]).then_inc(s["in_x"], 16)
            sp.dma_start(C[:, :], cst).then_inc(s["in_const"], 16)
            sp.dma_start(V[:, :], vec).then_inc(s["in_const"], 16)
            sp.dma_start(RW[:, 0:NROW1], row1).then_inc(s["in_const"], 16)
            sp.dma_start(posi[:, :], pos).then_inc(s["in_const"], 16)

            def load(i):
                cols, src, k, _, _ = chunks[i]
                if i >= NWR:
                    _, _, _, chan, job = chunks[i - NWR]
                    if chan == "down":
                        sp.wait_ge(s_down, job + 1)
                    else:
                        sp.wait_ge(s[chan + "_full"], job + 1)
                dst = WR[:, i % NWR, 0:cols]
                if len(src.shape) == 3:
                    dst = dst.rearrange("p (k n) -> p k n", k=k)
                sp.dma_start(dst, src).then_inc(w_sem[i % NWR], 16)

            for i in range(len(chunks)):
                load(i)
                if i == CNUM["pq"]:
                    sp.wait_ge(s["d_free"], FIRST_D["wo"])
                    sp.dma_start(GF, gffn).then_inc(s["in_gffn"], 16)
                if i == CNUM["wout"]:
                    sp.wait_ge(s["row2free"], 1)
                    sp.dma_start(R2, row2).then_inc(s["in_row2"], 16)
            for t in range(NT):
                sp.wait_ge(s["fin"], t + 1)
                sp.dma_start(out[P * t:P * t + P, :], X[:, t, :]).then_inc(s["out_done"], 16)
            sp.wait_ge(s["out_done"], 16 * NT)

        @block.tensor
        def _(pe):
            cnt = {"a": 0, "d": 0}

            def bank(chan):
                j = cnt[chan]
                cnt[chan] += 1
                if j >= 4:
                    pe.wait_ge(s[chan + "_free"], j - 3)
                return (PA if chan == "a" else PD)[:, j % 4, :]

            def full(chan, ins):
                ins.then_inc(s[chan + "_full"], 1)

            def transposes(chan, srcs, rows=P, cols=P):
                b = bank(chan)
                for i, src in enumerate(srcs):
                    ins = nc.tensor.transpose(b[0:cols, rows * i:rows * i + rows], src, ident[0:rows, 0:rows])
                full(chan, ins)

            def product(chan, pairs, w=512, rows=P):
                b = bank(chan)[0:rows, 0:w]
                for i, (lhsT, rhs) in enumerate(pairs):
                    ins = nc.tensor.matmul(b, lhsT, rhs, start=(i == 0), stop=(i == len(pairs) - 1))
                full(chan, ins)

            def turn_block(ready, t, chans):
                pe.wait_ge(s[ready], t + 1)
                for i in range(2):
                    transposes(chans[i], [HN[:, t, P * k:P * k + P] for k in range(4 * i, 4 * i + 4)])

            def turn(ready, count=1):
                for k in range(KD):
                    if k == 0:
                        pe.wait_ge(s[ready], NT * count)
                    transposes("ad"[k % 2], [HN[:, t, P * k:P * k + P] for t in range(NT)])

            pe.wait_ge(s["in_const"], 64)
            turn("xn")

            pe.wait_ge(s["a_free"], FIRST_A["pm"])
            pe.wait_ge(s["d_free"], FIRST_D["pm"])
            w0_, w1_ = chunk(pe, 0), chunk(pe, 1)
            for t in range(NT):
                product("a", [(HT[:, k, P * t:P * t + P], w0_[:, k, :]) for k in range(KD)])
            for t in range(NT):
                product("d", [(HT[:, k, P * t:P * t + P], w1_[:, k, :]) for k in range(KD)], 160)
            pe.wait_ge(s["cn"], NT)
            for g in range(5):
                transposes("ad"[g % 2], [PM[:, t, P * g:P * g + P] for t in range(NT)])
            pe.wait_ge(s["a_free"], FIRST_A["q"])
            pe.wait_ge(s["d_free"], FIRST_D["q"])
            uq = chunk(pe, CNUM["uq"])
            for t in range(NT):
                for half in range(2):
                    product("ad"[half], [(CT[:, k, P * t:P * t + P], uq[:, k, 384 * half:384 * half + 384])
                                         for k in range(3)], 384)
            uk, uvw = chunk(pe, CNUM["uk"]), chunk(pe, CNUM["uv"])
            for t in range(NT):
                product("a", [(CT[:, 3 + k, P * t:P * t + P], uk[:, k, :]) for k in range(2)])
                product("d", [(CT[:, 3 + k, P * t:P * t + P], uvw[:, k, :]) for k in range(2)])
            def projection(m):
                w = chunk(pe, CNUM["pr"] + m // 4)
                product("a", [(w[:, k, P * (m % 4):P * (m % 4) + P], HT[:, k, :]) for k in range(KD)])

            for m in range(PR_EARLY):
                projection(m)
            pe.wait_ge(s["qk_normed"], NT)
            for g in range(2 * H):
                transposes("ad"[g % 2], [QK[:, t, g, :] for t in range(NT)], P, DQK)
            pe.wait_ge(s["a_free"], FIRST_A["att"])
            pe.wait_ge(s["d_free"], FIRST_D["att"])
            units = [(t, h) for t in range(NT) for h in range(H)]
            for u in range(len(units) + 2):
                if u < len(units):
                    t, h = units[u]
                    nk = P * (t + 1)
                    b = bank("a")
                    nc.tensor.matmul(b[:, 0:nk], QKT[0:DQK, h, P * t:P * t + P], QKT[0:DQK, H + h, 0:nk],
                                     start=True, stop=False)
                    full("a", nc.tensor.matmul(b[:, nk - P:nk], cc("lowrow")[0:1, :], cc("negrow")[0:1, :],
                                               start=False, stop=True))
                if 1 <= u <= len(units):
                    t, h = units[u - 1]
                    pe.wait_ge(s["probs"], u)
                    transposes("d", [PB[:, (u - 1) % 2, P * j:P * j + P] for j in range(t + 1)])
                if u >= 2:
                    t, h = units[u - 2]
                    pe.wait_ge(s["d_free"], FIRST_D["att"] + (1 if u == 2 else 2 * (u - 2)))
                    product("d", [(PT[:, (u - 2) % 2, P * j:P * j + P], VA[:, j, 64 * h:64 * h + 64])
                                  for j in range(t + 1)], 64)
                if pr_after(u) is not None:
                    projection(pr_after(u))
            for m in range(PR_IN_ATT, 14):
                projection(m)
            lw = chunk(pe, CNUM["lora"], 1)[:, 0, :]
            pe.wait_ge(s["lora_in"], 2)
            pe.wait_ge(s["prt"], 14)
            for m in range(4):
                product("a", [(lw[0:64, P * m:P * m + P], LT[0:64, 2, :])])
            for m in range(4):
                product("a", [(lw[64:128, P * m:P * m + P], LT[64:128, 0, :])])
            for t in range(NT):
                product("a", [(LT[:, 3, P * t:P * t + P], lw[:, 512:1024])])
            for m in range(4):
                pe.wait_ge(s["kx_sq"], m + 1)
                product("d", [(cc("heads"), E1[:, m, :])])
            pe.wait_ge(s["rkk"], 1)
            b = bank("d")
            for t in range(NT):
                for m in range(4):
                    o = 8 * t + 2 * m
                    ins = nc.tensor.matmul(b[:, o:o + 2], E1[:, m, P * t:P * t + P], cc("head2"),
                                           start=True, stop=True)
            full("d", ins)
            for t in range(NT):
                transposes("d", [VT[:, m, P * t:P * t + P] for m in range(4)])
            pe.wait_ge(s["rhat"], 4)
            for t in range(NT):
                transposes("a", [KT[:, m, P * t:P * t + P] for m in range(4)])
                transposes("d", [AT[:, m, P * t:P * t + P] for m in range(4)])
            for grp in range(2):
                fa, fd = FIRST_A[f"inv{grp}"], FIRST_D[f"inv{grp}"]
                if grp == 0:
                    pe.wait_ge(s["a_free"], fa)
                    pe.wait_ge(s["d_free"], fd)
                for q in range(4):
                    h = 4 * grp + q
                    o = 64 * (h % 2)
                    b = bank("d")
                    for c in range(NT):
                        sl = slice(P * c, P * c + P)
                        ins = nc.tensor.matmul(b[:, sl], AT[o:o + 64, h // 2, sl], KK[o:o + 64, h // 2, sl],
                                               start=True, stop=True)
                    full("d", ins)
                for q in range(4):
                    pe.wait_ge(s["x1t"], 4 * grp + q + 1)
                    transposes("a", [XT(4 * grp + q)[:, P * c:P * c + P] for c in range(NT)])
                for lev in range(1, LEVELS):
                    last = lev == LEVELS - 1
                    for q in range(4):
                        if lev == 1:
                            pe.wait_ge(s["a_free"], fa + q + 1)
                        else:
                            pe.wait_ge(s["d_free"], fd + 4 + 8 * (lev - 2) + 2 * q + 2)
                        pe.wait_ge(s["ct"], 24 * grp + 4 * (lev - 1) + q + 1)
                        b = bank("a")
                        for c in range(NT):
                            sl = slice(P * c, P * c + P)
                            ins = nc.tensor.matmul(b[:, sl], CTL[:, q, sl], XI[:, q, sl], start=True, stop=True)
                        full("a", ins)
                    for q in range(4):
                        xt = XT(4 * grp + q)
                        pe.wait_ge(s["a_free"], fa + 4 * lev + q + 1)
                        b = bank("d")
                        for c in range(NT):
                            sl = slice(P * c, P * c + P)
                            ins = nc.tensor.matmul(b[:, sl], ZI[:, q, sl], xt[:, sl], start=True, stop=True)
                        full("d", ins)
                        if not last:
                            b = bank("d")
                            for c in range(NT):
                                sl = slice(P * c, P * c + P)
                                ins = nc.tensor.matmul(b[:, sl], xt[:, sl], ZI[:, q, sl], start=True, stop=True)
                            full("d", ins)
            fa, fd = FIRST_A["chain"], FIRST_D["chain"]

            def matrices(c):
                sl = slice(P * c, P * c + P)
                for left, right in ((KT, KK), (KT, RT), (AT, RT)):
                    for odd in range(2):
                        b = bank("d")
                        o = 64 * odd
                        for q in range(4):
                            ins = nc.tensor.matmul(b[:, P * q:P * q + P], left[o:o + 64, q, sl],
                                                   right[o:o + 64, q, sl], start=True, stop=True)
                        full("d", ins)

            matrices(0)
            pe.wait_ge(s["d_free"], fd)
            pe.wait_ge(s["tmid"], 1)
            for c in range(NT):
                sl = slice(P * c, P * c + P)
                mat, f_, sk_ = MATS[c % 2], FS[c % 2][:, 0, :], FS[c % 2][:, 1, :]
                heads = [(h, slice(64 * h, 64 * h + 64)) for h in range(H)]
                pe.wait_ge(s["d_free"], fd + 7 * c + 6)
                b = bank("a")
                for h, hv in heads:
                    nc.tensor.matmul(b[:, hv], KK[:, h // 2, sl], tmid[:, hv], start=True, stop=False)
                    ins = nc.tensor.matmul(b[:, hv], mat[:, 0, h, :], VTOK[:, c, hv], start=False, stop=True)
                full("a", ins)
                if c + 1 < NT:
                    matrices(c + 1)
                pe.wait_ge(s["a_free"], fa + 3 * c + 1)
                b = bank("a")
                for h, hv in heads:
                    ins = nc.tensor.matmul(b[:, hv], XT(h)[:, sl], f_[:, hv], start=True, stop=True)
                full("a", ins)
                pe.wait_ge(s["a_free"], fa + 3 * c + 2)
                b = bank("d")
                for pr in range(4):
                    f2 = slice(P * pr, P * pr + P)
                    nc.tensor.matmul(b[:, f2], ident, tmid[:, f2], start=True, stop=False)
                    nc.tensor.matmul(b[:, f2], KTOK[:, c, f2], VTOK[:, c, f2], start=False, stop=False)
                    ins = nc.tensor.matmul(b[:, f2], BTOK[:, c, f2], sk_[:, f2], start=False, stop=True)
                full("d", ins)
                b = bank("a")
                for h, hv in heads:
                    nc.tensor.matmul(b[:, hv], RT[:, h // 2, sl], tmid[:, hv], start=True, stop=False)
                    nc.tensor.matmul(b[:, hv], mat[:, 1, h, :], VTOK[:, c, hv], start=False, stop=False)
                    ins = nc.tensor.matmul(b[:, hv], mat[:, 2, h, :], sk_[:, hv], start=False, stop=True)
                full("a", ins)
            def modulation(w):
                product("a", [(SILU[:, k, :], w[:, k, :]) for k in range(KD)])

            pe.wait_ge(s["csil"], 8)
            for i in range(ADA_EARLY):
                modulation(chunk(pe, CNUM["ada_early"] + i))
            pe.wait_ge(s["ycomb"], NT)
            for t in range(NT):
                turn_block("ycomb", t, "ad")
            pe.wait_ge(s["a_free"], FIRST_A["wo"])
            pe.wait_ge(s["d_free"], FIRST_D["wo"])
            w = [chunk(pe, CNUM["wo"] + half) for half in range(2)]
            for t in range(NT):
                for half in range(2):
                    product("d", [(HT[:, k, P * t:P * t + P], w[half][:, k, :]) for k in range(KD)])
                if t >= 1:
                    turn_block("xn2", t - 1, "ad")
            turn_block("xn2", NT - 1, "ad")
            pe.wait_ge(s["a_free"], FIRST_A["pq"])
            pe.wait_ge(s["d_free"], FIRST_D["pq"])
            for m in range(16):
                w = chunk(pe, CNUM["pq"] + m // 4)
                product("ad"[m % 2], [(w[:, k, P * (m % 4):P * (m % 4) + P], HT[:, k, :]) for k in range(KD)])
            pe.wait_ge(s["a_free"], FIRST_A["s"])
            pe.wait_ge(s["d_free"], FIRST_D["ada"])
            kw = chunk(pe, CNUM["keys"], 16)
            for t in range(NT):
                for g4 in range(4):
                    b = bank("a")
                    for i in range(4):
                        g = 4 * g4 + i
                        ins = nc.tensor.matmul(b[:, P * i:P * i + P], QPT[:, g, P * t:P * t + P], kw[:, g, :],
                                               start=True, stop=True)
                    full("a", ins)
            for i in range(ADA_EARLY, 12):
                modulation(chunk(pe, CNUM["ada"] + i - ADA_EARLY))
            pe.wait_ge(s["a_free"], FIRST_A["acc"])
            b = bank("d")
            for i in range(32):
                ins = nc.tensor.matmul(b[:, i:i + 1], MODROW[0:1, P * i:P * i + P], cc("ones")[0:1, 0:1],
                                       start=True, stop=True)
            full("d", ins)
            fours = cc("ones")[0:1, :].unsqueeze(1).broadcast_to([1, 4, P])
            for t in range(NT):
                acc = [bank("d"), bank("d")]
                for half in range(2):
                    nc.tensor.matmul(acc[half], cc("zero")[0:1, :], fours, start=True, stop=False)
                for first, last in ((0, TURN_AT), (TURN_AT, TURNS)):
                    if first > 0 and t > 0:
                        turn_block("xn3", t - 1, "aa")
                    with pe.Fori(first, last) as it:
                        for j in range(RING):
                            pe.wait_ge(s["diag"], it * RING + (NSEL * t + j + 1))
                            for half in range(2):
                                ins = nc.tensor.matmul(acc[half], DG[:, j, :],
                                                       UV[:, j, D + 512 * half:D + 512 * half + 512],
                                                       start=False, stop=False)
                            ins.then_inc(s["uv_used"], 1)
                for half in range(2):
                    full("d", nc.tensor.matmul(acc[half], cc("zero")[0:1, :], fours, start=False,
                                               stop=True))
            turn_block("xn3", NT - 1, "aa")
            pe.wait_ge(s["a_free"], FIRST_A["in2"])
            pe.wait_ge(s["d_free"], FIRST_D["in2"])
            for i in range(7):
                w = chunk(pe, CNUM["in2"] + i)
                for m in range(4):
                    product("d" if i == 1 else "a",
                            [(w[:, k, P * m:P * m + P], HT[:, k, :]) for k in range(KD)])
            pe.wait_ge(s["conv"], 4)
            product("d", [(cc("ones"), CV[:, m, :]) for m in range(4)])
            pe.wait_ge(s["convsq"], 4)
            product("d", [(cc("ones"), HN[:, m, 0:512]) for m in range(4)])
            pe.wait_ge(s["silu"], 4)
            w = chunk(pe, CNUM["pw"])
            for m in range(8):
                product("d", [(w[:, k, P * m:P * m + P], CV[:, k, :]) for k in range(4)])
            w = chunk(pe, CNUM["pool"])
            pe.wait_ge(s["pooled"], 4)
            for m in range(8):
                product("d", [(w[:, m // 2, P * (m % 2):P * (m % 2) + P], PO[:, m // 2, :])])
            pe.wait_ge(s["merged"], 8)
            w = [chunk(pe, CNUM["wout"] + half) for half in range(2)]
            for t in range(NT):
                for half in range(2):
                    product("d", [(MG[:, k, P * t:P * t + P], w[half][:, k, :]) for k in range(KD)])
                if t >= 1:
                    turn_block("xn4", t - 1, "ad")
            turn_block("xn4", NT - 1, "ad")
            pe.wait_ge(s["a_free"], FIRST_A["up"])
            pe.wait_ge(s["d_free"], FIRST_D["up"])
            for i in range(11):
                w = chunk(pe, CNUM["up"] + i)
                for m in range(4):
                    product("a", [(w[:, k, P * m:P * m + P], HT4[:, k, :]) for k in range(KD)])
            banks = [[bank("a") for _ in range(NT)], [bank("d") for _ in range(NT)]]

            def down(w, i, kk, t):
                k = 4 * i + kk
                for half in range(2):
                    ins = nc.tensor.matmul(banks[half][t], FT[:, k, P * t:P * t + P],
                                           w[:, kk, 512 * half:512 * half + 512],
                                           start=(k == 0), stop=(k == NF - 1))
                    if k == NF - 1:
                        full("ad"[half], ins)

            for i in range(3):
                w = chunk(pe, CNUM["down"] + i)
                for kk in range(4):
                    pe.wait_ge(s["ff"], 4 * i + kk + 1)
                    for t in range(NT):
                        down(w, i, kk, t)
                pe.drain().then_inc(s_down, 1)
            w = [chunk(pe, CNUM["down"] + i) for i in range(3, 6)]
            pe.wait_ge(s["ff"], NF)
            for t in range(NT):
                for i in range(3, 6):
                    for kk in range(w[i - 3].shape[1]):
                        down(w[i - 3], i, kk, t)

        @block.scalar
        def _(act):
            A = nc.scalar.activation

            def take():
                j = n["a_free"]
                act.wait_ge(s["a_full"], j + 1)
                return PA[:, j % 4, :]

            def link():
                act.wait_ge(s["act"], n["act"])

            def turned(dst, scale=None, bias=None):
                for k in range(0, KD, 2):
                    tell(A(dst[:, k, :], take(), ACT.Identity, scale=scale(k) if scale else 1.0,
                           bias=bias(k) if bias else 0.0), "a_free")

            def turned_block(dst, t, k0, scale=None, bias=None):
                b = take()
                if scale is None:
                    tell(nc.scalar.copy(dst[:, k0:k0 + 4, P * t:P * t + P],
                                        b.rearrange("p (k n) -> p k n", k=4)), "a_free")
                    return
                for i in range(4):
                    k = k0 + i
                    tell(A(dst[:, k, P * t:P * t + P], b[:, P * i:P * i + P], ACT.Identity, scale=scale(k),
                           bias=bias(k)), "a_free" if i == 3 else "act")

            def roots(*tiles):
                for v in tiles:
                    act.wait_ge(s["var"], n["rstd"] + 1)
                    tell(A(v, v, ACT.Sqrt), "rstd")

            def ffv(t):
                return ffst[:, 14 * t + 13:14 * t + 14]

            roots(st_a[:, 0:4])
            act.wait_ge(s["in_const"], 64)
            turned(HT, lambda k: vv("g_mix", k))
            for t in range(NT):
                tell(nc.scalar.copy(PM[:, t, 0:512], take()), "a_free")
            act.wait_ge(s["sscan"], 1)
            tell(A(sinb[:, :], ang[:, :], ACT.Sin), "act")
            act.wait_ge(s["sscan"], 2)
            tell(A(cosb[:, :], kint[:, :], ACT.Sin), "act")
            roots(st_a[:, 8:16])
            for g in (0, 2, 4):
                sc_ = vv("g_cq", g) if g < 3 else vv("g_ckv", g - 3)
                tell(A(CT[:, g, :], take(), ACT.Copy, scale=sc_), "a_free")
            for t in range(NT):
                tell(nc.scalar.copy(QK[:, t, 0:4, :].rearrange("p g d -> p (g d)"), take()[:, 0:384]), "a_free")
            for t in range(NT):
                tell(nc.scalar.copy(QK[:, t, H:2 * H, 0:DN], take().rearrange("p (h d) -> p h d", h=H)), "a_free")
            def raw(m):
                b = take()
                if m == 0:
                    act.wait_ge(s["raw_used"], 1)
                if m >= 4:
                    act.wait_ge(s["raw_used"], m - 2)
                tell(nc.scalar.copy(RAW[:, m % 4, 1:513], b), "a_free")

            for t in range(NT):
                roots(st_a[:, 16:32])
                raw(t)
            for g in range(0, 2 * H, 2):
                tell(nc.scalar.copy(QKT[0:DQK, g, :], take()[0:DQK, :]), "a_free")
            u = 0
            for t in range(NT):
                for h in range(H):
                    b = take()
                    nk = P * (t + 1)
                    act.wait_ge(s["smax"], u + 1)
                    if u >= 2:
                        act.wait_ge(s["d_full"], FIRST_D["att"] + (1 if u == 2 else 2 * u - 4))
                    tell(A(PB[:, u % 2, 0:nk], b[:, 0:nk], ACT.Exp, bias=nmax[:, u:u + 1], scale=DQK ** -0.5,
                           accum_out=rsum[:, u:u + 1]), "probs")
                    act.wait_ge(s["probs"], u + 1)
                    tell(nc.scalar.copy(st_a[:, 63:64], rsum[:, u:u + 1]), "a_free")
                    if pr_after(u) is not None:
                        raw(pr_after(u))
                    u += 1
            for m in range(PR_IN_ATT, 14):
                raw(m)
            act.wait_ge(s["prt"], 14)
            tell(A(LT[0:64, 2, :], LT[0:64, 0, :], ACT.Tanh), "lora_in")
            tell(A(LT[:, 3, :], LT[:, 1, :], ACT.Sigmoid), "lora_in")
            for m in range(4):
                tell(A(SG[:, m, :], take(), ACT.Sigmoid, bias=vv("w0", m)), "a_free")
            for m in range(4):
                tell(A(AT[:, m, :], take(), ACT.Sigmoid, bias=vv("a0", m)), "a_free")
            for t in range(NT):
                tell(nc.scalar.copy(GT[:, t, :], take()), "a_free")
            roots(*[E2[:, m, :] for m in range(4)])
            act.wait_ge(s["Lm"], 1)
            tell(A(fdec[:, :], fdec[:, :], ACT.Exp, scale=-KAPPA), "rexp")
            act.wait_ge(s["Lm"], 2)
            act.wait_ge(s["d_full"], FIRST_D["tok"])
            tell(A(E1[:, :, :], CS[:, :, :], ACT.Exp, scale=-KAPPA), "rexp")
            tell(A(E2[:, :, :], CS[:, :, :], ACT.Exp, scale=KAPPA), "rexp")
            act.wait_ge(s["Lm"], 3)
            act.wait_ge(s["d_full"], FIRST_D["tok"] + 4)
            tell(A(EQ[:, :, :], SG[:, :, :], ACT.Exp, scale=-KAPPA), "rexp")
            act.wait_ge(s["rexp"], n["rexp"])
            for t in range(NT):
                tell(nc.scalar.copy(KTOK[:, t, :], take()), "a_free")
            for grp in range(2):
                for q in range(4):
                    tell(nc.scalar.copy(XI[:, q, :], take()), "a_free")
                for lev in range(1, LEVELS):
                    for q in range(4):
                        b = take()
                        if lev > 1:
                            act.wait_ge(s["d_full"], FIRST_D[f"inv{grp}"] + 4 + 8 * (lev - 2) + 2 * q + 2)
                        tell(nc.scalar.copy(ZI[:, q, :], b), "a_free")
            for c in range(NT):
                for dst in (FS[c % 2][:, 0, :], FS[c % 2][:, 1, :], HN[:, c, 512:1024]):
                    tell(nc.scalar.copy(dst, take()), "a_free")
                roots(st_a[:, 16:24])
                if c > 0:
                    roots(st_a[:, 16:24])
            tell(A(csil2, vv("c"), ACT.Silu), "act")
            link()
            for k in range(KD):
                tell(A(SILU[:, k, :], cc("ones"), ACT.Copy, scale=csil2[:, k:k + 1]), "csil")
            roots(st_a[:, 16:24])

            def modulation(i):
                b = take()
                if i // 2 in (2, 5):
                    g = (0 if i < 6 else 1024) + 512 * (i % 2)
                    tell(nc.scalar.copy(RW[:, g:g + 512], b), "a_free")
                else:
                    r = i if i < 4 else i - 2
                    tell(nc.scalar.copy(MODROW[0:1, 512 * r:512 * r + 512], b[0:1, :]), "a_free")

            for i in range(ADA_EARLY):
                modulation(i)
            for t in range(NT):
                turned_block(HT, t, 0)
            for t in range(NT + 1):
                if t < NT:
                    roots(st_a[:, t:t + 1])
                if t >= 1:
                    turned_block(HT, t - 1, 0)
            for m in range(0, 16, 2):
                tell(nc.scalar.copy(QPT[:, m, :], take()), "a_free")
            for t in range(NT):
                for g4 in range(4):
                    tell(nc.scalar.copy(SS[t][:, 512 * g4:512 * g4 + 512], take()), "a_free")
            for i in range(ADA_EARLY, 12):
                modulation(i)
            def gate_exp(t):
                act.wait_ge(s["topk"], t + 1)
                tell(A(GATE[:, t % 2, :], GATE[:, t % 2, :], ACT.Exp), "geluv")

            def turned_both(t):
                for k0 in (0, 4):
                    turned_block(HT, t, k0, lambda k: modc[:, 8 + k:9 + k], lambda k: modc[:, k:k + 1])

            for t in range(NT):
                gate_exp(t)
                for first, last in ((0, NORM_AT), (NORM_AT, TURN_AT), (TURN_AT, TURNS)):
                    if first == NORM_AT and t > 0:
                        roots(ffv(t - 1))
                    if first == TURN_AT and t > 0:
                        turned_both(t - 1)
                    with act.Fori(first, last) as it:
                        for g in range(RING // GRP):
                            act.wait_ge(s["dots"], it * RING + (NSEL * t + GRP * (g + 1)))
                            A(GEL[:, g, :], DOT[:, g, :], ACT.Gelu).then_inc(s["gelu"], 1)
            roots(ffv(NT - 1))
            turned_both(NT - 1)
            for m in range(4):
                tell(A(SGA[:, m, :], take(), ACT.Sigmoid), "a_free")
            for m in range(4):
                tell(nc.scalar.copy(UP[:, m, 16:528], take()), "a_free")
            for m in range(8):
                tell(A(GA[:, m, :], take(), ACT.Sigmoid), "a_free")
            for m in range(8):
                tell(A(GB[:, m, :], take(), ACT.Sigmoid), "a_free")
            roots(HN[:, 0, 512:1024])
            for m in range(4):
                act.wait_ge(s["silu_in"], m + 1)
                tell(A(CV[:, m, :], CV[:, m, :], ACT.Silu, scale=vv("ln_a_g", m), bias=vv("ln_a_b", m)), "silu")
            for t in range(NT + 1):
                if t < NT:
                    roots(ffv(t), ffv(t))
                if t >= 1:
                    turned_block(HT4, t - 1, 0, lambda k: modc[:, 24 + k:25 + k], lambda k: modc[:, 16 + k:17 + k])
            for j in range(NF):
                for i in range(2):
                    b = take()
                    q = 2 * (j % 2) + i
                    act.wait_ge(s["upraw_used"], max(1, 2 * (j - 2) + i + 2))
                    tell(nc.scalar.copy(UR[:, q, 2:514], b), "a_free")
                if j >= 1:
                    act.wait_ge(s["gelu_in"], j)
                    tell(A(UC[:, 2 * ((j - 1) % 2) + 1, :], UC[:, 2 * ((j - 1) % 2) + 1, :],
                           ACT.Gelu_apprx_tanh), "ffgelu")
            act.wait_ge(s["gelu_in"], NF)
            tell(A(UC[:, 2 * ((NF - 1) % 2) + 1, :], UC[:, 2 * ((NF - 1) % 2) + 1, :],
                   ACT.Gelu_apprx_tanh), "ffgelu")
            for t in range(NT):
                tell(nc.scalar.copy(HN[:, t, 0:512], take()), "a_free")
                roots(ffv(t))

        @block.vector
        def _(dve):
            tt, ts, stt = nc.vector.tensor_tensor, nc.vector.tensor_scalar, nc.vector.scalar_tensor_tensor
            ttr = nc.vector.tensor_tensor_reduce

            def take():
                j = n["d_free"]
                dve.wait_ge(s["d_full"], j + 1)
                return PD[:, j % 4, :]

            def link(ins=None, name="dve"):
                if ins is not None:
                    tell(ins, name)
                dve.wait_ge(s[name], n[name])

            def rstd(dst, scale, eps):
                w = dst.shape[-1]
                r_, v_ = root[:, 0:w], root[:, 16:16 + w]
                link(ts(v_, dst, scale, eps, ALU.mult, ALU.add))
                tell(nc.vector.tensor_copy(dst, v_), "var")
                dve.wait_ge(s["rstd"], n["var"])
                link(nc.vector.reciprocal(r_, dst))
                link(tt(v_, v_, r_, ALU.mult))
                link(stt(v_, v_, -0.5, r_, ALU.mult, ALU.mult))
                link(stt(dst, v_, 1.5, r_, ALU.add, ALU.mult))

            def turned_block(dst, t, scale=None, bias=None):
                b = take()
                if scale is None:
                    tell(nc.vector.tensor_copy(dst[:, 4:8, P * t:P * t + P],
                                               b.rearrange("p (k n) -> p k n", k=4)), "d_free")
                    return
                for k in range(4, 8):
                    tell(ts(dst[:, k, P * t:P * t + P], b[:, P * (k - 4):P * (k - 4) + P], scale(k), bias(k),
                            ALU.mult, ALU.add), "d_free" if k == 7 else "dve")

            def turned(dst, scale=None, bias=None):
                for k in range(1, KD, 2):
                    b = take()
                    if bias:
                        tell(ts(dst[:, k, :], b, scale(k), bias(k), ALU.mult, ALU.add), "d_free")
                    elif scale:
                        tell(ts(dst[:, k, :], b, scale(k), None, ALU.mult), "d_free")
                    else:
                        tell(nc.vector.tensor_copy(dst[:, k, :], b), "d_free")

            def rms_rows(ready):
                for t in range(NT):
                    link(ttr(HN[:, t, :], X[:, t, :], X[:, t, :], 1.0, 0.0, ALU.mult, ALU.add, st_a[:, t:t + 1]))
                rstd(st_a[:, 0:NT], 1.0 / D, EPS)
                for t in range(NT):
                    tell(ts(HN[:, t, :], X[:, t, :], st_a[:, t:t + 1], None, ALU.mult), ready)

            def rms_row(ready, t, gain):
                link(ttr(HN[:, t, :], X[:, t, :], X[:, t, :], 1.0, 0.0, ALU.mult, ALU.add, st_a[:, t:t + 1]))
                rstd(st_a[:, t:t + 1], 1.0 / D, EPS)
                tell(stt(HN[:, t, :], X[:, t, :], st_a[:, t:t + 1], gain, ALU.mult, ALU.mult), ready)

            dve.wait_ge(s["in_x"], 64)
            rms_rows("xn")
            dve.wait_ge(s["in_const"], 64)
            TWO_PI = [6.28125, 0.0019350051879882812, 3.0199159819567e-07]
            MAGIC = 12582912.0
            link(nc.vector.tensor_copy(posf[:, :], posi[:, :]))
            a3 = ang.rearrange("p (t i) -> p t i", t=NT)
            k3 = kint.rearrange("p (t i) -> p t i", t=NT)
            link(tt(a3, posf.unsqueeze(2).broadcast_to([P, NT, HALF]),
                    cc("invfreq").unsqueeze(1).broadcast_to([P, NT, HALF]), ALU.mult))
            link(ts(kint[:, :], ang[:, :], 1.0 / (2 * np.pi), 0.25, ALU.mult, ALU.add))
            link(ts(kint[:, :], kint[:, :], MAGIC, -MAGIC, ALU.add, ALU.add))
            link(stt(cosb[:, :], kint[:, :], -TWO_PI[0], ang[:, :], ALU.mult, ALU.add))
            link(stt(cosb[:, :], kint[:, :], -TWO_PI[1], cosb[:, :], ALU.mult, ALU.add))
            link(stt(cosb[:, :], kint[:, :], -TWO_PI[2], cosb[:, :], ALU.mult, ALU.add))
            link(ts(cosb[:, :], cosb[:, :], np.pi / 2, 3.1415925, ALU.add, ALU.min))
            link(ts(cosb[:, :], cosb[:, :], -3.1415925, None, ALU.max))
            link(ts(sinb[:, :], ang[:, :], 1.0 / (2 * np.pi), None, ALU.mult))
            link(ts(sinb[:, :], sinb[:, :], MAGIC, -MAGIC, ALU.add, ALU.add))
            for c_ in TWO_PI:
                link(stt(ang[:, :], sinb[:, :], -c_, ang[:, :], ALU.mult, ALU.add))
            link(ts(ang[:, :], ang[:, :], 3.1415925, -3.1415925, ALU.min, ALU.max), "sscan")
            link(nc.vector.tensor_copy(kint[:, :], cosb[:, :]), "sscan")
            turned(HT, lambda k: vv("g_mix", k))
            for t in range(NT):
                tell(nc.vector.tensor_copy(PM[:, t, 512:672], take()[:, 0:160]), "d_free")
            dve.wait_ge(s["a_free"], FIRST_A["cT"])
            dve.wait_ge(s["d_free"], n["d_free"])
            TMP = HN[:, 0:2, :].rearrange("p a b -> p (a b)")
            dve.wait_ge(s["a_full"], FIRST_A["pm"])
            dve.wait_ge(s["d_full"], FIRST_D["pm"])
            st = st_a[:, 8:16]
            for t in range(NT):
                link(ttr(TMP[:, 0:QR], PM[:, t, 0:QR], PM[:, t, 0:QR], 1.0 / QR, 0.0, ALU.mult, ALU.add,
                         st[:, 2 * t:2 * t + 1]))
                link(ttr(TMP[:, QR:QR + KVR], PM[:, t, QR:QR + KVR], PM[:, t, QR:QR + KVR], 1.0 / KVR, 0.0,
                         ALU.mult, ALU.add, st[:, 2 * t + 1:2 * t + 2]))
            rstd(st, 1.0, EPS)
            for t in range(NT):
                link(ts(PM[:, t, 0:QR], PM[:, t, 0:QR], st[:, 2 * t:2 * t + 1], None, ALU.mult))
                tell(ts(PM[:, t, QR:QR + KVR], PM[:, t, QR:QR + KVR], st[:, 2 * t + 1:2 * t + 2], None,
                        ALU.mult), "cn")
            for t in range(NT):
                link(nc.vector.tensor_copy(QK[:, t, H:2 * H, DN:DQK],
                                           PM[:, t, QR + KVR:MLA_COLS].unsqueeze(1).broadcast_to([P, H, DR])))
            for g in (1, 3):
                sc_ = vv("g_cq", g) if g < 3 else vv("g_ckv", g - 3)
                tell(ts(CT[:, g, :], take(), sc_, None, ALU.mult), "d_free")
            for t in range(NT):
                tell(nc.vector.tensor_copy(QK[:, t, 4:8, :].rearrange("p g d -> p (g d)"), take()[:, 0:384]),
                     "d_free")
            for t in range(NT):
                tell(nc.vector.tensor_copy(VA[:, t, :], take()), "d_free")
            dve.wait_ge(s["d_free"], n["d_free"])
            dve.wait_ge(s["a_free"], FIRST_A["qkT"])
            tell(nc.vector.memset(RAW[:, :, 0:1], 0.0), "raw_used")
            dve.wait_ge(s["act"], 2)
            tmp3 = TMP[:, 0:1536].rearrange("p (g d) -> p g d", g=2 * H)
            ro = [TMP[:, 256 * i:256 * i + 256].rearrange("p (g i) -> p g i", g=2 * H) for i in range(4)]
            for t in range(NT):
                st = st_a[:, 16:32]
                q3 = QK[:, t, :, :]
                link(tt(tmp3, q3, q3, ALU.mult))
                link(nc.vector.tensor_reduce(st, tmp3, AX, ALU.add))
                rstd(st, 1.0 / DQK, EPS)
                link(tt(q3, q3, st.unsqueeze(2).broadcast_to([P, 2 * H, DQK]), ALU.mult))
                link(tt(q3[:, 0:H, :], q3[:, 0:H, :], r1("g_q").unsqueeze(1).broadcast_to([P, H, DQK]), ALU.mult))
                link(tt(q3[:, H:2 * H, :], q3[:, H:2 * H, :], r1("g_k").unsqueeze(1).broadcast_to([P, H, DQK]),
                        ALU.mult))
                co = cosb[:, HALF * t:HALF * t + HALF].unsqueeze(1).broadcast_to([P, 2 * H, HALF])
                si = sinb[:, HALF * t:HALF * t + HALF].unsqueeze(1).broadcast_to([P, 2 * H, HALF])
                t1, t2 = q3[:, :, DN:DN + HALF], q3[:, :, DN + HALF:DQK]
                tell(tt(ro[0], t1, co, ALU.mult), "dve")
                tell(tt(ro[1], t2, si, ALU.mult), "dve")
                tell(tt(ro[2], t1, si, ALU.mult), "dve")
                link(tt(ro[3], t2, co, ALU.mult))
                tell(tt(t1, ro[0], ro[1], ALU.subtract), "dve")
                link(tt(t2, ro[2], ro[3], ALU.add), "qk_normed")
                link()
            for g in range(1, 2 * H, 2):
                tell(nc.vector.tensor_copy(QKT[0:DQK, g, :], take()[0:DQK, :]), "d_free")
            def mix(m):
                dst = (RT, KT, VT, LT)[m // 4][:, m % 4, :]
                dve.wait_ge(s["a_free"], pr_job(m) + 1)
                raw = RAW[:, m % 4, :]
                link(tt(dst, raw[:, 0:512], raw[:, 1:513], ALU.subtract))
                link(stt(dst, dst, vv("mu", m), raw[:, 1:513], ALU.mult, ALU.add), "raw_used")
                tell(dve.nop(), "prt")

            units = [(t, h) for t in range(NT) for h in range(H)]
            for u in range(len(units) + 2):
                if u < len(units):
                    t, h = units[u]
                    nk = P * (t + 1)
                    dve.wait_ge(s["a_full"], unit_job(u) + 1)
                    b = PA[:, unit_job(u) % 4, 0:nk]
                    link(nc.vector.tensor_reduce(nmax[:, u:u + 1], b, AX, ALU.max))
                    tell(ts(nmax[:, u:u + 1], nmax[:, u:u + 1], -DQK ** -0.5, None, ALU.mult), "smax")
                if 1 <= u <= len(units):
                    t, h = units[u - 1]
                    b = take()
                    if u >= 3:
                        dve.wait_ge(s["d_full"], FIRST_D["att"] + 2 * (u - 3) + 3)
                    tell(nc.vector.tensor_copy(PT[:, (u - 1) % 2, 0:P * (t + 1)], b[:, 0:P * (t + 1)]), "d_free")
                if u >= 2:
                    t, h = units[u - 2]
                    b = take()
                    dve.wait_ge(s["a_free"], unit_job(u - 2) + 1)
                    link(nc.vector.reciprocal(st_a[:, 32:33], rsum[:, u - 2:u - 1]))
                    link(ts(HN[:, t, 64 * h:64 * h + 64], b[:, 0:64], st_a[:, 32:33], None, ALU.mult), "d_free")
                if u < PR_EARLY:
                    mix(u)
                if pr_after(u - 2) is not None:
                    mix(pr_after(u - 2))
            dve.wait_ge(s["d_free"], n["d_free"])
            for m in range(PR_IN_ATT, 14):
                mix(m)
            for m in range(4):
                link(ts(KK[:, m, :], KT[:, m, :], vv("k_k", m), None, ALU.mult))
                tell(tt(E1[:, m, :], KK[:, m, :], KK[:, m, :], ALU.mult), "kx_sq")
            for m in range(4):
                b = take()
                link(ts(E2[:, m, :], b, 1e-24, None, ALU.max), "d_free")
                tell(dve.nop(), "var")
            for m in range(4):
                dve.wait_ge(s["rstd"], n["var"] - 3 + m)
                link(nc.vector.reciprocal(E2[:, m, :], E2[:, m, :]))
                link(tt(KK[:, m, :], KK[:, m, :], E2[:, m, :], ALU.mult))
            dve.wait_ge(s["a_free"], FIRST_A["lora"] + 12)
            omk = st_a[:, 40:44]
            link(ts(omk, vv("k_a"), -1.0, 1.0, ALU.mult, ALU.add))
            for m in range(4):
                link(ts(E2[:, m, :], AT[:, m, :], vv("k_a", m), omk[:, m:m + 1], ALU.mult, ALU.add))
                link(tt(KT[:, m, :], KT[:, m, :], E2[:, m, :], ALU.mult))
                link(stt(E1[:, m, :], RT[:, m, :], vv("r_k", m), KT[:, m, :], ALU.mult, ALU.mult))
            tell(dve.nop(), "rkk")
            b = take()
            tell(nc.vector.tensor_copy(bon[:, :], b[:, 0:32]), "d_free")
            for m in range(4):
                for c in range(NT):
                    sl = slice(P * c, P * c + P)
                    tell(nc.vector.tensor_tensor_scan(CS[:, m, sl], cc("ones"), SG[:, m, sl], 0.0,
                                                      ALU.mult, ALU.add), "dve")
            link()
            cs4 = CS.rearrange("p m (c n) -> p m c n", c=NT)
            f4 = fdec.rearrange("p (m c) -> p m c", m=4)
            mid, end = cs4[:, :, :, 63:64].squeeze(3), cs4[:, :, :, 127:128].squeeze(3)
            md = st_a[:, 44:60].rearrange("p (m c) -> p m c", m=4)
            link(nc.vector.tensor_copy(md, mid))
            link(tt(f4, end, md, ALU.subtract))
            link(tt(f4[:, :, 0:3], f4[:, :, 0:3], md[:, :, 1:4], ALU.add), "Lm")
            link()
            for m in range(4):
                tell(tt(cs4[:, m, :, :], cs4[:, m, :, :], md[:, m, :].unsqueeze(2).broadcast_to([P, NT, P]),
                        ALU.subtract), "dve")
            link()
            tell(dve.nop(), "Lm")
            link(tt(SG[:, :, :], CS[:, :, :], SG[:, :, :], ALU.subtract), "Lm")
            for t in range(NT):
                tell(nc.vector.tensor_copy(VTOK[:, t, :], take()), "d_free")
            dve.wait_ge(s["rexp"], 2)
            link(tt(RT[:, :, :], RT[:, :, :], E1[:, :, :], ALU.mult), "rhat")
            dve.wait_ge(s["rexp"], 3)
            link(tt(KT[:, :, :], KT[:, :, :], E2[:, :, :], ALU.mult), "rhat")
            link(stt(AT[:, :, :], AT[:, :, :], -1.0, KK[:, :, :], ALU.mult, ALU.mult))
            link(tt(AT[:, :, :], AT[:, :, :], E2[:, :, :], ALU.mult), "rhat")
            dve.wait_ge(s["rexp"], 4)
            link(tt(KK[:, :, :], KK[:, :, :], EQ[:, :, :], ALU.mult), "rhat")
            for t in range(NT):
                tell(nc.vector.tensor_copy(BTOK[:, t, :], take()), "d_free")
            def by_chunk(z):
                return z.rearrange("p (c n) -> p c n", c=NT)

            def mask(m_):
                return m_.unsqueeze(1).broadcast_to([P, NT, P])

            for grp in range(2):
                fa = FIRST_A[f"inv{grp}"]
                dve.wait_ge(s["a_free"], fa)
                dve.wait_ge(s["d_free"], n["d_free"])
                if grp == 0:
                    dve.wait_ge(s["rhat"], 4)
                    tell(nc.vector.memset(tmid[:, :], 0.0), "tmid")
                for q in range(4):
                    b = take()
                    tell(tt(by_chunk(MT[:, q, :]), by_chunk(b), mask(cc("strict")), ALU.mult), "d_free")
                dve.wait_ge(s["d_free"], n["d_free"])
                for q in range(4):
                    xt = by_chunk(XT(4 * grp + q))
                    link(tt(xt, by_chunk(MT[:, q, :]), mask(LV[:, 0, :]), ALU.mult))
                    link(tt(xt, xt, mask(ident), ALU.add), "x1t")
                for q in range(4):
                    tell(tt(by_chunk(CTL[:, q, :]), by_chunk(MT[:, q, :]), mask(LV[:, 1, :]), ALU.mult), "ct")
                for lev in range(1, LEVELS):
                    for q in range(4):
                        xt = XT(4 * grp + q)
                        b = take()
                        if lev < LEVELS - 1:
                            dve.wait_ge(s["d_full"], n["d_free"] + 2)
                        tell(tt(xt, xt, b, ALU.add), "d_free")
                        if lev < LEVELS - 1:
                            b = take()
                            tell(tt(XI[:, q, :], XI[:, q, :], b, ALU.add), "d_free")
                            dve.wait_ge(s["a_full"], fa + 4 * lev + q + 1)
                            tell(tt(by_chunk(CTL[:, q, :]), by_chunk(MT[:, q, :]), mask(LV[:, lev + 1, :]),
                                    ALU.mult), "ct")
            def attention_norm(t):
                o3 = HN[:, t, 0:512].rearrange("p (h d) -> p h d", h=H)
                t3 = lvl[:, 0:512].rearrange("p (h d) -> p h d", h=H)
                st = st_a[:, 16:24]
                link(tt(t3, o3, o3, ALU.mult))
                link(nc.vector.tensor_reduce(st, t3, AX, ALU.add))
                rstd(st, 1.0 / 64, EPS)
                link(tt(o3, o3, st.unsqueeze(2).broadcast_to([P, H, 64]), ALU.mult))
                link(tt(HN[:, t, 0:512], HN[:, t, 0:512], r1("g_attn"), ALU.mult))

            def output_norm(t):
                dve.wait_ge(s["a_free"], FIRST_A["chain"] + 3 * t + 3)
                g_ = lvl[:, 0:512]
                h3 = lambda z: z.rearrange("p (h d) -> p h d", h=H)
                y = HN[:, t, 512:1024]
                st = st_a[:, 16:24]
                bc = lambda z: z.unsqueeze(2).broadcast_to([P, H, 64])
                link(nc.vector.tensor_reduce(st, h3(y), AX, ALU.add))
                link(ts(st, st, 1.0 / 64, None, ALU.mult))
                link(tt(h3(y), h3(y), bc(st), ALU.subtract))
                link(tt(g_, y, y, ALU.mult))
                link(nc.vector.tensor_reduce(st, h3(g_), AX, ALU.add))
                rstd(st, 1.0 / 64, LN_X_EPS)
                link(tt(h3(y), h3(y), bc(st), ALU.mult))
                link(tt(y, y, r1("ln_x_w"), ALU.mult))
                link(tt(y, y, r1("ln_x_b"), ALU.add))
                link(tt(h3(g_), h3(VTOK[:, t, :]), bc(bon[:, 8 * t:8 * t + 8]), ALU.mult))
                link(tt(y, y, g_, ALU.add))
                link(tt(y, y, GT[:, t, :], ALU.mult), "ycomb")

            def matrices(c):
                for m, mk in enumerate(("strict", "incl", "incl")):
                    for odd in range(2):
                        b = take()
                        tell(tt(MATS[c % 2][:, m, odd:H:2, :], by_chunk(b), mask(cc(mk)), ALU.mult),
                             "d_free")

            dve.wait_ge(s["d_free"], n["d_free"])
            matrices(0)
            for c in range(NT):
                if c + 1 < NT:
                    matrices(c + 1)
                b = take()
                dve.wait_ge(s["a_full"], FIRST_A["chain"] + 3 * c + 3)
                for pr in range(4):
                    f2 = slice(P * pr, P * pr + P)
                    ins = stt(tmid[:, f2], b[:, f2], fdec[:, 4 * pr + c:4 * pr + c + 1], cc("heads"),
                              ALU.mult, ALU.mult)
                    tell(ins, "d_free" if pr == 3 else "dve")
                attention_norm(c)
                if c > 0:
                    output_norm(c - 1)
            output_norm(NT - 1)
            for t in range(NT):
                turned_block(HT, t)
            dve.wait_ge(s["in_gffn"], 16)
            for t in range(NT + 1):
                if t < NT:
                    for half in range(2):
                        b = take()
                        xs = X[:, t, 512 * half:512 * half + 512]
                        link(tt(xs, xs, b, ALU.add), "d_free")
                    rms_row("xn2", t, GF)
                if t >= 1:
                    turned_block(HT, t - 1)
            for m in range(1, 16, 2):
                tell(nc.vector.tensor_copy(QPT[:, m, :], take()), "d_free")

            def top_sixteen(vals, idx, src, width, first, last):
                for g in range(first, last):
                    tell(nc.vector.max(vals[:, 16 * g:16 * g + 8], src[:, width * g:width * g + width]), "dve")
                link()
                for g in range(first, last):
                    tell(nc.vector.max_index(idx[:, 16 * g:16 * g + 8], vals[:, 16 * g:16 * g + 8],
                                             src[:, width * g:width * g + width]), "dve")
                link()
                for g in range(first, last):
                    sg_ = src[:, width * g:width * g + width]
                    tell(nc.vector.match_replace(sg_, vals[:, 16 * g:16 * g + 8], sg_, -3e38), "dve")
                link()
                for g in range(first, last):
                    tell(nc.vector.max(vals[:, 16 * g + 8:16 * g + 16], src[:, width * g:width * g + width]), "dve")
                link()
                for g in range(first, last):
                    tell(nc.vector.max_index(idx[:, 16 * g + 8:16 * g + 16], vals[:, 16 * g + 8:16 * g + 16],
                                             src[:, width * g:width * g + width]), "dve")
                link()

            STEPS = 8

            def select(t, step):
                c4 = CAND.rearrange("p (h a b) -> p h a b", h=H, a=TOPK)
                halves = s1v.rearrange("p (h q k) -> p h q k", h=H, q=2)
                pa_, pb_ = i1u[:, 0:128], i1u[:, 128:256]
                acc_ = [SS[t][:, 0:NSEL], SS[t][:, NSEL:2 * NSEL]]
                if step == 0:
                    dve.wait_ge(s["a_free"], FIRST_A["s"] + 4 * t + 4)
                    top_sixteen(s1v, i1u, SS[t], NK, 0, 8)
                elif step == 1:
                    top_sixteen(s1v, i1u, SS[t], NK, 8, 16)
                elif step == 2:
                    for h in range(H):
                        tell(tt(c4[:, h, :, :], halves[:, h, 0, :].unsqueeze(2).broadcast_to([P, TOPK, TOPK]),
                                halves[:, h, 1, :].unsqueeze(1).broadcast_to([P, TOPK, TOPK]), ALU.add), "dve")
                    link()
                elif step == 3:
                    top_sixteen(tpv, tpu, CAND, TOPK * TOPK, 0, 4)
                elif step == 4:
                    top_sixteen(tpv, tpu, CAND, TOPK * TOPK, 4, 8)
                elif step == 5:
                    g3 = GATE[:, t % 2, :].rearrange("p (h k) -> p h k", h=H)
                    p3 = tpv.rearrange("p (h k) -> p h k", h=H)
                    if t >= 2:
                        dve.wait_ge(s["uv_used"], NSEL * (t - 1))
                    link(tt(g3, p3, p3[:, :, 0:1].broadcast_to([P, H, TOPK]), ALU.subtract), "topk")
                    link(nc.vector.tensor_copy(s1v[:, :], i1u[:, :]))
                    tell(ts(pa_, tpu[:, :], 4, None, ALU.logical_shift_right), "dve")
                    link(ts(pb_, tpu[:, :], 15, None, ALU.bitwise_and))
                if step in (6, 7):
                    q = step - 6
                    link(nc.vector.tensor_copy(tpv[:, :], (pa_, pb_)[q]))
                    eq = CAND.rearrange("p (k a) -> p k a", k=NSEL)
                    link(tt(eq, tpv.unsqueeze(2).broadcast_to([P, NSEL, TOPK]),
                            cc("iota").unsqueeze(1).broadcast_to([P, NSEL, TOPK]), ALU.is_equal))
                    for h in range(H):
                        e3 = c4[:, h, :, :]
                        tell(tt(e3, e3, halves[:, h, q, :].unsqueeze(1).broadcast_to([P, TOPK, TOPK]), ALU.mult), "dve")
                    link()
                    link(nc.vector.tensor_reduce(acc_[q], eq, AX, ALU.add))
                if step == 7:
                    link(stt(acc_[0], acc_[0], float(NK), acc_[1], ALU.mult, ALU.add))
                    link(nc.vector.tensor_copy(IDX[:, t % 2, :], acc_[0]), "idx")

            def gates(t):
                dve.wait_ge(s["geluv"], t + 1)
                g3 = GATE[:, t % 2, :].rearrange("p (h k) -> p h k", h=H)
                link(nc.vector.tensor_reduce(gmx[:, 0:8], g3, AX, ALU.add))
                link(nc.vector.reciprocal(gmx[:, 8:16], gmx[:, 0:8]))
                link(tt(g3, g3, gmx[:, 8:16].unsqueeze(2).broadcast_to([P, H, TOPK]), ALU.mult))

            def layer_rows(ready, t, src, dst, gain=None, shift=None):
                st = ffst[:, 14 * t:14 * t + 14]
                for i in range(2):
                    tell(nc.vector.bn_stats(st[:, 6 * i:6 * i + 6], src[:, 512 * i:512 * i + 512]), "dve")
                link()
                link(nc.vector.bn_aggr(st[:, 12:14], st[:, 0:12]))
                rstd(st[:, 13:14], 1.0, LN_EPS)
                if gain is None:
                    tell(ts(dst, src, st[:, 12:13], st[:, 13:14], ALU.subtract, ALU.mult), ready)
                else:
                    link(ts(dst, src, st[:, 12:13], st[:, 13:14], ALU.subtract, ALU.mult))
                    link(tt(dst, dst, gain, ALU.mult))
                    link(tt(dst, dst, shift, ALU.add), ready)

            for step in range(STEPS):
                select(0, step)
            b = take()
            link(tt(modc[:, :], b[:, 0:32], vv("b_mod"), ALU.add), "d_free")
            for o in (8, 24):
                link(ts(modc[:, o:o + 8], modc[:, o:o + 8], 1.0, None, ALU.add))
            tell(dve.nop(), "peer_clear")
            for t in range(NT):
                gates(t)
                cuts = (0, NORM_AT) + (SELECT_AT if t + 1 < NT else ()) + (TURNS,)
                for first, last in zip(cuts[:-1], cuts[1:]):
                    if first == NORM_AT and t > 0:
                        layer_rows("xn3", t - 1, X[:, t - 1, :], HN[:, t - 1, :])
                    if first in SELECT_AT:
                        select(t + 1, SELECT_AT.index(first))
                    with dve.Fori(first, last) as it:
                        for g in range(RING // GRP + 1):
                            if g < RING // GRP:
                                for j in range(GRP * g, GRP * g + GRP):
                                    dve.wait_ge(uv_full[j], it * 16 + 16 * (NSEL // RING * t + 1))
                                    ttr(UV[:, j, 0:D], UV[:, j, 0:D], HN[:, t, :], 1.0, 0.0, ALU.mult, ALU.add,
                                        DOT[:, g, j % GRP:j % GRP + 1]).then_inc(s["dots"], 1)
                            if g >= 1:
                                dve.wait_ge(s["gelu"], it * (RING // GRP) + (NSEL // GRP * t + g))
                                for j in range(GRP * (g - 1), GRP * g):
                                    sel_ = GATE[:, t % 2, bass.ds(it * RING + j, 1)]
                                    ts(DG[:, j, :], ident, GEL[:, g - 1, j % GRP:j % GRP + 1], sel_,
                                       ALU.mult, ALU.mult).then_inc(s["diag"], 1)
                for half in range(2):
                    b = take()
                    xs = X[:, t, 512 * half:512 * half + 512]
                    link(tt(xs, xs, b, ALU.add), "d_free")
            layer_rows("xn3", NT - 1, X[:, NT - 1, :], HN[:, NT - 1, :])
            tell(dve.nop(), "row2free")
            tell(nc.vector.memset(YAP[:, :, 0:30], 0.0), "bufs")
            link(nc.vector.memset(UP[:, :, 0:16], 0.0), "bufs")
            dve.wait_ge(s["a_free"], FIRST_A["in2"] + 4)
            for m in range(4):
                b = take()
                link(tt(YAP[:, m, 30:542], b, SGA[:, m, :], ALU.mult), "d_free")
            for m in range(4):
                w = vv("w_conv")[:, CONV_K * m:CONV_K * m + CONV_K]
                link(ts(CV[:, m, :], YAP[:, m, 0:512], w[:, 0:1], vv("b_conv", m), ALU.mult, ALU.add))
                for j in range(1, CONV_K):
                    link(stt(CV[:, m, :], YAP[:, m, j:j + 512], w[:, j:j + 1], CV[:, m, :], ALU.mult, ALU.add))
                tell(dve.nop(), "conv")
            b = take()
            for m in range(4):
                ins = stt(CV[:, m, :], b, -1.0 / RD, CV[:, m, :], ALU.mult, ALU.add)
                if m < 3:
                    tell(ins, "dve")
                else:
                    tell(ins, "d_free")
            dve.wait_ge(s["d_free"], n["d_free"])
            link()
            dve.wait_ge(s["a_full"], FIRST_A["in2"])
            for m in range(4):
                tell(tt(HN[:, m, 0:512], CV[:, m, :], CV[:, m, :], ALU.mult), "convsq")
            b = take()
            link(ts(HN[:, 0, 512:1024], b, 1.0 / RD, LN_EPS, ALU.mult, ALU.add), "d_free")
            tell(dve.nop(), "var")
            dve.wait_ge(s["rstd"], n["var"])
            link(nc.vector.reciprocal(HN[:, 0, 512:1024], HN[:, 0, 512:1024]))
            for m in range(4):
                tell(tt(CV[:, m, :], CV[:, m, :], HN[:, 0, 512:1024], ALU.mult), "silu_in")
            for m, w in enumerate(POOL):
                if m == 0:
                    dve.wait_ge(s["a_free"], FIRST_A["in2"] + 8)
                u = UP[:, m, :]
                src = u
                step = 1
                bufs_ = [HN[:, 1, 0:528], HN[:, 2, 0:528]]
                i = 0
                while step < w:
                    dst = bufs_[i % 2]
                    if 2 * step == w:
                        link(tt(dst[:, 16:528], src[:, 16:528], src[:, 16 - step:528 - step], ALU.add))
                    else:
                        link(nc.vector.memset(dst[:, 0:16], 0.0))
                        link(tt(dst[:, 16:528], src[:, 16:528], src[:, 16 - step:528 - step], ALU.add))
                    src = dst
                    step *= 2
                    i += 1
                cn_ = cc("cnt")[:, 16 * m:16 * m + 16]
                link(tt(src[:, 16:32], src[:, 16:32], cn_, ALU.mult))
                link(ts(src[:, 32:528], src[:, 32:528], 1.0 / w, None, ALU.mult))
                link(tt(PO[:, m, :], src[:, 16:528], u[:, 16:528], ALU.subtract), "pooled")
            dve.wait_ge(s["a_free"], FIRST_A["in2"] + 24)
            for m in range(8):
                b = take()
                link(tt(MG[:, m, :], b, GA[:, m, :], ALU.mult), "d_free")
            dve.wait_ge(s["a_free"], FIRST_A["in2"] + 24)
            for m in range(8):
                b = take()
                q = HN[:, 3, 512 * (m % 2):512 * (m % 2) + 512]
                link(stt(q, b, vv("pool_scale", m), GB[:, m, :], ALU.mult, ALU.mult), "d_free")
                link(tt(MG[:, m, :], MG[:, m, :], q, ALU.add), "merged")
            dve.wait_ge(s["in_row2"], 16)

            def r2(name):
                return R2[:, ROW2[name][0]:ROW2[name][1]]
            link(tt(RW[:, 0:2048], RW[:, 0:2048], R2[:, 0:2048], ALU.add))
            for t in range(NT + 1):
                if t < NT:
                    for half in range(2):
                        sl = slice(512 * half, 512 * half + 512)
                        b = take()
                        q = HN[:, t, sl]
                        link(tt(q, b, RW[:, sl], ALU.mult), "d_free")
                        link(stt(X[:, t, sl], X[:, t, sl], ALPHA, q, ALU.mult, ALU.add))
                    layer_rows("lnx", t, X[:, t, :], X[:, t, :], r2("ln1_g"), r2("ln1_b"))
                    layer_rows("xn4", t, X[:, t, :], HN[:, t, :])
                if t >= 1:
                    turned_block(HT4, t - 1, lambda k: modc[:, 24 + k:25 + k], lambda k: modc[:, 16 + k:17 + k])
            link(nc.vector.memset(UR[:, :, 0:2], 0.0), "upraw_used")

            def gated(j):
                dve.wait_ge(s["ffgelu"], j + 1)
                v_ = UC[:, 2 * (j % 2), :]
                link(tt(FT[:, j, :], v_, UC[:, 2 * (j % 2) + 1, :], ALU.mult), "ff")
            for j in range(NF):
                for i in range(2):
                    f = j + NF * i
                    q = 2 * (j % 2) + i
                    w = vv("w_ff")[:, 3 * f:3 * f + 3]
                    dve.wait_ge(s["a_free"], FIRST_A["up"] + 2 * j + i + 1)
                    u, o = UR[:, q, :], UC[:, q, :]
                    link(ts(o, u[:, 0:512], w[:, 0:1], vv("b_ff", f), ALU.mult, ALU.add))
                    link(stt(o, u[:, 1:513], w[:, 1:2], o, ALU.mult, ALU.add))
                    link(stt(o, u[:, 2:514], w[:, 2:3], o, ALU.mult, ALU.add), "upraw_used")
                    if i == 1:
                        tell(dve.nop(), "gelu_in")
                if j >= 1:
                    gated(j - 1)
            gated(NF - 1)
            for t in range(NT):
                b = take()
                link(tt(HN[:, t, 512:1024], b, RW[:, 1536:2048], ALU.mult), "d_free")
                dve.wait_ge(s["a_free"], FIRST_A["down"] + t + 1)
                link(tt(HN[:, t, 0:512], HN[:, t, 0:512], RW[:, 1024:1536], ALU.mult))
                link(stt(X[:, t, :], X[:, t, :], ALPHA, HN[:, t, :], ALU.mult, ALU.add))
                layer_rows("fin", t, X[:, t, :], X[:, t, :], r2("ln2_g"), r2("ln2_b"))

        @block.gpsimd
        def _(pool):
            pool.wait_ge(s["a_full"], FIRST_A["ada"])

            for t in range(NT):
                pool.wait_ge(s["idx"], t + 1)
                for i in range(NSEL):
                    turn = NSEL * t + i
                    if turn == 4:
                        pool.wait_ge(s["peer_clear"], 1)
                    if turn >= RING:
                        pool.wait_ge(s["uv_used"], turn - RING + 1)
                    nc.gpsimd.indirect_dma_start(
                        UV[:, turn % RING, :], None, uv,
                        bass.IndirectOffsetOnAxis(ap=IDX[:, t % 2, i:i + 1], axis=0),
                    ).then_inc(uv_full[turn % RING], 16)


def kernel(**inputs):
    import numpy as _np
    import concourse.bacc as _bacc
    from concourse import mybir as _mybir
    from concourse.bass_utils import run_bass_kernel_spmd as _run

    def f(name):
        return _np.asarray(inputs[name])

    def cols(v):
        return _np.ascontiguousarray(_np.asarray(v).reshape(-1, P).T)

    def rows(*vs):
        return _np.ascontiguousarray(_np.broadcast_to(_np.concatenate([_np.asarray(v).reshape(-1) for v in vs])[None], (P, sum(_np.asarray(v).size for v in vs))))

    b_ada = f("b_ada_2")[0].reshape(6, D)
    w_conv = f("w_dw_a_2")[0].reshape(CONV_K, 4, P).transpose(2, 1, 0).reshape(P, 4 * CONV_K)
    w_ff = f("w_dw_f_2")[0].reshape(3, 44, P).transpose(2, 1, 0).reshape(P, 44 * 3)
    vec = _np.concatenate([
        cols(f("g_mix")[0]), cols(f("rwkv_mu")[0]), cols(f("g_cq")[0]), cols(f("g_ckv")[0]), cols(f("w0")[0]),
        cols(f("a0")[0]), cols(f("k_k")[0]), cols(f("k_a")[0]), cols(f("r_k")[0]), cols(f("c_2")[0]),
        cols(b_ada[0]), cols(b_ada[1]), cols(b_ada[3]), cols(b_ada[4]), w_conv, cols(f("b_dw_a_2")[0]),
        cols(f("ln_a_g_2")[0]), cols(f("ln_a_b_2")[0]), cols(f("pool_scale_2")[0]), w_ff,
        cols(f("b_dw_f_2")[0])], 1)
    lora = _np.concatenate([_np.concatenate([f("w2")[0], f("a2")[0]], 0), f("g2")[0]], 1)
    keys = f("sub_keys")[0].transpose(3, 0, 1, 2).reshape(P, 16 * NK)
    uv = _np.concatenate([f("expert_u")[0], f("expert_v")[0]], 1)
    w_up = f("w_up_2")[0].reshape(D, 2, NF, P).transpose(0, 2, 1, 3).reshape(D, 2 * D_FF)
    arrays = {
        "x": f("x")[0], "pos": _np.ascontiguousarray(f("positions")[0].reshape(NT, P).T), "cst": constants(),
        "vec": vec, "row1": rows(f("g_qnorm"), f("g_knorm"), f("g_attn_out"), f("ln_x_w"), f("ln_x_b")),
        "gffn": rows(f("g_ffn")),
        "row2": rows(b_ada[2], b_ada[5], f("ln1_g_2"), f("ln1_b_2"), f("ln2_g_2"), f("ln2_b_2")),
        "w_in": f("w_in")[0], "w_uq": f("w_uq")[0], "w_uk": f("w_uk")[0], "w_uv": f("w_uv")[0], "lora": lora,
        "w_o": f("w_o")[0], "w_pq": f("w_pq")[0], "keys": keys, "uv": uv, "w_ada": f("w_ada_2")[0],
        "w_in2": f("w_in_2")[0], "w_pw": f("w_pw_a_2")[0], "w_pool": f("w_pool_2")[0], "w_out": f("w_out_2")[0],
        "w_up": w_up, "w_down": f("w_down_2")[0],
    }
    nc = _bacc.Bacc("TRN2", target_bir_lowering=False, num_devices=1)
    arrays = {f"in_{k}": _np.ascontiguousarray(v) for k, v in arrays.items()}
    args = [nc.dram_tensor(k, v.shape, _mybir.dt.from_np(v.dtype), kind="ExternalInput").ap()
            for k, v in arrays.items()]
    out = nc.dram_tensor("out_0", (S, D), F32, kind="ExternalOutput").ap()
    build(nc, *args, out)
    r = _run(nc, [arrays], core_ids=[0])
    return r.results[0]["out_0"].reshape(1, S, D)
```
